# Optimizing a Trainium2 kernel written in Bass

```python
import jax, jax.numpy as jnp
from jax import lax
import numpy as np

D_MODEL = 1024
BATCH = 1
SEQ = 2048
DEPTH = 1

CTX_LEN = 256
GRID_W = 64
CONV_WIDTH = 512
HGRN_WIDTH = 512
MIX_WIDTH = CONV_WIDTH + HGRN_WIDTH
HGRN_HEAD_DIM = 128
HGRN_HEADS = HGRN_WIDTH // HGRN_HEAD_DIM
CONV_K = 31
CONV_PAD = (CONV_K - 1) // 2
CHUNK = 64
N_EXPERTS = 16
EXPERT_FF = D_MODEL
CAPACITY_FACTOR = 2
N_MOD = 6
EPS = 1e-6

OFF_CONV_A = 0
OFF_CONV_B = OFF_CONV_A + CONV_WIDTH
OFF_Q = OFF_CONV_B + CONV_WIDTH
OFF_I = OFF_Q + HGRN_WIDTH
OFF_FF = OFF_I + HGRN_WIDTH
OFF_FB = OFF_FF + HGRN_WIDTH
OFF_G = OFF_FB + HGRN_WIDTH
IN_COLS = OFF_G + HGRN_WIDTH

kernel_name = 'hymba_conformer_hgrn2_ecmoe_dit'

def rmsnorm(x, g):
    xf = x.astype(jnp.float32)
    y = xf * lax.rsqrt(jnp.mean(xf * xf, axis=-1, keepdims=True) + EPS)
    return (y * g.astype(jnp.float32)).astype(x.dtype)

def layernorm(x, g, b):
    xf = x.astype(jnp.float32)
    mu = jnp.mean(xf, axis=-1, keepdims=True)
    xc = xf - mu
    y = xc * lax.rsqrt(jnp.mean(xc * xc, axis=-1, keepdims=True) + EPS)
    return (y * g.astype(jnp.float32) + b.astype(jnp.float32)).astype(x.dtype)

def modulation(cvec, w, b):
    m = jnp.einsum('bd,de->be', jax.nn.silu(cvec), w) + b
    return [t[:, None, :] for t in jnp.split(m, N_MOD, axis=-1)]

def modulate(h, shift, scale):
    return h * (1 + scale) + shift

def dwconv_seq(u, taps):
    ch = u.shape[-1]
    return lax.conv_general_dilated(u, taps[:, None, :], window_strides=(1,),
                                    padding=[(CONV_PAD, CONV_PAD)],
                                    dimension_numbers=('NWC', 'WIO', 'NWC'),
                                    feature_group_count=ch)

def dwconv_grid(u, taps):
    b, n, ch = u.shape
    rows = n // GRID_W
    g = u.reshape(b, rows, GRID_W, ch)
    half = ch // 2
    dn = ('NHWC', 'HWIO', 'NHWC')
    horiz = lax.conv_general_dilated(g[..., :half], taps[None, :, None, :half], (1, 1),
                                     [(0, 0), (CONV_PAD, CONV_PAD)], dimension_numbers=dn,
                                     feature_group_count=half)
    vert = lax.conv_general_dilated(g[..., half:], taps[:, None, None, half:], (1, 1),
                                    [(CONV_PAD, CONV_PAD), (0, 0)], dimension_numbers=dn,
                                    feature_group_count=ch - half)
    return jnp.concatenate([horiz, vert], axis=-1).reshape(b, n, ch)

def conv_module(proj, taps, bias, ln_g, ln_b, conv_fn):
    u = proj[..., OFF_CONV_A:OFF_CONV_B] * jax.nn.sigmoid(proj[..., OFF_CONV_B:OFF_Q])
    u = conv_fn(u, taps) + bias
    return jax.nn.silu(layernorm(u, ln_g, ln_b))

def split_heads(t):
    b, n, _ = t.shape
    return t.reshape(b, n, HGRN_HEADS, HGRN_HEAD_DIM).transpose(0, 2, 1, 3)

def merge_heads(t):
    b, h, n, d = t.shape
    return t.transpose(0, 2, 1, 3).reshape(b, n, h * d)

def forget_gate(f_logits, lb):
    f = lb + (1.0 - lb) * jax.nn.sigmoid(f_logits.astype(jnp.float32))
    return split_heads(jnp.log(f)), split_heads(1.0 - f)

def gla_scan(k, v, log_f, s0, q=None):
    def to_chunks(t):
        b, h, n, d = t.shape
        return t.reshape(b, h, n // CHUNK, CHUNK, d).transpose(2, 0, 1, 3, 4)

    causal = jnp.tril(jnp.ones((CHUNK, CHUNK), dtype=bool))

    def step(state, xs):
        if q is None:
            kc, vc, gc = xs
        else:
            qc, kc, vc, gc = xs
        b = jnp.cumsum(gc, axis=2)
        b_last = b[:, :, -1:, :]
        k_dec = kc * jnp.exp(b_last - b)
        new_state = (jnp.exp(b_last[:, :, 0, :, None]) * state
                     + jnp.einsum('bhck,bhcv->bhkv', k_dec, vc))
        if q is None:
            return new_state, None
        o_inter = jnp.einsum('bhtk,bhkv->bhtv', qc * jnp.exp(b), state)
        diff = b[:, :, :, None, :] - b[:, :, None, :, :]
        decay = jnp.exp(jnp.where(causal[:, :, None], diff, -jnp.inf))
        scores = jnp.einsum('bhtk,bhsk,bhtsk->bhts', qc, kc, decay)
        o = o_inter + jnp.einsum('bhts,bhsv->bhtv', scores, vc)
        return new_state, o

    inputs = (k, v, log_f) if q is None else (q, k, v, log_f)
    xs = tuple(to_chunks(t) for t in inputs)
    state, o = lax.scan(step, s0, xs)
    if q is None:
        return state, None
    nc, b, h, cl, dv = o.shape
    return state, o.transpose(1, 2, 0, 3, 4).reshape(b, h, nc * cl, dv)

def hgrn_bidir(p_i, p_ff, p_fb, lb_l, s0_f, s0_b, q=None):
    v = split_heads(p_i.astype(jnp.float32))
    logf_f, k_f = forget_gate(p_ff, lb_l[0])
    logf_b, k_b = forget_gate(p_fb, lb_l[1])
    rev = lambda t: t[:, :, ::-1]
    qh = None if q is None else split_heads(q.astype(jnp.float32))
    s_f, o_f = gla_scan(k_f, v, logf_f, s0_f, qh)
    s_b, o_b = gla_scan(rev(k_b), rev(v), rev(logf_b), s0_b, None if qh is None else rev(qh))
    if q is None:
        return None, s_f, s_b
    return o_f + rev(o_b), s_f, s_b

def hgrn_readout(o, g, norm_g):
    y = o * lax.rsqrt(jnp.mean(o * o, axis=-1, keepdims=True) + EPS)
    return merge_heads(y) * norm_g.astype(jnp.float32) * jax.nn.silu(g.astype(jnp.float32))

def token_mixer(h, p, lb_l, conv_fn, s0_f, s0_b):
    proj = jnp.einsum('bnd,dc->bnc', h, p['w_in'])
    conv_out = conv_module(proj, p['taps'], p['conv_bias'], p['ln_g'], p['ln_b'], conv_fn)
    o, s_f, s_b = hgrn_bidir(proj[..., OFF_I:OFF_FF], proj[..., OFF_FF:OFF_FB],
                             proj[..., OFF_FB:OFF_G], lb_l, s0_f, s0_b,
                             q=proj[..., OFF_Q:OFF_I])
    hg = hgrn_readout(o, proj[..., OFF_G:IN_COLS], p['hgrn_g']).astype(h.dtype)
    mixed = jnp.concatenate([conv_out.astype(h.dtype), hg], axis=-1)
    return jnp.einsum('bnc,cd->bnd', mixed, p['w_out']), s_f, s_b

def expert_choice_ffn(h, p):
    b, n, d = h.shape
    cap = CAPACITY_FACTOR * n // N_EXPERTS
    logits = jnp.einsum('bnd,de->bne', h, p['router']).astype(jnp.float32)
    probs = jax.nn.softmax(logits, axis=-1)
    gate, idx = lax.top_k(probs.transpose(0, 2, 1), cap)
    xs = jax.vmap(lambda hb, ib: hb[ib])(h, idx)
    hid = (jax.nn.silu(jnp.einsum('becd,edf->becf', xs, p['w_gate']))
           * jnp.einsum('becd,edf->becf', xs, p['w_up']))
    out = jnp.einsum('becf,efd->becd', hid, p['w_down']) * gate[..., None].astype(h.dtype)
    y = jax.vmap(lambda ob, ib: jnp.zeros((n, d), ob.dtype).at[ib.reshape(-1)].add(
        ob.reshape(-1, d)))(out, idx)
    return y.astype(h.dtype)

def setup_inputs(seed: int = 0) -> dict:
    key = jax.random.key(seed)
    ks = jax.random.split(key, 21)
    f32 = jnp.float32

    def nrm(k, shape, scale):
        return jax.random.normal(k, shape, f32) * scale

    return {
        'x': nrm(ks[0], (BATCH, SEQ, D_MODEL), 1.0),
        'c': nrm(ks[1], (BATCH, D_MODEL), 1.0),
        'ctx': nrm(ks[2], (BATCH, CTX_LEN, D_MODEL), 1.0),
        'c_ctx': nrm(ks[3], (D_MODEL,), 1.0),
        'ada_w': nrm(ks[4], (DEPTH, D_MODEL, N_MOD * D_MODEL), D_MODEL ** -0.5),
        'ada_b': nrm(ks[5], (DEPTH, N_MOD * D_MODEL), 0.02),
        'norm1_g': 1.0 + nrm(ks[6], (DEPTH, D_MODEL), 0.02),
        'w_in': nrm(ks[7], (DEPTH, D_MODEL, IN_COLS), D_MODEL ** -0.5),
        'conv_taps': nrm(ks[8], (DEPTH, CONV_K, CONV_WIDTH), CONV_K ** -0.5),
        'conv_bias': nrm(ks[9], (DEPTH, CONV_WIDTH), 0.02),
        'conv_ln_g': 1.0 + nrm(ks[10], (DEPTH, CONV_WIDTH), 0.02),
        'conv_ln_b': nrm(ks[11], (DEPTH, CONV_WIDTH), 0.02),
        'hgrn_lb_logits': nrm(ks[12], (DEPTH + 1, 2, HGRN_WIDTH), 0.5),
        'hgrn_norm_g': 1.0 + nrm(ks[13], (DEPTH, HGRN_WIDTH), 0.02),
        'w_out': nrm(ks[14], (DEPTH, MIX_WIDTH, D_MODEL), MIX_WIDTH ** -0.5),
        'norm2_g': 1.0 + nrm(ks[15], (DEPTH, D_MODEL), 0.02),
        'router_w': nrm(ks[16], (DEPTH, D_MODEL, N_EXPERTS), D_MODEL ** -0.5),
        'w_gate': nrm(ks[17], (DEPTH, N_EXPERTS, D_MODEL, EXPERT_FF), D_MODEL ** -0.5),
        'w_up': nrm(ks[18], (DEPTH, N_EXPERTS, D_MODEL, EXPERT_FF), D_MODEL ** -0.5),
        'w_down': nrm(ks[19], (DEPTH, N_EXPERTS, EXPERT_FF, D_MODEL), EXPERT_FF ** -0.5),
        'final_g': 1.0 + nrm(ks[20], (D_MODEL,), 0.02),
    }

def reference(x, c, ctx, c_ctx, ada_w, ada_b, norm1_g, w_in, conv_taps, conv_bias,
              conv_ln_g, conv_ln_b, hgrn_lb_logits, hgrn_norm_g, w_out, norm2_g,
              router_w, w_gate, w_up, w_down, final_g):
    lower_bounds = jnp.cumsum(jax.nn.softmax(hgrn_lb_logits.astype(jnp.float32), axis=0),
                              axis=0)[:DEPTH]
    bsz = x.shape[0]
    zero_state = jnp.zeros((bsz, HGRN_HEADS, HGRN_HEAD_DIM, HGRN_HEAD_DIM), jnp.float32)
    for l in range(DEPTH):
        p = {'w_in': w_in[l], 'taps': conv_taps[l], 'conv_bias': conv_bias[l],
             'ln_g': conv_ln_g[l], 'ln_b': conv_ln_b[l], 'hgrn_g': hgrn_norm_g[l],
             'w_out': w_out[l], 'router': router_w[l], 'w_gate': w_gate[l],
             'w_up': w_up[l], 'w_down': w_down[l]}
        sh1, sc1, g1, sh2, sc2, g2 = modulation(c, ada_w[l], ada_b[l])
        csh1, csc1, cg1, csh2, csc2, cg2 = modulation(c_ctx[None, :], ada_w[l], ada_b[l])

        h_ctx = modulate(rmsnorm(ctx, norm1_g[l]), csh1, csc1)
        if l == DEPTH - 1:
            p_ctx = jnp.einsum('bnd,dc->bnc', h_ctx, w_in[l][:, OFF_I:OFF_G])
            _, s_f, s_b = hgrn_bidir(p_ctx[..., :HGRN_WIDTH],
                                     p_ctx[..., HGRN_WIDTH:2 * HGRN_WIDTH],
                                     p_ctx[..., 2 * HGRN_WIDTH:], lower_bounds[l],
                                     zero_state, zero_state)
        else:
            mix_ctx, s_f, s_b = token_mixer(h_ctx, p, lower_bounds[l], dwconv_seq,
                                            zero_state, zero_state)
            ctx = ctx + cg1 * mix_ctx
            ctx = ctx + cg2 * expert_choice_ffn(modulate(rmsnorm(ctx, norm2_g[l]), csh2, csc2), p)

        h = modulate(rmsnorm(x, norm1_g[l]), sh1, sc1)
        mix, _, _ = token_mixer(h, p, lower_bounds[l], dwconv_grid, s_f, s_b)
        x = x + g1 * mix
        x = x + g2 * expert_choice_ffn(modulate(rmsnorm(x, norm2_g[l]), sh2, sc2), p)
    return rmsnorm(x, final_g)


_drawn_inputs = setup_inputs


def setup_inputs(seed=0):
    import zlib

    import numpy as np

    out = dict(_drawn_inputs(seed))
    spreads = {}
    factors = {'ctx': 6.908,
     'c_ctx': 5.569,
     'norm1_g': 2.703,
     'conv_bias': 16.882,
     'conv_ln_g': 34.736,
     'conv_ln_b': 38.463,
     'hgrn_norm_g': 13.742,
     'final_g': 8.747,
     'norm2_g': 8.0}
    for name, (base, spread) in spreads.items():
        noise = np.random.default_rng([zlib.crc32(name.encode()), seed]).standard_normal(out[name].shape)
        drawn = base * np.exp(spread * noise) if base else spread * noise
        out[name] = __import__('jax').numpy.asarray(drawn.astype(out[name].dtype))
    for name, factor in factors.items():
        out[name] = (out[name] * factor).astype(out[name].dtype)
    return out
```

```python
from contextlib import ExitStack

import concourse.bass as bass
from concourse import mybir

F32 = mybir.dt.float32
BF16 = mybir.dt.bfloat16
I32 = mybir.dt.int32
U32 = mybir.dt.uint32
ACT = mybir.ActivationFunctionType
ALU = mybir.AluOpType
AX = mybir.AxisListType

P = 128
D = 1024
KD = D // P
T = 2048
TC = 256
NT = T // P
SEG = 512
NSEG = T // SEG
CW = 512
NCT = CW // P
HEADS = 4
TAPS = 31
PAD = (TAPS - 1) // 2
GW = 64
GH = T // GW
CH = 32
NE = 16
CAP = 2 * T // NE
EPS = 1e-6
COL_A, COL_B, COL_Q, COL_I, COL_FF, COL_FB, COL_G = [512 * j for j in range(7)]
ROWW = D + NE
NOT_A_SLOT = 1000.0


class Mem:

    def __init__(self, nc, ctx):
        self.nc, self.ctx = nc, ctx

    def sb(self, name, shape, dt=F32):
        return self.ctx.enter_context(self.nc.sbuf_tensor(name, shape, dt))

    def ps(self, name, shape, dt=F32):
        return self.ctx.enter_context(self.nc.psum_tensor(name, shape, dt))

    def sem(self, name):
        return self.nc.alloc_semaphore(name)

    def sems(self, name, n):
        return [self.sem(f"{name}{i}") for i in range(n)]


def wait(engine, sem, value):
    if not (isinstance(value, int) and value == 0):
        engine.wait_ge(sem, value)


def peeled(engine, n, one):
    one(0)
    with engine.Fori(1, n) as i:
        one(i)


def triple(nc, out, pairs):
    n = len(pairs)
    for k, (lh, ll, rh, rl) in enumerate(pairs):
        nc.tensor.matmul(out, lh, rh, start=(k == 0), stop=False)
        nc.tensor.matmul(out, lh, rl, start=False, stop=False)
        last = nc.tensor.matmul(out, ll, rh, start=False, stop=(k == n - 1))
    return last


def modulate_stage(nc, K, I, scr):
    NCH = 12
    groups = [(0, 2)] + [(2 + 4 * s, 4) for s in range(NSEG)]
    with nc.cleanup_on_exit(), ExitStack() as ctx:
        m = Mem(nc, ctx)
        cc = m.sb("cc", [P, 2, KD])
        cth = m.sb("cth", [P, 2, KD])
        csil = m.sb("csil", [P, 2, KD])
        crep = m.sb("crep", [P, KD, P])
        cmix = m.sb("cmix", [P, KD, P])
        ada = m.sb("ada", [P, 2, KD, SEG])
        adab = m.sb("adab", [1, 2, SEG])
        modrow = m.sb("modrow", [P, 2 * D])
        modc = m.sb("modc", [P, 2 * KD, 2])
        n1c = m.sb("n1c", [P, KD])
        A1 = m.sb("A1", [P, KD, 2])
        n2r = m.sb("n2r", [P, D])
        rows = m.sb("rows", [P, 2, SEG])
        xb = m.sb("xb", [P, 2, 4, D])
        junk = m.sb("junk", [P, D])
        ss = m.sb("ss", [P, 5, 4])
        rstd = m.sb("rstd", [P, 5, 4])
        hf = m.sb("hf", [P, 2, SEG])
        pm = [m.ps(f"pm{i}", [P, SEG]) for i in range(2)]
        pt = [m.ps(f"pt{i}", [P, SEG]) for i in range(4)]

        c_in, col_in, n2_in = m.sem("c_in"), m.sem("col_in"), m.sem("n2_in")
        ada_in, x_in = m.sems("ada_in", 2), m.sems("x_in", 2)
        c_th, c_sil, c_rep = m.sem("c_th"), m.sem("c_sil"), m.sem("c_rep")
        mod_ps, mod_sb, modc_ps, modc_sb = m.sem("mod_ps"), m.sem("mod_sb"), m.sem("modc_ps"), m.sem("modc_sb")
        row_out = m.sems("row_out", 2)
        a1_ok, ss_ok, std_ok, rstd_ok, xn_ok = m.sem("a1_ok"), m.sem("ss_ok"), m.sem("std_ok"), m.sem("rstd_ok"), m.sem("xn_ok")
        tp_ps, hi_ok, hf_ok, lo_ok = m.sem("tp_ps"), m.sem("hi_ok"), m.sem("hf_ok"), m.sem("lo_ok")

        ada_v = I["ada_w"][0].rearrange("(p k) e -> p k e", k=KD)
        def chunks_after(g):
            return [] if g == 0 else [2 + 2 * g, 3 + 2 * g]

        with nc.Block() as block:
            @block.sync
            def _(sp):
                sp.dma_start(cc[:, 0, :], I["c"].rearrange("a (p k) -> (a p) k", k=KD)).then_inc(c_in, 16)
                sp.dma_start(cc[:, 1, :], I["c_ctx"].rearrange("(p k) -> p k", k=KD)).then_inc(c_in, 16)

                def load_ada(n):
                    if n >= 2:
                        sp.wait_ge(mod_ps, n - 1)
                    sp.dma_start(ada[:, n % 2], ada_v[:, :, n * SEG:(n + 1) * SEG]).then_inc(ada_in[n % 2], 16)
                    sp.dma_start(adab[:, n % 2], I["ada_b"][:, n * SEG:(n + 1) * SEG]).then_inc(ada_in[n % 2], 16)

                def load_x(g):
                    t0, n = groups[g]
                    src = I["ctx"][0] if g == 0 else I["x"][0, (t0 - 2) * P:(t0 - 2 + n) * P, :]
                    if g >= 2:
                        sp.wait_ge(tp_ps, KD * (g - 1))
                    sp.dma_start(xb[:, g % 2, 0:n, :], src.rearrange("(n p) d -> p n d", p=P)).then_inc(x_in[g % 2], 16)

                load_ada(0)
                load_ada(1)
                load_x(0)
                load_x(1)
                load_ada(2)
                load_ada(3)
                for g in range(1, 5):
                    for n in chunks_after(g):
                        load_ada(n)
                    if g + 1 < 5:
                        load_x(g + 1)

            @block.gpsimd
            def _(pool):
                with nc.allow_non_contiguous_dma(reason="1024 single norm weights into columns"):
                    pool.dma_start(n1c[:], I["norm1_g"][0].rearrange("(k p) -> p k", p=P)).then_inc(col_in, 16)
                pool.dma_start(n2r[:], I["norm2_g"][0].partition_broadcast(P)).then_inc(n2_in, 16)
                for n in range(4, NCH):
                    pool.wait_ge(mod_sb, n + 1)
                    pool.dma_start(scr["modrows"][n - 4:n - 3, :], rows[0:1, n % 2, :]).then_inc(row_out[n % 2], 16)
                for s in range(2):
                    pool.wait_ge(row_out[s], 16 * (NCH - 4) // 2)

            @block.scalar
            def _(act):
                act.wait_ge(c_in, 32)
                nc.scalar.activation(cth[:], cc[:], ACT.Tanh, scale=0.5).then_inc(c_th, 1)
                for g, (t0, n) in enumerate(groups):
                    act.wait_ge(x_in[g % 2], 16 * (g // 2 + 1))
                    for j in range(n):
                        if t0 + j:
                            act.wait_ge(ss_ok, t0 + j)
                        nc.scalar.activation(junk[:], xb[:, g % 2, j, :], ACT.Square,
                                             accum_out=ss[:, g, j:j + 1]).then_inc(ss_ok, 1)
                    act.wait_ge(ss_ok, sum(x[1] for x in groups[:g + 1]))
                    act.wait_ge(K["const_ok"], K["n_const"])
                    nc.scalar.activation(ss[:, g, 0:n], ss[:, g, 0:n], ACT.Sqrt, bias=K["eps"][:, 0:1],
                                         scale=1.0 / D).then_inc(std_ok, 1)
                    if g == 0:
                        act.wait_ge(a1_ok, 1)
                    s = 0 if g else 1
                    for k in range(KD):
                        q = g * KD + k
                        act.wait_ge(tp_ps, q + 1)
                        nc.scalar.activation(K["hhi"][:, k, t0 * P:(t0 + n) * P], pt[q % 4][:, 0:n * P], ACT.Identity,
                                             bias=modc[:, k, s:s + 1], scale=A1[:, k, s:s + 1]).then_inc(hi_ok, 1)

            @block.vector
            def _(dve):
                dve.wait_ge(c_th, 1)
                nc.vector.scalar_tensor_tensor(csil[:], cth[:], 1.0, cc[:], ALU.add, ALU.mult).then_inc(c_sil, 1)
                dve.wait_ge(c_sil, 1)
                nc.vector.tensor_scalar(crep[:], csil[:, 0, :].unsqueeze(2).broadcast_to([P, KD, P]), 0.5, None,
                                        ALU.mult).then_inc(c_rep, 1)
                for s in range(2):
                    nc.vector.tensor_scalar(cmix[:, :, 64 * s:64 * s + 64],
                                            csil[:, s, :].unsqueeze(2).broadcast_to([P, KD, 64]), 0.5, None,
                                            ALU.mult).then_inc(c_rep, 1)

                def mod_out(n):
                    dve.wait_ge(mod_ps, n + 1)
                    src = pm[n % 2][:]
                    if n < 4:
                        ins = nc.vector.tensor_copy(modrow[:, n * SEG:(n + 1) * SEG], src)
                    else:
                        if n >= 6:
                            dve.wait_ge(row_out[n % 2], 16 * ((n - 4) // 2))
                        if n in (8, 9):
                            dve.wait_ge(n2_in, 16)
                            ins = nc.vector.scalar_tensor_tensor(rows[:, n % 2, :], src, 1.0,
                                                                 n2r[:, (n - 8) * SEG:(n - 7) * SEG], ALU.add, ALU.mult)
                        else:
                            ins = nc.vector.tensor_copy(rows[:, n % 2, :], src)
                    ins.then_inc(mod_sb, 1)

                for n in range(4):
                    mod_out(n)
                for q in range(4):
                    dve.wait_ge(modc_ps, q + 1)
                    nc.vector.tensor_copy(modc[:, 4 * q:4 * q + 4, :],
                                          pt[q][:].rearrange("p (a s j) -> p a s j", a=4, s=2)[:, :, :, 0])\
                        .then_inc(modc_sb, 1)
                dve.wait_ge(modc_sb, 4)
                dve.wait_ge(col_in, 16)
                nc.vector.scalar_tensor_tensor(A1[:], modc[:, KD:2 * KD, :], 1.0,
                                               n1c[:].unsqueeze(2).broadcast_to([P, KD, 2]), ALU.add, ALU.mult)\
                    .then_inc(a1_ok, 1)
                dve.wait_ge(a1_ok, 1)
                for g, (t0, n) in enumerate(groups):
                    dve.wait_ge(std_ok, g + 1)
                    nc.vector.reciprocal(rstd[:, g, 0:n], ss[:, g, 0:n]).then_inc(rstd_ok, 1)
                    dve.wait_ge(rstd_ok, g + 1)
                    for j in range(n):
                        nc.vector.tensor_scalar(xb[:, g % 2, j, :], xb[:, g % 2, j, :], rstd[:, g, j:j + 1], None,
                                                ALU.mult).then_inc(xn_ok, 1)
                    s = 0 if g else 1
                    for k in range(KD):
                        q = g * KD + k
                        dve.wait_ge(hi_ok, q + 1)
                        nc.vector.tensor_scalar(hf[:, q % 2, 0:n * P], pt[q % 4][:, 0:n * P], A1[:, k, s:s + 1],
                                                modc[:, k, s:s + 1], ALU.mult, ALU.add).then_inc(hf_ok, 1)
                        dve.wait_ge(hf_ok, q + 1)
                        nc.vector.tensor_tensor(K["hlo"][:, k, t0 * P:(t0 + n) * P], hf[:, q % 2, 0:n * P],
                                                K["hhi"][:, k, t0 * P:(t0 + n) * P], ALU.subtract).then_inc(lo_ok, 1)
                    for c in chunks_after(g):
                        mod_out(c)

            @block.tensor
            def _(pe):
                pe.wait_ge(K["const_ok"], K["n_const"])
                pe.wait_ge(c_rep, 3)

                def mod_mm(n):
                    pe.wait_ge(ada_in[n % 2], 32 * (n // 2 + 1))
                    if n >= 2:
                        pe.wait_ge(mod_sb, n - 1)
                    w = cmix if n < 4 else crep
                    for k in range(KD):
                        nc.tensor.matmul(pm[n % 2][:], w[:, k, :], ada[:, n % 2, k, :], start=(k == 0), stop=False)
                    nc.tensor.matmul(pm[n % 2][:], K["ones"][0:1, :], adab[0:1, n % 2, :], start=False,
                                     stop=True).then_inc(mod_ps, 1)

                for n in range(4):
                    mod_mm(n)
                pe.wait_ge(mod_sb, 4)
                for q in range(4):
                    for a in range(4):
                        j = 4 * q + a
                        last = nc.tensor.transpose(pt[q][:, a * P:(a + 1) * P], modrow[:, j * P:(j + 1) * P], K["ident"][:])
                    last.then_inc(modc_ps, 1)
                tiles = 0
                for g, (t0, n) in enumerate(groups):
                    tiles += n
                    pe.wait_ge(xn_ok, tiles)
                    for k in range(KD):
                        q = g * KD + k
                        if q >= 4:
                            pe.wait_ge(hf_ok, q - 3)
                        else:
                            pe.wait_ge(modc_sb, 4)
                        for j in range(n):
                            last = nc.tensor.transpose(pt[q % 4][:, j * P:(j + 1) * P],
                                                       xb[:, g % 2, j, k * P:(k + 1) * P], K["ident"][:])
                        last.then_inc(tp_ps, 1)
                    for c in chunks_after(g):
                        mod_mm(c)


def conv_stage(nc, K, I, scr):
    with nc.cleanup_on_exit(), ExitStack() as ctx:
        m = Mem(nc, ctx)
        wst = m.sb("wst", [P, 4, KD, P])
        whi = m.sb("whi", [P, 4, KD, P], BF16)
        wlo = m.sb("wlo", [P, 4, KD, P], BF16)
        th = m.sb("th", [P, 2, SEG])
        u = m.sb("u", [P, 2, T])
        co = m.sb("co", [P, NCT, T])
        taps = m.sb("taps", [P, NCT, TAPS])
        cb = m.sb("cb", [P, NCT])
        lg = m.sb("lg", [P, 2, NCT])
        sq = m.sb("sq", [P, 2, SEG])
        rs = m.sb("rs", [P, 2, SEG])
        y = m.sb("y", [P, 2, SEG])
        tl = m.sb("tl", [P, 2, SEG])
        mh = m.sb("mh", [P, 2, SEG], BF16)
        ml = m.sb("ml", [P, 2, SEG], BF16)
        pa = [m.ps(f"pa{i}", [P, SEG]) for i in range(2)]
        pb = [m.ps(f"pb{i}", [P, SEG]) for i in range(2)]
        pmu = [m.ps(f"pmu{i}", [P, SEG]) for i in range(2)]
        pva = [m.ps(f"pva{i}", [P, SEG]) for i in range(2)]

        par_in, par_ok = m.sem("par_in"), m.sem("par_ok")
        w_in, w_hi, w_lo = m.sems("cw_in", 4), m.sem("cw_hi"), m.sem("cw_lo")
        ab_ps, b_th, u_ok, tap_ok = m.sem("ab_ps"), m.sem("b_th"), m.sem("u_ok"), m.sem("tap_ok")
        mu_ps, xc_ok, sq_ok, va_ps, sd_ok, rs_ok = (m.sem("mu_ps"), m.sem("xc_ok"), m.sem("sq_ok"), m.sem("va_ps"),
                                                    m.sem("sd_ok"), m.sem("rs_ok"))
        y_ok, yh_ok, t_ok, o_ok, mh_ok, ml_ok = (m.sem("y_ok"), m.sem("yh_ok"), m.sem("t_ok"), m.sem("o_ok"),
                                                 m.sem("mh_ok"), m.sem("ml_ok"))
        m_out = m.sems("m_out", 2)
        wv = I["w_in"][0].rearrange("(k p) n -> p k n", p=P)

        def slab_col(s):
            return (COL_A if s % 2 == 0 else COL_B) + (s // 2) * P

        with nc.Block() as block:
            @block.sync
            def _(sp):
                for s in range(2 * NCT):
                    if s >= 4:
                        sp.wait_ge(w_lo, s - 3)
                    sp.dma_start(wst[:, s % 4], wv[:, :, slab_col(s):slab_col(s) + P]).then_inc(w_in[s % 4], 16)
                for n in range(NSEG):
                    for c in range(NCT):
                        q = n * NCT + c
                        sp.wait_ge(ml_ok, q + 1)
                        for part, buf in ((0, mh), (1, ml)):
                            dst = scr["mixed"][4 * n:4 * n + 4, :, part, c, :]
                            sp.dma_start(dst.rearrange("t p j -> p t j"),
                                         buf[:, q % 2, :].rearrange("p (t j) -> p t j", j=P)).then_inc(m_out[q % 2], 16)
                for s in range(2):
                    sp.wait_ge(m_out[s], 32 * (NSEG * NCT // 2))

            @block.gpsimd
            def _(pool):
                with nc.allow_non_contiguous_dma(reason="per-channel constants into columns"):
                    for c in range(NCT):
                        pool.dma_start(taps[:, c, :], I["conv_taps"][0, :, c * P:(c + 1) * P].rearrange("k p -> p k"))\
                            .then_inc(par_in, 16)
                    pool.dma_start(cb[:], I["conv_bias"][0].rearrange("(c p) -> p c", p=P)).then_inc(par_in, 16)
                    pool.dma_start(lg[:, 0, :], I["conv_ln_g"][0].rearrange("(c p) -> p c", p=P)).then_inc(par_in, 16)
                    pool.dma_start(lg[:, 1, :], I["conv_ln_b"][0].rearrange("(c p) -> p c", p=P)).then_inc(par_in, 16)

            @block.scalar
            def _(act):
                def w_split(s):
                    act.wait_ge(w_in[s % 4], 16 * (s // 4 + 1))
                    if s >= 4:
                        act.wait_ge(ab_ps, 4 * ((s - 4) // 2 + 1))
                    nc.scalar.activation(whi[:, s % 4], wst[:, s % 4], ACT.Copy).then_inc(w_hi, 1)

                for s in range(4):
                    w_split(s)
                for c in range(NCT):
                    for n in range(NSEG):
                        q = c * NSEG + n
                        act.wait_ge(ab_ps, q + 1)
                        if q >= 2:
                            act.wait_ge(u_ok, q - 1)
                        nc.scalar.activation(th[:, q % 2], pb[q % 2][:], ACT.Tanh, scale=0.5).then_inc(b_th, 1)
                    for s in (2 * c + 4, 2 * c + 5):
                        if s < 2 * NCT:
                            w_split(s)
                for n in range(NSEG):
                    for c in range(NCT):
                        q = n * NCT + c
                        act.wait_ge(xc_ok, q + 1)
                        if q >= 2:
                            act.wait_ge(va_ps, q - 1)
                        nc.scalar.activation(sq[:, q % 2], co[:, c, n * SEG:(n + 1) * SEG], ACT.Square).then_inc(sq_ok, 1)
                    act.wait_ge(va_ps, NCT * (n + 1))
                    if n >= 2:
                        act.wait_ge(y_ok, NCT * (n - 1))
                    nc.scalar.activation(rs[:, n % 2], pva[n % 2][:], ACT.Sqrt, bias=K["eps"][:, 0:1]).then_inc(sd_ok, 1)
                    for c in range(NCT):
                        q = n * NCT + c
                        act.wait_ge(y_ok, q + 1)
                        sl = co[:, c, n * SEG:(n + 1) * SEG]
                        if q >= 2:
                            act.wait_ge(ml_ok, q - 1)
                        nc.scalar.activation(y[:, q % 2], sl, ACT.Identity, bias=lg[:, 1, c:c + 1],
                                             scale=lg[:, 0, c:c + 1]).then_inc(yh_ok, 1)
                        act.wait_ge(yh_ok, q + 1)
                        nc.scalar.activation(tl[:, q % 2], y[:, q % 2], ACT.Tanh).then_inc(t_ok, 1)
                        act.wait_ge(o_ok, q + 1)
                        if q >= 2:
                            act.wait_ge(m_out[q % 2], 32 * (q // 2))
                        nc.scalar.activation(mh[:, q % 2], y[:, q % 2], ACT.Copy).then_inc(mh_ok, 1)

            @block.vector
            def _(dve):
                def w_split(s):
                    dve.wait_ge(w_hi, s + 1)
                    nc.vector.tensor_tensor(wlo[:, s % 4], wst[:, s % 4], whi[:, s % 4], ALU.subtract).then_inc(w_lo, 1)

                for s in range(4):
                    w_split(s)
                dve.wait_ge(par_in, 16 * (NCT + 3))
                nc.vector.tensor_scalar(taps[:], taps[:], 0.5, None, ALU.mult).then_inc(par_ok, 1)
                nc.vector.tensor_scalar(lg[:], lg[:], 0.5, None, ALU.mult).then_inc(par_ok, 1)
                steps = 0
                for c in range(NCT):
                    up = u[:, c % 2, :]
                    for n in range(NSEG):
                        q = c * NSEG + n
                        dve.wait_ge(b_th, q + 1)
                        nc.vector.scalar_tensor_tensor(up[:, n * SEG:(n + 1) * SEG], th[:, q % 2], 1.0, pa[q % 2][:],
                                                       ALU.add, ALU.mult).then_inc(u_ok, 1)
                    for s in (2 * c + 4, 2 * c + 5):
                        if s < 2 * NCT:
                            w_split(s)
                    dve.wait_ge(u_ok, NSEG * (c + 1))
                    dve.wait_ge(par_ok, 2)
                    acc = co[:, c, :]
                    nc.vector.tensor_scalar(acc, up, taps[:, c, PAD:PAD + 1], cb[:, c:c + 1], ALU.mult, ALU.add)\
                        .then_inc(tap_ok, 1)
                    steps += 1
                    a3, u3 = acc.rearrange("p (r w) -> p r w", w=GW), up.rearrange("p (r w) -> p r w", w=GW)
                    for k in range(TAPS):
                        off = k - PAD
                        if off == 0:
                            continue
                        if c < NCT // 2:
                            lo, hi = max(0, -off), GW - max(0, off)
                            o, i = a3[:, :, lo:hi], u3[:, :, lo + off:hi + off]
                        else:
                            lo, hi = max(0, -off), GH - max(0, off)
                            o, i = acc[:, lo * GW:hi * GW], up[:, (lo + off) * GW:(hi + off) * GW]
                        dve.wait_ge(tap_ok, steps)
                        nc.vector.scalar_tensor_tensor(o, i, taps[:, c, k:k + 1], o, ALU.mult, ALU.add).then_inc(tap_ok, 1)
                        steps += 1
                dve.wait_ge(tap_ok, steps)

                def centre(n):
                    dve.wait_ge(mu_ps, n + 1)
                    for c in range(NCT):
                        sl = co[:, c, n * SEG:(n + 1) * SEG]
                        nc.vector.tensor_tensor(sl, sl, pmu[n % 2][:], ALU.subtract).then_inc(xc_ok, 1)

                centre(0)
                for n in range(NSEG):
                    if n + 1 < NSEG:
                        centre(n + 1)
                    dve.wait_ge(sd_ok, n + 1)
                    nc.vector.reciprocal(rs[:, n % 2], rs[:, n % 2]).then_inc(rs_ok, 1)
                    dve.wait_ge(rs_ok, n + 1)
                    for c in range(NCT):
                        sl = co[:, c, n * SEG:(n + 1) * SEG]
                        nc.vector.tensor_tensor(sl, sl, rs[:, n % 2], ALU.mult).then_inc(y_ok, 1)
                    for c in range(NCT):
                        q = n * NCT + c
                        dve.wait_ge(t_ok, q + 1)
                        nc.vector.scalar_tensor_tensor(y[:, q % 2], tl[:, q % 2], 1.0, y[:, q % 2], ALU.add, ALU.mult)\
                            .then_inc(o_ok, 1)
                        dve.wait_ge(mh_ok, q + 1)
                        if q >= 2:
                            dve.wait_ge(m_out[q % 2], 32 * (q // 2))
                        nc.vector.tensor_tensor(ml[:, q % 2], y[:, q % 2], mh[:, q % 2], ALU.subtract).then_inc(ml_ok, 1)

            @block.tensor
            def _(pe):
                for c in range(NCT):
                    pe.wait_ge(w_lo, 2 * c + 2)
                    for n in range(NSEG):
                        q = c * NSEG + n
                        if q >= 2:
                            pe.wait_ge(u_ok, q - 1)
                        t0 = TC + n * SEG
                        for s, bank in ((2 * c, pa), (2 * c + 1, pb)):
                            last = triple(nc, bank[q % 2][:], [
                                (whi[:, s % 4, k, :], wlo[:, s % 4, k, :], K["hhi"][:, k, t0:t0 + SEG],
                                 K["hlo"][:, k, t0:t0 + SEG]) for k in range(KD)])
                        last.then_inc(ab_ps, 1)
                pe.wait_ge(tap_ok, NCT * TAPS)

                def mean(n):
                    if n >= 2:
                        pe.wait_ge(xc_ok, NCT * (n - 1))
                    for c in range(NCT):
                        last = nc.tensor.matmul(pmu[n % 2][:], K["mean_cw"][:], co[:, c, n * SEG:(n + 1) * SEG],
                                                start=(c == 0), stop=(c == NCT - 1))
                    last.then_inc(mu_ps, 1)

                mean(0)
                for n in range(NSEG):
                    if n + 1 < NSEG:
                        mean(n + 1)
                    if n >= 2:
                        pe.wait_ge(sd_ok, n - 1)
                    for c in range(NCT):
                        q = n * NCT + c
                        pe.wait_ge(sq_ok, q + 1)
                        nc.tensor.matmul(pva[n % 2][:], K["mean_cw"][:], sq[:, q % 2], start=(c == 0),
                                         stop=(c == NCT - 1)).then_inc(va_ps, 1)


def heads_stage(nc, K, I, scr):
    UNITS = [(0, -1), (1, -1), (0, 0), (1, 3), (0, 1), (1, 2), (0, 2), (1, 1), (0, 3), (1, 0)]
    NU = len(UNITS)
    NX = NU - 2
    CS = SEG // CH
    BLK = P // CH
    CHAIN = 2 * (TC // CH) + NX * CS + NX
    SLABS = [COL_Q, COL_I, COL_FF, COL_FB, COL_G]

    def size(i):
        return TC if UNITS[i][1] < 0 else SEG

    def tok0(i):
        return 0 if UNITS[i][1] < 0 else TC + SEG * UNITS[i][1]

    def xs(i):
        return max(0, i - 2)

    def order(i):
        n = size(i) // CH
        return range(n) if UNITS[i][0] == 0 else range(n - 1, -1, -1)

    chain_at, total = [], 0
    for i in range(NU):
        chain_at.append(total)
        total += size(i) // CH + (1 if UNITS[i][1] >= 0 else 0)
    assert total == CHAIN
    seen, first = set(), []
    for d, s in UNITS:
        first.append(s not in seen)
        seen.add(s)

    with nc.cleanup_on_exit(), ExitStack() as ctx:
        m = Mem(nc, ctx)
        wst = m.sb("hwst", [P, 5, KD, P])
        whi = m.sb("hwhi", [P, 5, KD, P], BF16)
        wlo = m.sb("hwlo", [P, 5, KD, P], BF16)
        qT = m.sb("qT", [P, T])
        oT = m.sb("oT", [P, T])
        v = m.sb("v", [P, 2 + NT, P])
        G = m.sb("G", [P, 2, SEG])
        KK = m.sb("KK", [P, 2, SEG])
        B = m.sb("B", [P, 2, SEG])
        E = m.sb("E", [P, 2, SEG])
        QI = m.sb("QI", [P, 2, SEG])
        KT = m.sb("KT", [P, 2, SEG])
        AT = m.sb("AT", [P, 2, SEG])
        S = m.sb("S", [P, 2, CS + 1, P])
        sm = m.sb("sm", [P, 2, 3, CS])
        se = m.sb("se", [P, 2, 3, CS])
        lbr = m.sb("lbr", [P, 2, 2, HEADS])
        lbd = m.sb("lbd", [P, 2, HEADS])
        gh = m.sb("gh", [P, 2, HEADS])
        gb = m.sb("gb", [P, 2, HEADS])
        lh = m.sb("lh", [P, 2, 2])
        ng = m.sb("ng", [P, HEADS])
        ngh = m.sb("ngh", [P, 1])
        segm = m.sb("segm", [P, SEG])
        msk = m.sb("msk", [P, 2, SEG])
        mh = m.sb("hmh", [P, 2, SEG], BF16)
        ml = m.sb("hml", [P, 2, SEG], BF16)
        pu = [m.ps(f"pu{i}", [P, SEG]) for i in range(4)]
        pj, pk, pat, po = m.ps("pj", [P, SEG]), m.ps("pk", [P, SEG]), m.ps("pat", [P, SEG]), m.ps("po", [P, SEG])

        flag = m.sb("hflag", [1, 1])
        pflag = m.sb("hpflag", [1, 1])

        hpar_in, lb_ok, msk_ok, zero_ok = m.sem("hpar_in"), m.sem("lb_ok"), m.sem("msk_ok"), m.sem("zero_ok")
        hd_ok = m.sem("hd_ok")
        w_in, w_hi, w_lo = m.sems("hw_in", 5), m.sem("hw_hi"), m.sem("hw_lo")
        qv_ps, qv_ok = m.sem("qv_ps"), m.sem("qv_ok")
        pj_ps, th_ok, f_ok, kk_ok, lf_ok, b_ok = (m.sem("pj_ps"), m.sem("hth_ok"), m.sem("f_ok"), m.sem("kk_ok"),
                                                  m.sem("lf_ok"), m.sem("b_ok"))
        sm_ok, d_ok, ex_ok, qh_ok, qi_ok, kh_ok, kd_ok = (m.sem("sm_ok"), m.sem("d_ok"), m.sem("ex_ok"), m.sem("qh_ok"),
                                                          m.sem("qi_ok"), m.sem("kh_ok"), m.sem("kd_ok"))
        kt_ps, kt_ok, at_ps, at_ok, u_ps, ch_ok, o_ps, o_ok = (
            m.sem("kt_ps"), m.sem("kt_ok"), m.sem("at_ps"), m.sem("at_ok"), m.sem("u_ps"), m.sem("ch_ok"),
            m.sem("o_ps"), m.sem("ho_ok"))
        osq_ok, ms_ps, g_ps, sd_ok, rs_ok, g_th = (m.sem("osq_ok"), m.sem("ms_ps"), m.sem("g_ps"), m.sem("hsd_ok"),
                                                   m.sem("hrs_ok"), m.sem("g_th"))
        y_ok, sg_ok, hm_ok, hmh_ok, hml_ok = (m.sem("hy_ok"), m.sem("sg_ok"), m.sem("hm_ok"), m.sem("hmh_ok"),
                                              m.sem("hml_ok"))
        m_out = m.sems("hm_out", 2)
        wv = I["w_in"][0].rearrange("(k p) n -> p k n", p=P)
        ms_bank = [pk, pat, pj, po]
        sq_buf = [KT[:, 0], KT[:, 1], G[:, 0], G[:, 1]]
        rs_buf = [KK[:, 0], KK[:, 1], E[:, 0], E[:, 1]]
        tg_buf = [B[:, 0], B[:, 1], QI[:, 0], QI[:, 1]]

        with nc.Block() as block:
            @block.sync
            def _(sp):
                def one(h):
                    for j, col in enumerate(SLABS):
                        if j == 0:
                            wait(sp, w_lo, h * 5)
                        sp.dma_start(wst[:, j], wv[:, :, bass.ds(h * P + col, P)]).then_inc(w_in[j], 16)
                    for n in range(NSEG):
                        wait(sp, hml_ok, h * NSEG + n + 1)
                        for part, buf in ((0, mh), (1, ml)):
                            dst = scr["mixed"][4 * n:4 * n + 4, :, part, bass.ds(h + NCT, 1), :]
                            sp.dma_start(dst.rearrange("t p a j -> p t (a j)"),
                                         buf[:, n % 2, :].rearrange("p (t j) -> p t j", j=P)).then_inc(m_out[n % 2], 16)
                peeled(sp, HEADS, one)
                for s in range(2):
                    wait(sp, m_out[s], 32 * (HEADS * NSEG // 2))

            @block.gpsimd
            def _(pool):
                with nc.allow_non_contiguous_dma(reason="per-channel constants into columns"):
                    for l in range(2):
                        for d in range(2):
                            pool.dma_start(lbr[:, l, d, :], I["hgrn_lb_logits"][l, d].rearrange("(h p) -> p h", p=P))\
                                .then_inc(hpar_in, 16)
                    pool.dma_start(ng[:], I["hgrn_norm_g"][0].rearrange("(h p) -> p h", p=P)).then_inc(hpar_in, 16)
                nc.gpsimd.memset(segm[:], 1.0).then_inc(msk_ok, 1)
                nc.gpsimd.memset(msk[:], 1.0).then_inc(msk_ok, 1)
                wait(pool, msk_ok, 2)
                nc.gpsimd.memset(segm[:, 0:SEG:CH], 0.0).then_inc(msk_ok, 1)
                pat4 = [[0, SEG // P], [-CH, BLK], [0, CH]]
                for d in range(2):
                    mv = msk[:, d, :].rearrange("p (r b i) -> p r b i", r=SEG // P, b=BLK)
                    conds = [(0, 1, pat4), (CH - 1, -1, [[0, SEG // P], [CH, BLK], [0, CH]]),
                             (0, -1 if d == 0 else 1,
                              [[0, SEG // P], [CH if d == 0 else -CH, BLK], [1 if d == 0 else -1, CH]])]
                    for n, (base, mult, pattern) in enumerate(conds):
                        wait(pool, msk_ok, 3 + 3 * d + n)
                        nc.gpsimd.affine_select(out=mv, in_=mv, compare_op=ALU.is_ge, fill=0.0, base=base,
                                                pattern=pattern, channel_multiplier=mult).then_inc(msk_ok, 1)
                nc.gpsimd.memset(pflag[:], 0.0)
                nc.gpsimd.memset(AT[:], 0.0).then_inc(zero_ok, 1)
                wait(pool, zero_ok, 1)
                def one(h):
                    for i in range(NU):
                        p, n = i % 2, size(i)
                        wait(pool, f_ok, h * NU + i + 1)
                        wait(pool, kt_ps, h * NU + max(0, i - 1))
                        if i < 2:
                            wait(pool, hml_ok, h * NSEG)
                        nc.gpsimd.tensor_tensor(pflag[:], pflag[:], pflag[:], ALU.mult)
                        nc.gpsimd.tensor_scalar(KK[:, p, 0:n], G[:, p, 0:n], -1.0, 1.0, ALU.mult, ALU.add)\
                            .then_inc(kk_ok, 1)
                        wait(pool, ex_ok, h * NU + i + 1)
                        wait(pool, kk_ok, h * NU + i + 1)
                        nc.gpsimd.tensor_tensor(B[:, p, 0:n], KK[:, p, 0:n], B[:, p, 0:n], ALU.mult).then_inc(kh_ok, 1)
                        wait(pool, kh_ok, h * NU + i + 1)
                        c3 = lambda t: t[:, p, 0:n].rearrange("p (c j) -> p c j", j=CH)
                        nc.gpsimd.tensor_tensor(c3(KK), c3(B), se[:, p, 1, 0:n // CH].unsqueeze(2)
                                                .broadcast_to([P, n // CH, CH]), ALU.mult).then_inc(kd_ok, 1)
                peeled(pool, HEADS, one)

            @block.scalar
            def _(act):
                wait(act, lb_ok, 1)
                nc.scalar.activation(lbd[:], lbd[:], ACT.Tanh, scale=0.5).then_inc(lb_ok, 1)

                def one(h):
                    for j in range(5):
                        wait(act, w_in[j], h * 16 + 16)
                        wait(act, ms_ps, h * NSEG)
                        nc.scalar.activation(whi[:, j], wst[:, j], ACT.Copy).then_inc(w_hi, 1)
                    for n in range(4):
                        wait(act, qv_ps, h * 9 + n + 1)
                        wait(act, qi_ok, h * NX)
                        nc.scalar.activation(qT[:, n * SEG:(n + 1) * SEG], pu[n][:], ACT.Copy).then_inc(qv_ok, 1)
                    for n in range(5):
                        wait(act, qv_ps, h * 9 + n + 5)
                        t0, k = (0, 2) if n == 4 else (2 + 4 * n, 4)
                        bank = pj if n == 4 else pu[n]
                        wait(act, o_ps, h * NX)
                        nc.scalar.activation(v[:, t0:t0 + k, :], bank[:, 0:k * P].rearrange("p (t j) -> p t j", j=P),
                                             ACT.Copy).then_inc(qv_ok, 1)

                    def gate(i):
                        p, n = i % 2, size(i)
                        wait(act, pj_ps, h * NU + i + 1)
                        wait(act, kk_ok, h * NU + max(0, i - 1))
                        if i < 2:
                            wait(act, hml_ok, h * NSEG)
                        nc.scalar.activation(G[:, p, 0:n], pj[:, 0:n], ACT.Tanh, scale=0.5).then_inc(th_ok, 1)

                    def logs(i):
                        p, n = i % 2, size(i)
                        wait(act, f_ok, h * NU + i + 1)
                        wait(act, at_ps, h * NX + max(0, xs(i) - 1) if i >= 2 else h * NX)
                        nc.scalar.activation(E[:, p, 0:n], G[:, p, 0:n], ACT.Ln).then_inc(lf_ok, 1)

                    def exps(i):
                        p, n = i % 2, size(i)
                        wait(act, d_ok, h * NU + i + 1)
                        wait(act, kd_ok, h * NU + max(0, i - 1))
                        wait(act, qi_ok, h * NX + max(0, xs(i) - 1) if i >= 2 else h * NX)
                        wait(act, ch_ok, h * CHAIN + (chain_at[i - 1] if i >= 2 else 0))
                        nc.scalar.activation(se[:, p, :, 0:n // CH], sm[:, p, :, 0:n // CH], ACT.Exp).then_inc(sm_ok, 1)
                        if UNITS[i][1] >= 0:
                            nc.scalar.activation(E[:, p, 0:n], B[:, p, 0:n], ACT.Exp).then_inc(sm_ok, 1)
                        nc.scalar.activation(B[:, p, 0:n], B[:, p, 0:n], ACT.Exp, scale=-1.0).then_inc(ex_ok, 1)

                    def turn(i):
                        p, n = i % 2, size(i)
                        wait(act, kt_ps, h * NU + i + 1)
                        wait(act, u_ps, h * NU + max(0, i - 1))
                        if i < 2:
                            wait(act, hml_ok, h * NSEG)
                        nc.scalar.activation(KT[:, p, 0:n], pk[:, 0:n], ACT.Copy).then_inc(kt_ok, 1)

                    gate(0)
                    logs(0)
                    exps(0)
                    for i in range(NU):
                        if i + 1 < NU:
                            gate(i + 1)
                        turn(i)
                        if i + 1 < NU:
                            logs(i + 1)
                            exps(i + 1)
                    wait(act, o_ok, h * NX + NX)
                    wait(act, u_ps, h * NU + NU)
                    wait(act, kk_ok, h * NU + NU)
                    for n in range(NSEG):
                        nc.scalar.activation(sq_buf[n], oT[:, n * SEG:(n + 1) * SEG], ACT.Square).then_inc(osq_ok, 1)
                    wait(act, kt_ps, h * NU + NU)
                    wait(act, at_ps, h * NX + NX)
                    for n in range(NSEG):
                        wait(act, ms_ps, h * NSEG + n + 1)
                        nc.scalar.activation(rs_buf[n], ms_bank[n][:], ACT.Sqrt, bias=K["eps"][:, 0:1])\
                            .then_inc(sd_ok, 1)
                    wait(act, o_ps, h * NX + NX)
                    for n in range(NSEG):
                        wait(act, g_ps, h * NSEG + n + 1)
                        nc.scalar.activation(tg_buf[n], pu[n][:], ACT.Tanh, scale=0.5).then_inc(g_th, 1)
                    for n in range(NSEG):
                        wait(act, hm_ok, h * NSEG + n + 1)
                        wait(act, m_out[n % 2], h * 64 + 32 * (n // 2))
                        nc.scalar.activation(mh[:, n % 2], oT[:, n * SEG:(n + 1) * SEG], ACT.Copy).then_inc(hmh_ok, 1)
                peeled(act, HEADS, one)

            @block.vector
            def _(dve):
                wait(dve, hpar_in, 80)
                nc.vector.tensor_tensor(lbd[:], lbr[:, 0], lbr[:, 1], ALU.subtract).then_inc(lb_ok, 1)
                wait(dve, lb_ok, 2)
                nc.vector.tensor_scalar(gh[:], lbd[:], -0.25, 0.25, ALU.mult, ALU.add).then_inc(lb_ok, 1)
                nc.vector.tensor_scalar(gb[:], lbd[:], 0.25, 0.75, ALU.mult, ALU.add).then_inc(lb_ok, 1)
                nc.vector.tensor_scalar(ng[:], ng[:], 0.5, None, ALU.mult).then_inc(lb_ok, 1)
                wait(dve, lb_ok, 5)
                wait(dve, msk_ok, 9)
                wait(dve, zero_ok, 1)

                def one(h):
                    wait(dve, hml_ok, h * NSEG)
                    for d in range(2):
                        nc.vector.tensor_copy(lh[:, d, 0:1], gh[:, d, bass.ds(h, 1)]).then_inc(hd_ok, 1)
                        nc.vector.tensor_copy(lh[:, d, 1:2], gb[:, d, bass.ds(h, 1)]).then_inc(hd_ok, 1)
                    nc.vector.tensor_copy(ngh[:], ng[:, bass.ds(h, 1)]).then_inc(hd_ok, 1)
                    wait(dve, o_ps, h * NX)
                    nc.vector.memset(S[:, :, 0, :], 0.0).then_inc(hd_ok, 1)
                    for j in range(5):
                        wait(dve, w_hi, h * 5 + j + 1)
                        nc.vector.tensor_tensor(wlo[:, j], wst[:, j], whi[:, j], ALU.subtract).then_inc(w_lo, 1)
                    wait(dve, hd_ok, h * 6 + 6)

                    def forget(i):
                        p, n, d = i % 2, size(i), UNITS[i][0]
                        wait(dve, th_ok, h * NU + i + 1)
                        nc.vector.tensor_scalar(G[:, p, 0:n], G[:, p, 0:n], lh[:, d, 0:1], lh[:, d, 1:2], ALU.mult,
                                                ALU.add).then_inc(f_ok, 1)

                    def sums(i):
                        p, n, d = i % 2, size(i), UNITS[i][0]
                        nch = n // CH
                        mid, end = (CH // 2 - 1, CH - 1) if d == 0 else (CH // 2, 0)
                        wait(dve, lf_ok, h * NU + i + 1)
                        wait(dve, kd_ok, h * NU + max(0, i - 1))
                        way = slice(0, n) if d == 0 else slice(n - 1, None, -1)
                        nc.vector.tensor_tensor_scan(B[:, p, way], segm[:, 0:n], E[:, p, way], 0.0, ALU.mult, ALU.add)\
                            .then_inc(b_ok, 1)
                        b3 = B[:, p, 0:n].rearrange("p (c j) -> p c j", j=CH)
                        wait(dve, b_ok, h * 3 * NU + 3 * i + 1)
                        wait(dve, ex_ok, h * NU + max(0, i - 1))
                        nc.vector.tensor_copy(sm[:, p, 0, 0:nch], b3[:, :, mid]).then_inc(b_ok, 1)
                        nc.vector.tensor_copy(sm[:, p, 2, 0:nch], b3[:, :, end]).then_inc(b_ok, 1)
                        wait(dve, b_ok, h * 3 * NU + 3 * i + 3)
                        nc.vector.tensor_tensor(sm[:, p, 1, 0:nch], sm[:, p, 2, 0:nch], sm[:, p, 0, 0:nch],
                                                ALU.subtract)
                        nc.vector.tensor_tensor(b3, b3, sm[:, p, 0, 0:nch].unsqueeze(2).broadcast_to([P, nch, CH]),
                                                ALU.subtract).then_inc(d_ok, 1)

                    def decay_q(i):
                        p = i % 2
                        if UNITS[i][1] < 0:
                            return
                        t0 = UNITS[i][1] * SEG
                        wait(dve, ex_ok, h * NU + i + 1)
                        wait(dve, qv_ok, h * 9 + 4)
                        nc.vector.tensor_tensor(E[:, p], qT[:, t0:t0 + SEG], E[:, p], ALU.mult).then_inc(qh_ok, 1)
                        wait(dve, qh_ok, h * NX + xs(i) + 1)
                        wait(dve, o_ps, h * NX + max(0, xs(i) - 1))
                        c3 = lambda t: t[:, p].rearrange("p (c j) -> p c j", j=CH)
                        nc.vector.tensor_tensor(c3(QI), c3(E), se[:, p, 0].unsqueeze(2).broadcast_to([P, CS, CH]),
                                                ALU.mult).then_inc(qi_ok, 1)

                    def mask(i):
                        if UNITS[i][1] < 0:
                            return
                        wait(dve, at_ps, h * NX + xs(i) + 1)
                        wait(dve, o_ps, h * NX + max(0, xs(i) - 1))
                        nc.vector.memset(flag[:], 0.0)
                        nc.vector.copy_predicated(AT[:, i % 2], msk[:, UNITS[i][0]].bitcast(U32), pat[:])\
                            .then_inc(at_ok, 1)

                    def chain(i):
                        p, d = i % 2, UNITS[i][0]
                        done = chain_at[i]
                        if UNITS[i][1] >= 0:
                            wait(dve, o_ps, h * NX + max(0, xs(i) - 1))
                            prev = size(i - 2) // CH
                            wait(dve, ch_ok, h * CHAIN + chain_at[i - 1])
                            nc.vector.tensor_copy(S[:, d, 0, :], S[:, d, prev, :]).then_inc(ch_ok, 1)
                            done += 1
                        wait(dve, u_ps, h * NU + i + 1)
                        for n, c in enumerate(order(i)):
                            wait(dve, ch_ok, h * CHAIN + done)
                            nc.vector.scalar_tensor_tensor(S[:, d, n + 1, :], S[:, d, n, :], se[:, p, 2, c:c + 1],
                                                           pu[c % BLK][:, (c // BLK) * P:(c // BLK + 1) * P],
                                                           ALU.mult, ALU.add).then_inc(ch_ok, 1)
                            done += 1

                    def collect(i):
                        if i < 2:
                            return
                        t0 = UNITS[i][1] * SEG
                        wait(dve, o_ps, h * NX + xs(i) + 1)
                        if first[i]:
                            ins = nc.vector.tensor_copy(oT[:, t0:t0 + SEG], po[:])
                        else:
                            wait(dve, o_ok, h * NX + xs(i))
                            ins = nc.vector.tensor_tensor(oT[:, t0:t0 + SEG], oT[:, t0:t0 + SEG], po[:], ALU.add)
                        ins.then_inc(o_ok, 1)

                    forget(0)
                    sums(0)
                    decay_q(0)
                    for i in range(NU):
                        mask(i)
                        if i + 1 < NU:
                            forget(i + 1)
                        chain(i)
                        if i + 1 < NU:
                            sums(i + 1)
                        if i >= 1:
                            collect(i - 1)
                        if i + 1 < NU:
                            decay_q(i + 1)
                    collect(NU - 1)
                    for n in range(NSEG):
                        wait(dve, sd_ok, h * NSEG + n + 1)
                        nc.vector.reciprocal(rs_buf[n], rs_buf[n]).then_inc(rs_ok, 1)
                    for n in range(NSEG):
                        sl = oT[:, n * SEG:(n + 1) * SEG]
                        wait(dve, rs_ok, h * NSEG + n + 1)
                        wait(dve, o_ok, h * NX + NX)
                        nc.vector.tensor_tensor(sl, sl, rs_buf[n], ALU.mult).then_inc(y_ok, 1)
                        wait(dve, g_th, h * NSEG + n + 1)
                        nc.vector.scalar_tensor_tensor(tg_buf[n], tg_buf[n], 1.0, pu[n][:], ALU.add, ALU.mult)\
                            .then_inc(sg_ok, 1)
                        wait(dve, y_ok, h * NSEG + n + 1)
                        wait(dve, sg_ok, h * NSEG + n + 1)
                        nc.vector.scalar_tensor_tensor(sl, sl, ngh[:, 0:1], tg_buf[n], ALU.mult, ALU.mult)\
                            .then_inc(hm_ok, 1)
                        wait(dve, hmh_ok, h * NSEG + n + 1)
                        wait(dve, m_out[n % 2], h * 64 + 32 * (n // 2))
                        nc.vector.tensor_tensor(ml[:, n % 2], sl, mh[:, n % 2], ALU.subtract).then_inc(hml_ok, 1)
                peeled(dve, HEADS, one)

            @block.tensor
            def _(pe):
                def one(h):
                    def pairs(j, t0, n):
                        return [(whi[:, j, k, :], wlo[:, j, k, :], K["hhi"][:, k, t0:t0 + n], K["hlo"][:, k, t0:t0 + n])
                                for k in range(KD)]

                    wait(pe, w_lo, h * 5 + 1)
                    wait(pe, sg_ok, h * NSEG)
                    for n in range(4):
                        last = triple(nc, pu[n][:], pairs(0, TC + n * SEG, SEG))
                        if n < 3:
                            last.then_inc(qv_ps, 1)
                    last.then_inc(qv_ps, 1)
                    wait(pe, w_lo, h * 5 + 2)
                    for n in range(5):
                        t0, cnt = (0, 2) if n == 4 else (2 + 4 * n, 4)
                        bank = pj if n == 4 else pu[n]
                        if n < 4:
                            wait(pe, qv_ok, h * 9 + n + 1)
                        for t in range(t0, t0 + cnt):
                            last = triple(nc, bank[:, (t - t0) * P:(t - t0 + 1) * P], [
                                (K["hhi"][:, k, t * P:(t + 1) * P], K["hlo"][:, k, t * P:(t + 1) * P],
                                 whi[:, 1, k, :], wlo[:, 1, k, :]) for k in range(KD)])
                        last.then_inc(qv_ps, 1)

                    def project(i):
                        j = 2 + UNITS[i][0]
                        if i == 0:
                            wait(pe, w_lo, h * 5 + 4)
                            wait(pe, qv_ok, h * 9 + 9)
                        wait(pe, th_ok, h * NU + i)
                        triple(nc, pj[:, 0:size(i)], pairs(j, tok0(i), size(i))).then_inc(pj_ps, 1)

                    def scores(i):
                        p, tiles = i % 2, size(i) // P
                        wait(pe, kd_ok, h * NU + i + 1)
                        wait(pe, kt_ok, h * NU + i)
                        for t in range(tiles):
                            last = nc.tensor.transpose(pk[:, t * P:(t + 1) * P], KK[:, p, t * P:(t + 1) * P],
                                                       K["ident"][:])
                        last.then_inc(kt_ps, 1)
                        if UNITS[i][1] >= 0:
                            wait(pe, qh_ok, h * NX + xs(i) + 1)
                            wait(pe, at_ok, h * NX + xs(i))
                            for t in range(tiles):
                                last = nc.tensor.matmul(pat[:, t * P:(t + 1) * P], B[:, p, t * P:(t + 1) * P],
                                                        E[:, p, t * P:(t + 1) * P], start=True, stop=True)
                            last.then_inc(at_ps, 1)

                    def updates(i):
                        p, tiles, v0 = i % 2, size(i) // P, tok0(i) // P
                        wait(pe, kt_ok, h * NU + i + 1)
                        wait(pe, ch_ok, h * CHAIN + chain_at[i])
                        for t in range(tiles):
                            for j in range(BLK):
                                rows = slice(CH * j, CH * (j + 1))
                                last = nc.tensor.matmul(pu[j][:, t * P:(t + 1) * P], KT[rows, p, t * P:(t + 1) * P],
                                                        v[rows, v0 + t, :], start=True, stop=True)
                        last.then_inc(u_ps, 1)

                    def outputs(i):
                        if i < 2:
                            return
                        p, d, v0 = i % 2, UNITS[i][0], tok0(i) // P
                        wait(pe, at_ok, h * NX + xs(i) + 1)
                        wait(pe, qi_ok, h * NX + xs(i) + 1)
                        wait(pe, o_ok, h * NX + xs(i))
                        wait(pe, ch_ok, h * CHAIN + (chain_at[i + 1] if i + 1 < NU else CHAIN))
                        for t in range(SEG // P):
                            nc.tensor.matmul(po[:, t * P:(t + 1) * P], v[:, v0 + t, :], AT[:, p, t * P:(t + 1) * P],
                                             start=(t == 0), stop=False, skip_group_check=True)
                        for n, c in enumerate(order(i)):
                            last = nc.tensor.matmul(po[:, c * CH:(c + 1) * CH], S[:, d, n, :], QI[:, p, c * CH:(c + 1) * CH],
                                                    start=False, stop=(n == CS - 1), skip_group_check=True)
                        last.then_inc(o_ps, 1)

                    project(0)
                    for i in range(NU):
                        if i + 1 < NU:
                            project(i + 1)
                        scores(i)
                        if i >= 1:
                            outputs(i - 1)
                        updates(i)
                    outputs(NU - 1)
                    wait(pe, w_lo, h * 5 + 5)
                    for n in range(NSEG):
                        triple(nc, pu[n][:], pairs(4, TC + n * SEG, SEG)).then_inc(g_ps, 1)
                    wait(pe, o_ok, h * NX + NX)
                    for n in range(NSEG):
                        wait(pe, osq_ok, h * NSEG + n + 1)
                        nc.tensor.matmul(ms_bank[n][:], K["mean_p"][:], sq_buf[n], start=True, stop=True)\
                            .then_inc(ms_ps, 1)
                peeled(pe, HEADS, one)


def outproj_stage(nc, K, I, scr):
    with nc.cleanup_on_exit(), ExitStack() as ctx:
        m = Mem(nc, ctx)
        wst = m.sb("owst", [P, 2, KD, SEG])
        whi = m.sb("owhi", [P, KD, D], BF16)
        wlo = m.sb("owlo", [P, KD, D], BF16)
        rw = m.sb("rw", [P, KD, NE])
        mrow = m.sb("mrow", [P, 3, D])
        xt = m.sb("xt", [P, 2, D])
        mx = m.sb("mx", [P, 2, 2, KD, P], BF16)
        t1 = m.sb("t1", [P, 2, D])
        x1 = m.sb("x1", [P, 2, D])
        junk = m.sb("ojunk", [P, D])
        st = m.sb("st", [P, 2, 4])
        h2 = m.sb("h2", [P, 2, D])
        row32 = m.sb("row", [P, 2, ROWW], I32)
        row = row32[:].bitcast(BF16)
        prob = row32[:, :, D:ROWW].bitcast(F32)
        h2T = m.sb("h2T", [P, D])
        nm = m.sb("nm", [P, 2, 4])
        pe_ = m.sb("pexp", [P, 2, NE])
        pT = m.sb("pT", [NE, T])
        pout = [m.ps(f"pout{i}", [P, 2, SEG]) for i in range(2)]
        ptp = m.ps("ptp", [P, 2, SEG])
        plg = m.ps("plg", [P, SEG])[:, 0:NE]
        ppt = m.ps("ppt", [P, SEG])[0:NE, 0:P]

        w_in, w_hi, w_lo, r_in = m.sems("ow_in", 2), m.sem("ow_hi"), m.sem("ow_lo"), m.sem("or_in")
        x_in, m_in = m.sems("ox_in", 2), m.sems("om_in", 2)
        out_ps, t1_ok, x1_ok, ss_ok, sd_ok, rs_ok, hn_ok, h2_ok = (
            m.sems("oo_ps", 2), m.sems("ot1", 2), m.sems("ox1", 2), m.sems("oss", 2), m.sems("osd", 2),
            m.sems("ors", 2), m.sems("ohn", 2), m.sems("oh2", 2))
        hi_ok, lo_ok, tp_ps, tp_ok, lg_ps, mx_ok, ex_ok, ri_ok, pr_ok, pt_ps, pt_ok = (
            m.sems("ohi", 2), m.sems("olo", 2), m.sems("otp", 2), m.sems("otc", 2), m.sems("olg", 2), m.sems("omx", 2),
            m.sems("oex", 2), m.sems("ori", 2), m.sems("opr", 2), m.sems("oppt", 2), m.sems("optc", 2))
        x1_out, row_out = m.sems("x1_out", 2), m.sems("orow_out", 2)
        pT_out = m.sem("pT_out")
        wv = I["w_out"][0].rearrange("(k p) n -> p k n", p=P)

        def steps(engine, front, back):
            def two(i):
                front(i * 2 + 1, 1, i)
                back(i * 2, 0, i)
                front(i * 2 + 2, 0, i + 1)
                back(i * 2 + 1, 1, i)

            front(0, 0, 0)
            peeled(engine, NT // 2 - 1, two)
            front(NT - 1, 1, NT // 2 - 1)
            back(NT - 2, 0, NT // 2 - 1)
            back(NT - 1, 1, NT // 2 - 1)

        def tile_rows(ap, t):
            return ap[bass.ds(t * P, P), :]

        with nc.Block() as block:
            @block.sync
            def _(sp):
                for c in range(2):
                    sp.dma_start(wst[:, c], wv[:, :, c * SEG:(c + 1) * SEG]).then_inc(w_in[c], 16)
                sp.dma_start(rw[:], I["router_w"][0].rearrange("(k p) e -> p k e", p=P)).then_inc(r_in, 16)
                for j, r in enumerate((0, 2, 1)):
                    sp.dma_start(mrow[:, j], scr["modrows"][2 * r:2 * r + 2, :].rearrange("a n -> (a n)")
                                 .partition_broadcast(P)).then_inc(r_in, 16)

                def front(t, p, n):
                    wait(sp, x1_ok[p], n)
                    sp.dma_start(xt[:, p], tile_rows(I["x"][0], t)).then_inc(x_in[p], 16)
                    wait(sp, out_ps[p], n)
                    sp.dma_start(mx[:, p], scr["mixed"][bass.ds(t, 1), :, :, :, :].rearrange("t p a c j -> (t p) a c j"))\
                        .then_inc(m_in[p], 16)

                def back(t, p, n):
                    wait(sp, x1_ok[p], n + 1)
                    sp.dma_start(tile_rows(scr["y"], t), x1[:, p]).then_inc(x1_out[p], 16)
                    wait(sp, pr_ok[p], n + 1)
                    wait(sp, lo_ok[p], n + 1)
                    sp.dma_start(tile_rows(scr["rows"], t), row32[:, p]).then_inc(row_out[p], 16)

                steps(sp, front, back)
                wait(sp, pt_ok[0], NT // 2)
                wait(sp, pt_ok[1], NT // 2)
                sp.dma_start(scr["pT"], pT[:]).then_inc(pT_out, 16)
                for s in range(2):
                    wait(sp, x1_out[s], 16 * NT // 2)
                    wait(sp, row_out[s], 16 * NT // 2)
                wait(sp, pT_out, 16)

            @block.gpsimd
            def _(pool):
                wait(pool, r_in, 64)

                def front(t, p, n):
                    wait(pool, x_in[p], n * 16 + 16)
                    wait(pool, t1_ok[p], n + 1)
                    wait(pool, x1_out[p], n * 16)
                    wait(pool, hn_ok[p], n)
                    nc.gpsimd.tensor_tensor(x1[:, p], xt[:, p], t1[:, p], ALU.add).then_inc(x1_ok[p], 1)
                    wait(pool, hn_ok[p], n + 1)
                    nc.gpsimd.tensor_tensor(h2[:, p], h2[:, p], mrow[:, 2], ALU.add).then_inc(h2_ok[p], 1)

                steps(pool, front, lambda t, p, n: None)

            @block.scalar
            def _(act):
                for c in range(2):
                    wait(act, w_in[c], 16)
                    nc.scalar.activation(whi[:, :, c * SEG:(c + 1) * SEG], wst[:, c], ACT.Copy).then_inc(w_hi, 1)

                def front(t, p, n):
                    wait(act, x1_ok[p], n + 1)
                    nc.scalar.activation(junk[:], x1[:, p], ACT.Square, accum_out=st[:, p, 0:1]).then_inc(ss_ok[p], 1)
                    wait(act, ss_ok[p], n + 1)
                    nc.scalar.activation(st[:, p, 1:2], st[:, p, 0:1], ACT.Sqrt, bias=K["eps"][:, 0:1], scale=1.0 / D)\
                        .then_inc(sd_ok[p], 1)
                    wait(act, h2_ok[p], n + 1)
                    wait(act, row_out[p], n * 16)
                    nc.scalar.activation(row[:, p, 0:D], h2[:, p], ACT.Copy).then_inc(hi_ok[p], 1)

                def back(t, p, n):
                    wait(act, tp_ps[p], n + 1)
                    nc.scalar.activation(h2T[:], ptp[:].rearrange("p a j -> p (a j)"), ACT.Copy).then_inc(tp_ok[p], 1)
                    wait(act, mx_ok[p], n + 1)
                    nc.scalar.activation(pe_[:, p], plg, ACT.Exp, bias=nm[:, p, 0:1], accum_out=nm[:, p, 1:2])\
                        .then_inc(ex_ok[p], 1)

                steps(act, front, back)

            @block.vector
            def _(dve):
                for c in range(2):
                    wait(dve, w_hi, c + 1)
                    nc.vector.tensor_tensor(wlo[:, :, c * SEG:(c + 1) * SEG], wst[:, c], whi[:, :, c * SEG:(c + 1) * SEG],
                                            ALU.subtract).then_inc(w_lo, 1)
                wait(dve, r_in, 64)

                def front(t, p, n):
                    wait(dve, out_ps[p], n + 1)
                    wait(dve, x1_ok[p], n)
                    nc.vector.tensor_tensor(t1[:, p], pout[p][:].rearrange("p a j -> p (a j)"), mrow[:, 0], ALU.mult)\
                        .then_inc(t1_ok[p], 1)
                    wait(dve, sd_ok[p], n + 1)
                    nc.vector.reciprocal(st[:, p, 2:3], st[:, p, 1:2]).then_inc(rs_ok[p], 1)
                    wait(dve, rs_ok[p], n + 1)
                    wait(dve, x1_ok[p], n + 1)
                    wait(dve, tp_ps[p], n)
                    nc.vector.scalar_tensor_tensor(h2[:, p], x1[:, p], st[:, p, 2:3], mrow[:, 1], ALU.mult, ALU.mult)\
                        .then_inc(hn_ok[p], 1)
                    wait(dve, hi_ok[p], n + 1)
                    nc.vector.tensor_tensor(row[:, p, D:2 * D], h2[:, p], row[:, p, 0:D], ALU.subtract).then_inc(lo_ok[p], 1)

                def back(t, p, n):
                    wait(dve, lg_ps[p], n + 1)
                    nc.vector.tensor_reduce(nm[:, p, 0:1], plg, AX.X, ALU.max, negate=True).then_inc(mx_ok[p], 1)
                    wait(dve, ex_ok[p], n + 1)
                    nc.vector.reciprocal(nm[:, p, 2:3], nm[:, p, 1:2]).then_inc(ri_ok[p], 1)
                    wait(dve, ri_ok[p], n + 1)
                    nc.vector.tensor_scalar(prob[:, p, :], pe_[:, p], nm[:, p, 2:3], None, ALU.mult)\
                        .then_inc(pr_ok[p], 1)
                    wait(dve, pt_ps[p], n + 1)
                    nc.vector.tensor_copy(pT[:, bass.ds(t * P, P)], ppt).then_inc(pt_ok[p], 1)

                steps(dve, front, back)

            @block.tensor
            def _(pe):
                wait(pe, w_lo, 2)
                wait(pe, r_in, 64)

                def front(t, p, n):
                    wait(pe, m_in[p], n * 16 + 16)
                    wait(pe, t1_ok[p], n)
                    for c in range(2):
                        last = triple(nc, pout[p][:, c, :], [
                            (mx[:, p, 0, k, :], mx[:, p, 1, k, :], whi[:, k, c * SEG:(c + 1) * SEG],
                             wlo[:, k, c * SEG:(c + 1) * SEG]) for k in range(KD)])
                    last.then_inc(out_ps[p], 1)

                def back(t, p, n):
                    wait(pe, h2_ok[p], n + 1)
                    for k in range(KD):
                        last = nc.tensor.transpose(ptp[:, k // 4, (k % 4) * P:(k % 4 + 1) * P], h2[:, p, k * P:(k + 1) * P],
                                                   K["ident"][:])
                    last.then_inc(tp_ps[p], 1)
                    wait(pe, tp_ok[p], n + 1)
                    for k in range(KD):
                        last = nc.tensor.matmul(plg, h2T[:, k * P:(k + 1) * P], rw[:, k, :], start=(k == 0),
                                                stop=(k == KD - 1))
                    last.then_inc(lg_ps[p], 1)
                    wait(pe, pr_ok[p], n + 1)
                    nc.tensor.transpose(ppt, prob[:, p, :], K["ident"][:]).then_inc(pt_ps[p], 1)

                steps(pe, front, back)


def topk_stage(nc, K, I, scr):
    NCK = P // NE
    W = T // NCK
    BITS = 30
    with nc.cleanup_on_exit(), ExitStack() as ctx:
        m = Mem(nc, ctx)
        pr = m.sb("pr", [P, W])
        tmp = m.sb("tmp", [P, W])
        gt = m.sb("gt", [P, W])
        eq = m.sb("eq", [P, W])
        cg = m.sb("cg", [P, W])
        ce = m.sb("ce", [P, W])
        slot = m.sb("slot", [P, W])
        onesw = m.sb("onesw", [P, W])
        same = m.sb("same", [P, P])
        before = m.sb("before", [P, P])
        thr = m.sb("thr", [P, 1])
        cand = m.sb("cand", [P, 2, 1])
        cnt = m.sb("cnt", [P, 2])
        acc = m.sb("accp", [P, 1])
        base = m.sb("base", [P, 4])
        sT = m.sb("sT", [P, NE, NCK, 2])
        hi = m.sb("thi", [P, NE, NCK, 2])
        pcol = m.sb("pcol", [P, 1])
        tcol = m.sb("tcol", [P, NCK, 2])
        R = K["R"]
        pc = m.ps("pc", [P, SEG])
        pc2 = m.ps("pc2", [P, SEG])
        ptr = m.ps("ptr", [P, 4, P])

        p_in, cst, c_ok, cnt_ok, tot, a_ok, t_ok = (m.sem("tp_in"), m.sem("tcst"), m.sem("tc_ok"), m.sem("tcnt"),
                                                    m.sem("ttot"), m.sem("ta_ok"), m.sem("tt_ok"))
        fin, ofs, slo, trp, ve = m.sem("tfin"), m.sem("tofs"), m.sem("tslo"), m.sem("ttrp"), m.sem("tve")
        with nc.Block() as block:
            @block.sync
            def _(sp):
                sp.dma_start(pr[:], scr["pT"].rearrange("e (c w) -> (e c) w", w=W)).then_inc(p_in, 16)

            @block.gpsimd
            def _(pool):
                nc.gpsimd.memset(same[:], 1.0).then_inc(cst, 1)
                nc.gpsimd.memset(onesw[:], 1.0).then_inc(cst, 1)
                nc.gpsimd.iota(pcol[:], [[0, 1]], base=0, channel_multiplier=1,
                               allow_small_or_imprecise_dtypes=True).then_inc(cst, 1)
                nc.gpsimd.iota(tcol[:], [[2, NCK], [1, 2]], base=0, channel_multiplier=0,
                               allow_small_or_imprecise_dtypes=True).then_inc(cst, 1)
                pool.wait_ge(cst, 4)
                sv = same[:].rearrange("p (e c) -> p e c", c=NCK)
                nc.gpsimd.affine_select(out=sv, in_=sv, compare_op=ALU.is_ge, fill=0.0, base=0,
                                        pattern=[[-NCK, NE], [0, NCK]], channel_multiplier=1).then_inc(cst, 1)
                pool.wait_ge(cst, 5)
                nc.gpsimd.affine_select(out=sv, in_=sv, compare_op=ALU.is_ge, fill=0.0, base=NCK - 1,
                                        pattern=[[NCK, NE], [0, NCK]], channel_multiplier=-1).then_inc(cst, 1)
                pool.wait_ge(cst, 6)
                nc.gpsimd.affine_select(out=before[:], in_=same[:], compare_op=ALU.is_ge, fill=0.0, base=-1,
                                        pattern=[[1, P]], channel_multiplier=-1).then_inc(cst, 1)

            @block.vector
            def _(dve):
                nc.vector.memset(thr[:], 0.0).then_inc(t_ok, 1)
                dve.wait_ge(p_in, 16)
                dve.wait_ge(cst, 7)
                for b in range(BITS):
                    dve.wait_ge(t_ok, b + 1)
                    nc.vector.tensor_scalar(cand[:, b % 2].bitcast(U32), thr[:].bitcast(U32), 1 << (BITS - 1 - b), None,
                                            ALU.bitwise_or).then_inc(c_ok, 1)
                    dve.wait_ge(c_ok, b + 1)
                    nc.vector.tensor_scalar(tmp[:], pr[:], cand[:, b % 2], None, ALU.is_ge, ALU.add,
                                            accum_out=cnt[:, b % 2:b % 2 + 1]).then_inc(cnt_ok, 1)
                    dve.wait_ge(tot, b + 1)
                    nc.vector.scalar_tensor_tensor(acc[:], pc[:, b % 2:b % 2 + 1], float(CAP), cand[:, b % 2], ALU.is_ge,
                                                   ALU.mult).then_inc(a_ok, 1)
                    dve.wait_ge(a_ok, b + 1)
                    nc.vector.tensor_tensor(thr[:], thr[:], acc[:], ALU.max).then_inc(t_ok, 1)
                dve.wait_ge(t_ok, BITS + 1)
                dve.wait_ge(cnt_ok, BITS)
                nc.vector.tensor_scalar(gt[:], pr[:], thr[:, 0:1], None, ALU.is_gt, ALU.add, accum_out=cnt[:, 0:1])\
                    .then_inc(fin, 1)
                nc.vector.tensor_scalar(eq[:], pr[:], thr[:, 0:1], None, ALU.is_equal, ALU.add, accum_out=cnt[:, 1:2])\
                    .then_inc(fin, 1)
                dve.wait_ge(fin, 2)
                nc.vector.tensor_tensor_scan(cg[:], onesw[:], gt[:], 0.0, ALU.mult, ALU.add).then_inc(ve, 1)
                nc.vector.tensor_tensor_scan(ce[:], onesw[:], eq[:], 0.0, ALU.mult, ALU.add).then_inc(ve, 1)
                dve.wait_ge(ofs, 1)
                nc.vector.tensor_copy(base[:, 0:3], pc2[:, 0:3]).then_inc(ve, 1)
                dve.wait_ge(ve, 3)
                nc.vector.tensor_scalar(cg[:], cg[:], base[:, 0:1], None, ALU.add).then_inc(ve, 1)
                nc.vector.tensor_scalar(ce[:], ce[:], base[:, 1:2], base[:, 2:3], ALU.add, ALU.add).then_inc(ve, 1)
                dve.wait_ge(ve, 5)
                nc.vector.tensor_tensor(cg[:], cg[:], gt[:], ALU.mult).then_inc(ve, 1)
                nc.vector.scalar_tensor_tensor(eq[:], ce[:], float(CAP), eq[:], ALU.is_le, ALU.mult).then_inc(ve, 1)
                dve.wait_ge(ve, 7)
                nc.vector.tensor_tensor(ce[:], ce[:], eq[:], ALU.mult).then_inc(ve, 1)
                nc.vector.tensor_tensor(gt[:], gt[:], eq[:], ALU.add).then_inc(ve, 1)
                dve.wait_ge(ve, 9)
                nc.vector.tensor_scalar(gt[:], gt[:], -(NOT_A_SLOT + 1.0), NOT_A_SLOT, ALU.mult, ALU.add).then_inc(ve, 1)
                nc.vector.tensor_tensor(cg[:], cg[:], ce[:], ALU.add).then_inc(ve, 1)
                dve.wait_ge(ve, 11)
                nc.vector.tensor_tensor(slot[:], cg[:], gt[:], ALU.add).then_inc(slo, 1)
                dve.wait_ge(trp, 1)
                for half in range(2):
                    nc.vector.tensor_copy(sT[:, :, :, half], ptr[:, half, :].rearrange("p (e c) -> p e c", c=NCK))\
                        .then_inc(ve, 1)
                dve.wait_ge(ve, 13)
                nc.vector.tensor_scalar(hi[:], sT[:], float(P), None, ALU.is_ge).then_inc(ve, 1)
                dve.wait_ge(ve, 14)
                nc.vector.scalar_tensor_tensor(K["place"][:], hi[:].rearrange("p e c h -> p e (c h)"), -float(P),
                                               sT[:].rearrange("p e c h -> p e (c h)"), ALU.mult, ALU.add).then_inc(ve, 1)
                hv = hi[:].rearrange("p e c h -> p e (c h)")
                tv = tcol[:].rearrange("p c h -> p (c h)").unsqueeze(1).broadcast_to([P, NE, NT])
                nc.vector.tensor_scalar(R[:, :, :, 2], hv, pcol[:, 0:1], None, ALU.mult).then_inc(ve, 1)
                nc.vector.tensor_tensor(R[:, :, :, 3], hv, tv, ALU.mult).then_inc(ve, 1)
                dve.wait_ge(ve, 17)
                nc.vector.tensor_scalar(R[:, :, :, 0], R[:, :, :, 2], -1.0, pcol[:, 0:1], ALU.mult, ALU.add).then_inc(ve, 1)
                nc.vector.scalar_tensor_tensor(R[:, :, :, 1], R[:, :, :, 3], -1.0, tv, ALU.mult, ALU.add).then_inc(ve, 1)

            @block.tensor
            def _(pe):
                pe.wait_ge(cst, 7)
                for b in range(BITS):
                    pe.wait_ge(cnt_ok, b + 1)
                    nc.tensor.matmul(pc[:, b % 2:b % 2 + 1], same[:], cnt[:, b % 2:b % 2 + 1], start=True,
                                     stop=True).then_inc(tot, 1)
                pe.wait_ge(fin, 2)
                nc.tensor.matmul(pc2[:, 0:2], before[:], cnt[:], start=True, stop=True)
                nc.tensor.matmul(pc2[:, 2:3], same[:], cnt[:, 0:1], start=True, stop=True).then_inc(ofs, 1)
                pe.wait_ge(slo, 1)
                for half in range(2):
                    last = nc.tensor.transpose(ptr[:, half, :], slot[:, half * P:(half + 1) * P], K["ident"][:])
                last.then_inc(trp, 1)


def moe_stage(nc, K, I, scr):
    FH = SEG
    NB = 6
    NS = 3
    with nc.cleanup_on_exit(), ExitStack() as ctx:
        m = Mem(nc, ctx)
        wst = m.sb("mwst", [P, NS, KD, FH])
        whi = m.sb("mwhi", [P, NB, KD, FH], BF16)
        wlo = m.sb("mwlo", [P, NB, KD, FH], BF16)
        rows32 = m.sb("mrows", [P, 2, ROWW], I32)
        rows = rows32[:].bitcast(BF16)
        probs = rows32[:].bitcast(F32)
        xhi = m.sb("xhi", [P, KD, CAP], BF16)
        xlo = m.sb("xlo", [P, KD, CAP], BF16)
        thb = m.sb("thb", [P, 2, CAP])
        hb = m.sb("hb", [P, 2, CAP])
        fhi = m.sb("fhi", [P, KD, CAP], BF16)
        flo = m.sb("flo", [P, KD, CAP], BF16)
        ysb = m.sb("ysb", [P, 2, D])
        g2 = m.sb("g2", [P, D])
        oneh = m.sb("oneh", [P, NT, P], BF16)
        Re = m.sb("Re", [P, NT, 4], BF16)
        iot = m.sb("iot", [P, P])
        idf = m.sb("idf", [P, 4])
        idn = m.sb("idn", [P, 2], I32)
        idc = m.sb("idc", [P, 2], I32)
        gate = m.sb("gate", [P, 2])
        pflag = m.sb("mpflag", [1, 1])
        pgu = [m.ps(f"pgu{i}", [P, 2, CAP]) for i in range(2)]
        pd = [m.ps(f"pd{i}", [P, SEG]) for i in range(2)]
        pid = m.ps("pid", [P, SEG])[:, 0:4]
        ptx = [m.ps(f"ptx{i}", [P, 4, CAP], BF16) for i in range(2)]

        g2_in, iot_ok, fl_ok = m.sem("g2_in"), m.sem("iot_ok"), m.sem("fl_ok")
        w_in, w_hi, w_lo = m.sems("mw_in", NS), m.sem("mw_hi"), m.sems("mw_lo", NS)
        oh_ok, id_ps, idf_ok, id_ok, idc_ok, gt_ok = (m.sem("oh_ok"), m.sem("id_ps"), m.sem("idf_ok"), m.sem("id_ok"),
                                                      m.sem("idc_ok"), m.sem("gt_ok"))
        got, tx_ps, tx_ok = m.sem("got"), m.sem("tx_ps"), m.sem("tx_ok")
        gu_ps, mth_ok, sg_ok, hid_ok, fhi_ok, flo_ok = (m.sem("gu_ps"), m.sem("mth_ok"), m.sem("msg_ok"), m.sem("hid_ok"),
                                                        m.sem("fhi_ok"), m.sem("flo_ok"))
        d_ps, y_ok, put = m.sem("d_ps"), m.sem("my_ok"), m.sem("put")
        mats = [I["w_gate"], I["w_up"], I["w_gate"], I["w_up"], I["w_down"], I["w_down"]]
        half_of = [0, 0, 1, 1, 0, 1]

        def experts(engine, prep, body):
            prep(0)
            peeled(engine, NE - 1, lambda e: body(e, True))
            body(NE - 1, False)

        with nc.Block() as block:
            @block.sync
            def _(sp):
                def one(e):
                    for b in range(NB):
                        wait(sp, w_lo[b % NS], e * 2 + b // NS)
                        src = mats[b][0, bass.ds(e, 1), :, :].rearrange("e (k p) n -> p (e k) n", p=P)
                        sp.dma_start(wst[:, b % NS], src[:, :, half_of[b] * FH:(half_of[b] + 1) * FH])\
                            .then_inc(w_in[b % NS], 16)
                peeled(sp, NE, one)

            @block.gpsimd
            def _(pool):
                pool.dma_start(g2[:], scr["modrows"][6:8, :].rearrange("a n -> (a n)").partition_broadcast(P))\
                    .then_inc(g2_in, 16)
                nc.gpsimd.memset(pflag[:], 0.0).then_inc(fl_ok, 1)
                wait(pool, fl_ok, 1)
                nc.gpsimd.iota(iot[:], [[1, P]], base=0, channel_multiplier=0,
                               allow_small_or_imprecise_dtypes=True).then_inc(iot_ok, 1)

                def carrier():
                    nc.gpsimd.tensor_tensor(pflag[:], pflag[:], pflag[:], ALU.mult).then_inc(fl_ok, 1)

                def prep(e, first=False):
                    wait(pool, fl_ok, 1 if first else e * 3 - 1)
                    wait(pool, id_ok, e + 1)
                    wait(pool, tx_ps, e * 4)
                    wait(pool, gt_ok, e)
                    carrier()
                    for s in range(2):
                        pool.indirect_dma_start(out=rows32[:, s, :], out_offset=None, in_=scr["rows"],
                                                in_offset=bass.IndirectOffsetOnAxis(ap=idn[:, s:s + 1], axis=0))\
                            .then_inc(got, 16)

                def body(e, nxt):
                    if nxt:
                        prep(e + 1)
                    wait(pool, put, e * 32)
                    for s in range(2):
                        wait(pool, y_ok, e * 4 + 2 * s + 2)
                        wait(pool, fl_ok, e * 3 + s + (3 if nxt else 2))
                        carrier()
                        pool.indirect_dma_start(out=scr["y"], out_offset=bass.IndirectOffsetOnAxis(ap=idc[:, s:s + 1], axis=0),
                                                in_=ysb[:, s, :], in_offset=None, compute_op=ALU.add).then_inc(put, 16)

                experts(pool, lambda e: prep(e, True), body)
                wait(pool, put, NE * 32)

            @block.scalar
            def _(act):
                def turn(e):
                    for j in range(2):
                        wait(act, tx_ps, e * 4 + 2 * j + 1)
                        wait(act, gu_ps, e * 8)
                        nc.scalar.activation(xhi[:, 4 * j:4 * j + 4, :], ptx[0][:], ACT.Copy).then_inc(tx_ok, 1)

                def split(e, b):
                    wait(act, w_in[b % NS], e * 32 + 16 * (b // NS) + 16)
                    if b < 2:
                        if not (isinstance(e, int) and e == 0):
                            wait(act, gu_ps, e * 8 - 4)
                    elif b < 4:
                        wait(act, gu_ps, e * 8)
                    else:
                        wait(act, d_ps, e * 4)
                    nc.scalar.activation(whi[:, b], wst[:, b % NS], ACT.Copy).then_inc(w_hi, 1)

                def hidden(e, j):
                    wait(act, gu_ps, e * 8 + j + 1)
                    if j < 2:
                        wait(act, sg_ok, e * 8)
                    else:
                        wait(act, sg_ok, e * 8 + j - 1)
                    nc.scalar.activation(thb[:, j % 2], pgu[j % 2][:, 0, :], ACT.Tanh, scale=0.5).then_inc(mth_ok, 1)
                    wait(act, hid_ok, e * 8 + j + 1)
                    wait(act, d_ps, e * 4)
                    nc.scalar.activation(fhi[:, j, :], hb[:, j % 2], ACT.Copy).then_inc(fhi_ok, 1)

                def body(e, nxt):
                    for j in range(8):
                        if j in (0, 4):
                            split(e, 2 + j // 2)
                        hidden(e, j)
                        if j == 2:
                            split(e, 3)
                        if j == 6:
                            split(e, 5)
                    if nxt:
                        split(e + 1, 0)
                        turn(e + 1)
                        split(e + 1, 1)

                def prep0(e):
                    split(0, 0)
                    split(0, 1)
                    turn(0)

                experts(act, prep0, body)

            @block.vector
            def _(dve):
                wait(dve, iot_ok, 1)
                wait(dve, g2_in, 16)

                def token_list(e):
                    wait(dve, id_ps, e)
                    nc.vector.tensor_tensor(oneh[:], iot[:].unsqueeze(1).broadcast_to([P, NT, P]),
                                            K["place"][:, bass.ds(e, 1), :].rearrange("p e t -> p (e t)").unsqueeze(2)
                                            .broadcast_to([P, NT, P]), ALU.is_equal).then_inc(oh_ok, 1)
                    nc.vector.tensor_copy(Re[:], K["R"][:, bass.ds(e, 1), :, :].rearrange("p e t j -> p (e t) j"))\
                        .then_inc(oh_ok, 1)

                def numbers(e):
                    wait(dve, id_ps, e + 1)
                    nc.vector.tensor_copy(idf[:], pid).then_inc(idf_ok, 1)
                    wait(dve, idf_ok, e + 1)
                    wait(dve, got, e * 32)
                    wait(dve, idc_ok, e)
                    f2 = idf[:].rearrange("p (s a) -> p s a", a=2)
                    nc.vector.scalar_tensor_tensor(idn[:], f2[:, :, 1], float(P), f2[:, :, 0], ALU.mult, ALU.add)\
                        .then_inc(id_ok, 1)

                def turn(e):
                    for j in range(2):
                        wait(dve, tx_ps, e * 4 + 2 * j + 2)
                        wait(dve, gu_ps, e * 8)
                        nc.vector.tensor_copy(xlo[:, 4 * j:4 * j + 4, :], ptx[1][:]).then_inc(tx_ok, 1)

                def split(e, b):
                    wait(dve, w_hi, e * NB + b + 1)
                    nc.vector.tensor_tensor(wlo[:, b], wst[:, b % NS], whi[:, b], ALU.subtract).then_inc(w_lo[b % NS], 1)

                def hidden(e, j):
                    p = j % 2
                    wait(dve, mth_ok, e * 8 + j + 1)
                    if j < 2:
                        wait(dve, flo_ok, e * 8)
                    else:
                        wait(dve, flo_ok, e * 8 + j - 1)
                    nc.vector.scalar_tensor_tensor(thb[:, p], thb[:, p], 1.0, pgu[p][:, 0, :], ALU.add, ALU.mult)\
                        .then_inc(sg_ok, 1)
                    wait(dve, sg_ok, e * 8 + j + 1)
                    nc.vector.tensor_tensor(hb[:, p], thb[:, p], pgu[p][:, 1, :], ALU.mult).then_inc(hid_ok, 1)
                    wait(dve, hid_ok, e * 8 + j + 1)
                    wait(dve, fhi_ok, e * 8 + j + 1)
                    nc.vector.tensor_tensor(flo[:, j, :], hb[:, p], fhi[:, j, :], ALU.subtract).then_inc(flo_ok, 1)

                def weigh(e, s, c):
                    q = 2 * s + c
                    wait(dve, d_ps, e * 4 + q + 1)
                    wait(dve, put, e * 32)
                    nc.vector.scalar_tensor_tensor(ysb[:, s, c * SEG:(c + 1) * SEG], pd[q % 2][:], gate[:, s:s + 1],
                                                   g2[:, c * SEG:(c + 1) * SEG], ALU.mult, ALU.mult).then_inc(y_ok, 1)

                def body(e, nxt):
                    wait(dve, got, e * 32 + 32)
                    wait(dve, y_ok, e * 4)
                    nc.vector.tensor_scalar(gate[:], probs[:, :, bass.ds(e + D, 1)]
                                            .rearrange("p s a -> p (s a)"), 0.5, None, ALU.mult).then_inc(gt_ok, 1)
                    if nxt:
                        token_list(e + 1)
                    for j in range(8):
                        if j in (0, 4):
                            split(e, 2 + j // 2)
                        hidden(e, j)
                        if j == 2:
                            split(e, 3)
                        if j == 3:
                            wait(dve, put, e * 32)
                            nc.vector.tensor_copy(idc[:], idn[:]).then_inc(idc_ok, 1)
                            if nxt:
                                numbers(e + 1)
                        if j == 6:
                            split(e, 5)
                    wait(dve, gt_ok, e + 1)
                    if nxt:
                        split(e + 1, 0)
                        turn(e + 1)
                    weigh(e, 0, 0)
                    weigh(e, 0, 1)
                    if nxt:
                        split(e + 1, 1)
                    weigh(e, 1, 0)
                    weigh(e, 1, 1)

                def prep0(e):
                    token_list(0)
                    numbers(0)
                    split(0, 0)
                    split(0, 1)
                    turn(0)

                experts(dve, prep0, body)

            @block.tensor
            def _(pe):
                def token_list(e):
                    wait(pe, oh_ok, e * 2 + 2)
                    wait(pe, idf_ok, e)
                    for t in range(NT):
                        last = nc.tensor.matmul(pid, oneh[:, t, :], Re[:, t, :], start=(t == 0), stop=(t == NT - 1))
                    last.then_inc(id_ps, 1)

                def turn(e):
                    wait(pe, got, e * 32 + 32)
                    for j in range(2):
                        for part in range(2):
                            if j == 0:
                                wait(pe, tx_ok, e * 4)
                            else:
                                wait(pe, tx_ok, e * 4 + 2)
                            for k in range(4):
                                for s in range(2):
                                    c = part * D + (4 * j + k) * P
                                    last = nc.tensor.transpose(ptx[part][:, k, s * P:(s + 1) * P], rows[:, s, c:c + P],
                                                               K["identb"][:])
                            last.then_inc(tx_ps, 1)

                def body(e, nxt):
                    wait(pe, tx_ok, e * 4 + 4)
                    for f in range(8):
                        h, jj = f // 4, f % 4
                        if jj == 0:
                            for b in (2 * h, 2 * h + 1):
                                wait(pe, w_lo[b % NS], e * 2 + b // NS + 1)
                        if f < 2:
                            wait(pe, hid_ok, e * 8)
                        else:
                            wait(pe, hid_ok, e * 8 + f - 1)
                        for part in range(2):
                            b = 2 * h + part
                            last = triple(nc, pgu[f % 2][:, part, :], [
                                (whi[:, b, k, jj * P:(jj + 1) * P], wlo[:, b, k, jj * P:(jj + 1) * P], xhi[:, k, :],
                                 xlo[:, k, :]) for k in range(KD)])
                        last.then_inc(gu_ps, 1)
                        if nxt and f == 1:
                            token_list(e + 1)
                    if nxt:
                        turn(e + 1)
                    wait(pe, flo_ok, e * 8 + 8)
                    wait(pe, fhi_ok, e * 8 + 8)
                    for b in (4, 5):
                        wait(pe, w_lo[b % NS], e * 2 + b // NS + 1)
                    for s in range(2):
                        for c in range(2):
                            q = 2 * s + c
                            wait(pe, y_ok, e * 4 + max(0, q - 1))
                            last = triple(nc, pd[q % 2][:], [
                                (fhi[:, k, s * P:(s + 1) * P], flo[:, k, s * P:(s + 1) * P], whi[:, 4 + c, k, :],
                                 wlo[:, 4 + c, k, :]) for k in range(KD)])
                            last.then_inc(d_ps, 1)

                def prep0(e):
                    token_list(0)
                    turn(0)

                experts(pe, prep0, body)


def finish_stage(nc, K, I, scr, out):
    with nc.cleanup_on_exit(), ExitStack() as ctx:
        m = Mem(nc, ctx)
        NBUF = 4
        yt = m.sb("yt", [P, NBUF, D])
        junk = m.sb("fjunk", [P, D])
        fg = m.sb("fg", [P, D])
        st = m.sb("fst", [P, NBUF, 4])
        fg_in, y_in, y_out = m.sem("fg_in"), m.sems("fy_in", NBUF), m.sems("fy_out", NBUF)
        ss, sd, rs, ok = m.sem("fss"), m.sem("fsd"), m.sem("frs"), m.sem("fok")
        with nc.Block() as block:
            @block.sync
            def _(sp):
                sp.dma_start(fg[:], I["final_g"].partition_broadcast(P)).then_inc(fg_in, 16)
                def one(i):
                    for b in range(NBUF):
                        wait(sp, y_out[b], i * 16)
                        sp.dma_start(yt[:, b], scr["y"][bass.ds((i * NBUF + b) * P, P), :]).then_inc(y_in[b], 16)
                peeled(sp, NT // NBUF, one)

            @block.gpsimd
            def _(pool):
                def one(i):
                    for b in range(NBUF):
                        wait(pool, ok, i * NBUF + b + 1)
                        pool.dma_start(out[0, bass.ds((i * NBUF + b) * P, P), :], yt[:, b]).then_inc(y_out[b], 16)
                peeled(pool, NT // NBUF, one)
                for b in range(NBUF):
                    wait(pool, y_out[b], 16 * NT // NBUF)

            @block.scalar
            def _(act):
                def one(i):
                    for b in range(NBUF):
                        wait(act, y_in[b], i * 16 + 16)
                        nc.scalar.activation(junk[:], yt[:, b], ACT.Square, accum_out=st[:, b, 0:1]).then_inc(ss, 1)
                        wait(act, ss, i * NBUF + b + 1)
                        nc.scalar.activation(st[:, b, 1:2], st[:, b, 0:1], ACT.Sqrt, bias=K["eps"][:, 0:1], scale=1.0 / D)\
                            .then_inc(sd, 1)
                peeled(act, NT // NBUF, one)

            @block.vector
            def _(dve):
                wait(dve, fg_in, 16)
                def one(i):
                    for b in range(NBUF):
                        wait(dve, sd, i * NBUF + b + 1)
                        nc.vector.reciprocal(st[:, b, 2:3], st[:, b, 1:2]).then_inc(rs, 1)
                        wait(dve, rs, i * NBUF + b + 1)
                        nc.vector.scalar_tensor_tensor(yt[:, b], yt[:, b], st[:, b, 2:3], fg[:], ALU.mult, ALU.mult)\
                            .then_inc(ok, 1)
                peeled(dve, NT // NBUF, one)


def build(nc, I, out, debug=False):
    kind = "ExternalOutput" if debug else "Internal"
    scr = {
        "modrows": nc.dram_tensor("s_modrows", [8, SEG], F32, kind=kind).ap(),
        "mixed": nc.dram_tensor("s_mixed", [NT, P, 2, KD, P], BF16, kind=kind).ap(),
        "rows": nc.dram_tensor("s_rows", [T, ROWW], I32, kind=kind).ap(),
        "pT": nc.dram_tensor("s_pT", [NE, T], F32, kind=kind).ap(),
        "y": nc.dram_tensor("s_y", [T, D], F32, kind=kind).ap(),
    }
    with ExitStack() as whole:
        m = Mem(nc, whole)
        K = {"ident": m.sb("ident", [P, P]), "identb": m.sb("identb", [P, P], BF16), "ones": m.sb("ones", [P, P]),
             "mean_cw": m.sb("mean_cw", [P, P]), "mean_p": m.sb("mean_p", [P, P]), "eps": m.sb("eps", [P, 1]),
             "const_ok": m.sem("const_ok"), "n_const": 8}
        with nc.Block() as block:
            @block.gpsimd
            def _(pool):
                for t, val in (("ident", 0.0), ("identb", 0.0), ("ones", 1.0), ("mean_cw", 1.0 / CW),
                               ("mean_p", 1.0 / P), ("eps", EPS)):
                    nc.gpsimd.memset(K[t][:], val).then_inc(K["const_ok"], 1)
                wait(pool, K["const_ok"], 6)
                for t in ("ident", "identb"):
                    nc.gpsimd.affine_select(out=K[t][:], in_=K[t][:], compare_op=ALU.not_equal, fill=1.0, base=0,
                                            pattern=[[-1, P]], channel_multiplier=1).then_inc(K["const_ok"], 1)
        with ExitStack() as mixer:
            mm = Mem(nc, mixer)
            K["hhi"] = mm.sb("hhi", [P, KD, TC + T], BF16)
            K["hlo"] = mm.sb("hlo", [P, KD, TC + T], BF16)
            modulate_stage(nc, K, I, scr)
            conv_stage(nc, K, I, scr)
            heads_stage(nc, K, I, scr)
        outproj_stage(nc, K, I, scr)
        K["place"] = m.sb("place", [P, NE, NT])
        K["R"] = m.sb("R", [P, NE, NT, 4], BF16)
        topk_stage(nc, K, I, scr)
        moe_stage(nc, K, I, scr)
        finish_stage(nc, K, I, scr, out)


_INS = ["x", "c", "ctx", "c_ctx", "ada_w", "ada_b", "norm1_g", "w_in", "conv_taps", "conv_bias", "conv_ln_g",
        "conv_ln_b", "hgrn_lb_logits", "hgrn_norm_g", "w_out", "norm2_g", "router_w", "w_gate", "w_up", "w_down",
        "final_g"]
DEBUG = False


def kernel(**inputs):
    import numpy as np
    import concourse.bacc as bacc
    from concourse.bass_utils import run_bass_kernel_spmd as run

    nc = bacc.Bacc("TRN2", target_bir_lowering=False, num_devices=1)
    arrays, aps = {}, {}
    for name in _INS:
        a = np.ascontiguousarray(inputs[name])
        arrays[f"in_{name}"] = a
        aps[name] = nc.dram_tensor(f"in_{name}", a.shape, mybir.dt.from_np(a.dtype), kind="ExternalInput").ap()
    o = nc.dram_tensor("out_0", (1, T, D), F32, kind="ExternalOutput").ap()
    build(nc, aps, o, debug=DEBUG)
    r = run(nc, [arrays], core_ids=[0])
    return r.results[0]["out_0"]
```

```python
from contextlib import ExitStack

import concourse.bass as bass
from concourse import mybir

F32 = mybir.dt.float32
BF16 = mybir.dt.bfloat16
I32 = mybir.dt.int32
U32 = mybir.dt.uint32
ACT = mybir.ActivationFunctionType
ALU = mybir.AluOpType
AX = mybir.AxisListType

P = 128
D = 1024
KD = D // P
T = 2048
TC = 256
NT = T // P
SEG = 512
NSEG = T // SEG
CW = 512
NCT = CW // P
HEADS = 4
TAPS = 31
PAD = (TAPS - 1) // 2
GW = 64
GH = T // GW
CH = 32
NE = 16
CAP = 2 * T // NE
EPS = 1e-6
COL_A, COL_B, COL_Q, COL_I, COL_FF, COL_FB, COL_G = [512 * j for j in range(7)]
ROWW = D + NE
NOT_A_SLOT = 1000.0


class Mem:

    def __init__(self, nc, ctx):
        self.nc, self.ctx = nc, ctx

    def sb(self, name, shape, dt=F32):
        return self.ctx.enter_context(self.nc.sbuf_tensor(name, shape, dt))

    def ps(self, name, shape, dt=F32):
        return self.ctx.enter_context(self.nc.psum_tensor(name, shape, dt))

    def sem(self, name):
        return self.nc.alloc_semaphore(name)

    def sems(self, name, n):
        return [self.sem(f"{name}{i}") for i in range(n)]


def wait(engine, sem, value):
    if not (isinstance(value, int) and value == 0):
        engine.wait_ge(sem, value)


def peeled(engine, n, one):
    one(0)
    with engine.Fori(1, n) as i:
        one(i)


def triple(nc, out, pairs):
    n = len(pairs)
    for k, (lh, ll, rh, rl) in enumerate(pairs):
        nc.tensor.matmul(out, lh, rh, start=(k == 0), stop=False)
        nc.tensor.matmul(out, lh, rl, start=False, stop=False)
        last = nc.tensor.matmul(out, ll, rh, start=False, stop=(k == n - 1))
    return last


def modulate_stage(nc, K, I, scr):
    NCH = 12
    groups = [(0, 2)] + [(2 + 4 * s, 4) for s in range(NSEG)]
    with nc.cleanup_on_exit(), ExitStack() as ctx:
        m = Mem(nc, ctx)
        cc = m.sb("cc", [P, 2, KD])
        cth = m.sb("cth", [P, 2, KD])
        csil = m.sb("csil", [P, 2, KD])
        crep = m.sb("crep", [P, KD, P])
        cmix = m.sb("cmix", [P, KD, P])
        ada = m.sb("ada", [P, 2, KD, SEG])
        adab = m.sb("adab", [1, 2, SEG])
        modrow = m.sb("modrow", [P, 2 * D])
        modc = m.sb("modc", [P, 2 * KD, 2])
        n1c = m.sb("n1c", [P, KD])
        A1 = m.sb("A1", [P, KD, 2])
        n2r = m.sb("n2r", [P, D])
        rows = m.sb("rows", [P, 2, SEG])
        xb = m.sb("xb", [P, 2, 4, D])
        junk = m.sb("junk", [P, D])
        ss = m.sb("ss", [P, 5, 4])
        rstd = m.sb("rstd", [P, 5, 4])
        hf = m.sb("hf", [P, 2, SEG])
        pm = [m.ps(f"pm{i}", [P, SEG]) for i in range(2)]
        pt = [m.ps(f"pt{i}", [P, SEG]) for i in range(4)]

        c_in, col_in, n2_in = m.sem("c_in"), m.sem("col_in"), m.sem("n2_in")
        ada_in, x_in = m.sems("ada_in", 2), m.sems("x_in", 2)
        c_th, c_sil, c_rep = m.sem("c_th"), m.sem("c_sil"), m.sem("c_rep")
        mod_ps, mod_sb, modc_ps, modc_sb = m.sem("mod_ps"), m.sem("mod_sb"), m.sem("modc_ps"), m.sem("modc_sb")
        row_out = m.sems("row_out", 2)
        a1_ok, ss_ok, std_ok, rstd_ok, xn_ok = m.sem("a1_ok"), m.sem("ss_ok"), m.sem("std_ok"), m.sem("rstd_ok"), m.sem("xn_ok")
        tp_ps, hi_ok, hf_ok, lo_ok = m.sem("tp_ps"), m.sem("hi_ok"), m.sem("hf_ok"), m.sem("lo_ok")

        ada_v = I["ada_w"][0].rearrange("(p k) e -> p k e", k=KD)
        def chunks_after(g):
            return [] if g == 0 else [2 + 2 * g, 3 + 2 * g]

        with nc.Block() as block:
            @block.sync
            def _(sp):
                sp.dma_start(cc[:, 0, :], I["c"].rearrange("a (p k) -> (a p) k", k=KD)).then_inc(c_in, 16)
                sp.dma_start(cc[:, 1, :], I["c_ctx"].rearrange("(p k) -> p k", k=KD)).then_inc(c_in, 16)

                def load_ada(n):
                    if n >= 2:
                        sp.wait_ge(mod_ps, n - 1)
                    sp.dma_start(ada[:, n % 2], ada_v[:, :, n * SEG:(n + 1) * SEG]).then_inc(ada_in[n % 2], 16)
                    sp.dma_start(adab[:, n % 2], I["ada_b"][:, n * SEG:(n + 1) * SEG]).then_inc(ada_in[n % 2], 16)

                def load_x(g):
                    t0, n = groups[g]
                    src = I["ctx"][0] if g == 0 else I["x"][0, (t0 - 2) * P:(t0 - 2 + n) * P, :]
                    if g >= 2:
                        sp.wait_ge(tp_ps, KD * (g - 1))
                    sp.dma_start(xb[:, g % 2, 0:n, :], src.rearrange("(n p) d -> p n d", p=P)).then_inc(x_in[g % 2], 16)

                load_ada(0)
                load_ada(1)
                load_x(0)
                load_x(1)
                load_ada(2)
                load_ada(3)
                for g in range(1, 5):
                    for n in chunks_after(g):
                        load_ada(n)
                    if g + 1 < 5:
                        load_x(g + 1)

            @block.gpsimd
            def _(pool):
                with nc.allow_non_contiguous_dma(reason="1024 single norm weights into columns"):
                    pool.dma_start(n1c[:], I["norm1_g"][0].rearrange("(k p) -> p k", p=P)).then_inc(col_in, 16)
                pool.dma_start(n2r[:], I["norm2_g"][0].partition_broadcast(P)).then_inc(n2_in, 16)
                for n in range(4, NCH):
                    pool.wait_ge(mod_sb, n + 1)
                    pool.dma_start(scr["modrows"][n - 4:n - 3, :], rows[0:1, n % 2, :]).then_inc(row_out[n % 2], 16)
                for s in range(2):
                    pool.wait_ge(row_out[s], 16 * (NCH - 4) // 2)

            @block.scalar
            def _(act):
                act.wait_ge(c_in, 32)
                nc.scalar.activation(cth[:], cc[:], ACT.Tanh, scale=0.5).then_inc(c_th, 1)
                for g, (t0, n) in enumerate(groups):
                    act.wait_ge(x_in[g % 2], 16 * (g // 2 + 1))
                    for j in range(n):
                        if t0 + j:
                            act.wait_ge(ss_ok, t0 + j)
                        nc.scalar.activation(junk[:], xb[:, g % 2, j, :], ACT.Square,
                                             accum_out=ss[:, g, j:j + 1]).then_inc(ss_ok, 1)
                    act.wait_ge(ss_ok, sum(x[1] for x in groups[:g + 1]))
                    act.wait_ge(K["const_ok"], K["n_const"])
                    nc.scalar.activation(ss[:, g, 0:n], ss[:, g, 0:n], ACT.Sqrt, bias=K["eps"][:, 0:1],
                                         scale=1.0 / D).then_inc(std_ok, 1)
                    if g == 0:
                        act.wait_ge(a1_ok, 1)
                    s = 0 if g else 1
                    for k in range(KD):
                        q = g * KD + k
                        act.wait_ge(tp_ps, q + 1)
                        nc.scalar.activation(K["hhi"][:, k, t0 * P:(t0 + n) * P], pt[q % 4][:, 0:n * P], ACT.Identity,
                                             bias=modc[:, k, s:s + 1], scale=A1[:, k, s:s + 1]).then_inc(hi_ok, 1)

            @block.vector
            def _(dve):
                dve.wait_ge(c_th, 1)
                nc.vector.scalar_tensor_tensor(csil[:], cth[:], 1.0, cc[:], ALU.add, ALU.mult).then_inc(c_sil, 1)
                dve.wait_ge(c_sil, 1)
                nc.vector.tensor_scalar(crep[:], csil[:, 0, :].unsqueeze(2).broadcast_to([P, KD, P]), 0.5, None,
                                        ALU.mult).then_inc(c_rep, 1)
                for s in range(2):
                    nc.vector.tensor_scalar(cmix[:, :, 64 * s:64 * s + 64],
                                            csil[:, s, :].unsqueeze(2).broadcast_to([P, KD, 64]), 0.5, None,
                                            ALU.mult).then_inc(c_rep, 1)

                def mod_out(n):
                    dve.wait_ge(mod_ps, n + 1)
                    src = pm[n % 2][:]
                    if n < 4:
                        ins = nc.vector.tensor_copy(modrow[:, n * SEG:(n + 1) * SEG], src)
                    else:
                        if n >= 6:
                            dve.wait_ge(row_out[n % 2], 16 * ((n - 4) // 2))
                        if n in (8, 9):
                            dve.wait_ge(n2_in, 16)
                            ins = nc.vector.scalar_tensor_tensor(rows[:, n % 2, :], src, 1.0,
                                                                 n2r[:, (n - 8) * SEG:(n - 7) * SEG], ALU.add, ALU.mult)
                        else:
                            ins = nc.vector.tensor_copy(rows[:, n % 2, :], src)
                    ins.then_inc(mod_sb, 1)

                for n in range(4):
                    mod_out(n)
                for q in range(4):
                    dve.wait_ge(modc_ps, q + 1)
                    nc.vector.tensor_copy(modc[:, 4 * q:4 * q + 4, :],
                                          pt[q][:].rearrange("p (a s j) -> p a s j", a=4, s=2)[:, :, :, 0])\
                        .then_inc(modc_sb, 1)
                dve.wait_ge(modc_sb, 4)
                dve.wait_ge(col_in, 16)
                nc.vector.scalar_tensor_tensor(A1[:], modc[:, KD:2 * KD, :], 1.0,
                                               n1c[:].unsqueeze(2).broadcast_to([P, KD, 2]), ALU.add, ALU.mult)\
                    .then_inc(a1_ok, 1)
                dve.wait_ge(a1_ok, 1)
                for g, (t0, n) in enumerate(groups):
                    dve.wait_ge(std_ok, g + 1)
                    nc.vector.reciprocal(rstd[:, g, 0:n], ss[:, g, 0:n]).then_inc(rstd_ok, 1)
                    dve.wait_ge(rstd_ok, g + 1)
                    for j in range(n):
                        nc.vector.tensor_scalar(xb[:, g % 2, j, :], xb[:, g % 2, j, :], rstd[:, g, j:j + 1], None,
                                                ALU.mult).then_inc(xn_ok, 1)
                    s = 0 if g else 1
                    for k in range(KD):
                        q = g * KD + k
                        dve.wait_ge(hi_ok, q + 1)
                        nc.vector.tensor_scalar(hf[:, q % 2, 0:n * P], pt[q % 4][:, 0:n * P], A1[:, k, s:s + 1],
                                                modc[:, k, s:s + 1], ALU.mult, ALU.add).then_inc(hf_ok, 1)
                        dve.wait_ge(hf_ok, q + 1)
                        nc.vector.tensor_tensor(K["hlo"][:, k, t0 * P:(t0 + n) * P], hf[:, q % 2, 0:n * P],
                                                K["hhi"][:, k, t0 * P:(t0 + n) * P], ALU.subtract).then_inc(lo_ok, 1)
                    for c in chunks_after(g):
                        mod_out(c)

            @block.tensor
            def _(pe):
                pe.wait_ge(K["const_ok"], K["n_const"])
                pe.wait_ge(c_rep, 3)

                def mod_mm(n):
                    pe.wait_ge(ada_in[n % 2], 32 * (n // 2 + 1))
                    if n >= 2:
                        pe.wait_ge(mod_sb, n - 1)
                    w = cmix if n < 4 else crep
                    for k in range(KD):
                        nc.tensor.matmul(pm[n % 2][:], w[:, k, :], ada[:, n % 2, k, :], start=(k == 0), stop=False)
                    nc.tensor.matmul(pm[n % 2][:], K["ones"][0:1, :], adab[0:1, n % 2, :], start=False,
                                     stop=True).then_inc(mod_ps, 1)

                for n in range(4):
                    mod_mm(n)
                pe.wait_ge(mod_sb, 4)
                for q in range(4):
                    for a in range(4):
                        j = 4 * q + a
                        last = nc.tensor.transpose(pt[q][:, a * P:(a + 1) * P], modrow[:, j * P:(j + 1) * P], K["ident"][:])
                    last.then_inc(modc_ps, 1)
                tiles = 0
                for g, (t0, n) in enumerate(groups):
                    tiles += n
                    pe.wait_ge(xn_ok, tiles)
                    for k in range(KD):
                        q = g * KD + k
                        if q >= 4:
                            pe.wait_ge(hf_ok, q - 3)
                        else:
                            pe.wait_ge(modc_sb, 4)
                        for j in range(n):
                            last = nc.tensor.transpose(pt[q % 4][:, j * P:(j + 1) * P],
                                                       xb[:, g % 2, j, k * P:(k + 1) * P], K["ident"][:])
                        last.then_inc(tp_ps, 1)
                    for c in chunks_after(g):
                        mod_mm(c)


def conv_stage(nc, K, I, scr):
    with nc.cleanup_on_exit(), ExitStack() as ctx:
        m = Mem(nc, ctx)
        wst = m.sb("wst", [P, 4, KD, P])
        whi = m.sb("whi", [P, 4, KD, P], BF16)
        wlo = m.sb("wlo", [P, 4, KD, P], BF16)
        th = m.sb("th", [P, 2, SEG])
        u = m.sb("u", [P, 2, T])
        co = m.sb("co", [P, NCT, T])
        taps = m.sb("taps", [P, NCT, TAPS])
        cb = m.sb("cb", [P, NCT])
        lg = m.sb("lg", [P, 2, NCT])
        sq = m.sb("sq", [P, 2, SEG])
        rs = m.sb("rs", [P, 2, SEG])
        y = m.sb("y", [P, 2, SEG])
        tl = m.sb("tl", [P, 2, SEG])
        mh = m.sb("mh", [P, 2, SEG], BF16)
        ml = m.sb("ml", [P, 2, SEG], BF16)
        pa = [m.ps(f"pa{i}", [P, SEG]) for i in range(2)]
        pb = [m.ps(f"pb{i}", [P, SEG]) for i in range(2)]
        pmu = [m.ps(f"pmu{i}", [P, SEG]) for i in range(2)]
        pva = [m.ps(f"pva{i}", [P, SEG]) for i in range(2)]

        par_in, par_ok = m.sem("par_in"), m.sem("par_ok")
        w_in, w_hi, w_lo = m.sems("cw_in", 4), m.sem("cw_hi"), m.sem("cw_lo")
        ab_ps, b_th, u_ok, tap_ok = m.sem("ab_ps"), m.sem("b_th"), m.sem("u_ok"), m.sem("tap_ok")
        mu_ps, xc_ok, sq_ok, va_ps, sd_ok, rs_ok = (m.sem("mu_ps"), m.sem("xc_ok"), m.sem("sq_ok"), m.sem("va_ps"),
                                                    m.sem("sd_ok"), m.sem("rs_ok"))
        y_ok, yh_ok, t_ok, o_ok, mh_ok, ml_ok = (m.sem("y_ok"), m.sem("yh_ok"), m.sem("t_ok"), m.sem("o_ok"),
                                                 m.sem("mh_ok"), m.sem("ml_ok"))
        m_out = m.sems("m_out", 2)
        wv = I["w_in"][0].rearrange("(k p) n -> p k n", p=P)

        def slab_col(s):
            return (COL_A if s % 2 == 0 else COL_B) + (s // 2) * P

        with nc.Block() as block:
            @block.sync
            def _(sp):
                for s in range(2 * NCT):
                    if s >= 4:
                        sp.wait_ge(w_lo, s - 3)
                    sp.dma_start(wst[:, s % 4], wv[:, :, slab_col(s):slab_col(s) + P]).then_inc(w_in[s % 4], 16)
                for n in range(NSEG):
                    for c in range(NCT):
                        q = n * NCT + c
                        sp.wait_ge(ml_ok, q + 1)
                        for part, buf in ((0, mh), (1, ml)):
                            dst = scr["mixed"][4 * n:4 * n + 4, :, part, c, :]
                            sp.dma_start(dst.rearrange("t p j -> p t j"),
                                         buf[:, q % 2, :].rearrange("p (t j) -> p t j", j=P)).then_inc(m_out[q % 2], 16)
                for s in range(2):
                    sp.wait_ge(m_out[s], 32 * (NSEG * NCT // 2))

            @block.gpsimd
            def _(pool):
                with nc.allow_non_contiguous_dma(reason="per-channel constants into columns"):
                    for c in range(NCT):
                        pool.dma_start(taps[:, c, :], I["conv_taps"][0, :, c * P:(c + 1) * P].rearrange("k p -> p k"))\
                            .then_inc(par_in, 16)
                    pool.dma_start(cb[:], I["conv_bias"][0].rearrange("(c p) -> p c", p=P)).then_inc(par_in, 16)
                    pool.dma_start(lg[:, 0, :], I["conv_ln_g"][0].rearrange("(c p) -> p c", p=P)).then_inc(par_in, 16)
                    pool.dma_start(lg[:, 1, :], I["conv_ln_b"][0].rearrange("(c p) -> p c", p=P)).then_inc(par_in, 16)

            @block.scalar
            def _(act):
                def w_split(s):
                    act.wait_ge(w_in[s % 4], 16 * (s // 4 + 1))
                    if s >= 4:
                        act.wait_ge(ab_ps, 4 * ((s - 4) // 2 + 1))
                    nc.scalar.activation(whi[:, s % 4], wst[:, s % 4], ACT.Copy).then_inc(w_hi, 1)

                for s in range(4):
                    w_split(s)
                for c in range(NCT):
                    for n in range(NSEG):
                        q = c * NSEG + n
                        act.wait_ge(ab_ps, q + 1)
                        if q >= 2:
                            act.wait_ge(u_ok, q - 1)
                        nc.scalar.activation(th[:, q % 2], pb[q % 2][:], ACT.Tanh, scale=0.5).then_inc(b_th, 1)
                    for s in (2 * c + 4, 2 * c + 5):
                        if s < 2 * NCT:
                            w_split(s)
                for n in range(NSEG):
                    for c in range(NCT):
                        q = n * NCT + c
                        act.wait_ge(xc_ok, q + 1)
                        if q >= 2:
                            act.wait_ge(va_ps, q - 1)
                        nc.scalar.activation(sq[:, q % 2], co[:, c, n * SEG:(n + 1) * SEG], ACT.Square).then_inc(sq_ok, 1)
                    act.wait_ge(va_ps, NCT * (n + 1))
                    if n >= 2:
                        act.wait_ge(y_ok, NCT * (n - 1))
                    nc.scalar.activation(rs[:, n % 2], pva[n % 2][:], ACT.Sqrt, bias=K["eps"][:, 0:1]).then_inc(sd_ok, 1)
                    for c in range(NCT):
                        q = n * NCT + c
                        act.wait_ge(y_ok, q + 1)
                        sl = co[:, c, n * SEG:(n + 1) * SEG]
                        if q >= 2:
                            act.wait_ge(ml_ok, q - 1)
                        nc.scalar.activation(y[:, q % 2], sl, ACT.Identity, bias=lg[:, 1, c:c + 1],
                                             scale=lg[:, 0, c:c + 1]).then_inc(yh_ok, 1)
                        act.wait_ge(yh_ok, q + 1)
                        nc.scalar.activation(tl[:, q % 2], y[:, q % 2], ACT.Tanh).then_inc(t_ok, 1)
                        act.wait_ge(o_ok, q + 1)
                        if q >= 2:
                            act.wait_ge(m_out[q % 2], 32 * (q // 2))
                        nc.scalar.activation(mh[:, q % 2], y[:, q % 2], ACT.Copy).then_inc(mh_ok, 1)

            @block.vector
            def _(dve):
                def w_split(s):
                    dve.wait_ge(w_hi, s + 1)
                    nc.vector.tensor_tensor(wlo[:, s % 4], wst[:, s % 4], whi[:, s % 4], ALU.subtract).then_inc(w_lo, 1)

                for s in range(4):
                    w_split(s)
                dve.wait_ge(par_in, 16 * (NCT + 3))
                nc.vector.tensor_scalar(taps[:], taps[:], 0.5, None, ALU.mult).then_inc(par_ok, 1)
                nc.vector.tensor_scalar(lg[:], lg[:], 0.5, None, ALU.mult).then_inc(par_ok, 1)

                def gated(c, n):
                    q = c * NSEG + n
                    dve.wait_ge(b_th, q + 1)
                    nc.vector.scalar_tensor_tensor(u[:, c % 2, n * SEG:(n + 1) * SEG], th[:, q % 2], 1.0, pa[q % 2][:],
                                                   ALU.add, ALU.mult).then_inc(u_ok, 1)

                def next_slabs(c):
                    for s in (2 * c + 4, 2 * c + 5):
                        if s < 2 * NCT:
                            w_split(s)

                for n in range(NSEG):
                    gated(0, n)
                next_slabs(0)
                steps = 0
                for c in range(NCT):
                    dve.wait_ge(u_ok, NSEG * (c + 1))
                    dve.wait_ge(par_ok, 2)
                    acc, up = co[:, c, :], u[:, c % 2, :]
                    nc.vector.tensor_scalar(acc, up, taps[:, c, PAD:PAD + 1], cb[:, c:c + 1], ALU.mult, ALU.add)\
                        .then_inc(tap_ok, 1)
                    steps += 1
                    a3, u3 = acc.rearrange("p (r w) -> p r w", w=GW), up.rearrange("p (r w) -> p r w", w=GW)
                    for k in range(TAPS):
                        off = k - PAD
                        if off == 0:
                            continue
                        if c < NCT // 2:
                            lo, hi = max(0, -off), GW - max(0, off)
                            o, i = a3[:, :, lo:hi], u3[:, :, lo + off:hi + off]
                        else:
                            lo, hi = max(0, -off), GH - max(0, off)
                            o, i = acc[:, lo * GW:hi * GW], up[:, (lo + off) * GW:(hi + off) * GW]
                        dve.wait_ge(tap_ok, steps)
                        nc.vector.scalar_tensor_tensor(o, i, taps[:, c, k:k + 1], o, ALU.mult, ALU.add).then_inc(tap_ok, 1)
                        steps += 1
                        if c + 1 < NCT and k % 7 == 6:
                            gated(c + 1, k // 7)
                            if k // 7 == NSEG - 1:
                                next_slabs(c + 1)
                dve.wait_ge(tap_ok, steps)

                def centre(n):
                    dve.wait_ge(mu_ps, n + 1)
                    for c in range(NCT):
                        sl = co[:, c, n * SEG:(n + 1) * SEG]
                        nc.vector.tensor_tensor(sl, sl, pmu[n % 2][:], ALU.subtract).then_inc(xc_ok, 1)

                centre(0)
                for n in range(NSEG):
                    if n + 1 < NSEG:
                        centre(n + 1)
                    dve.wait_ge(sd_ok, n + 1)
                    nc.vector.reciprocal(rs[:, n % 2], rs[:, n % 2]).then_inc(rs_ok, 1)
                    dve.wait_ge(rs_ok, n + 1)
                    for c in range(NCT):
                        sl = co[:, c, n * SEG:(n + 1) * SEG]
                        nc.vector.tensor_tensor(sl, sl, rs[:, n % 2], ALU.mult).then_inc(y_ok, 1)
                    for c in range(NCT):
                        q = n * NCT + c
                        dve.wait_ge(t_ok, q + 1)
                        nc.vector.scalar_tensor_tensor(y[:, q % 2], tl[:, q % 2], 1.0, y[:, q % 2], ALU.add, ALU.mult)\
                            .then_inc(o_ok, 1)
                        dve.wait_ge(mh_ok, q + 1)
                        if q >= 2:
                            dve.wait_ge(m_out[q % 2], 32 * (q // 2))
                        nc.vector.tensor_tensor(ml[:, q % 2], y[:, q % 2], mh[:, q % 2], ALU.subtract).then_inc(ml_ok, 1)

            @block.tensor
            def _(pe):
                for c in range(NCT):
                    pe.wait_ge(w_lo, 2 * c + 2)
                    for n in range(NSEG):
                        q = c * NSEG + n
                        if q >= 2:
                            pe.wait_ge(u_ok, q - 1)
                        t0 = TC + n * SEG
                        for s, bank in ((2 * c, pa), (2 * c + 1, pb)):
                            last = triple(nc, bank[q % 2][:], [
                                (whi[:, s % 4, k, :], wlo[:, s % 4, k, :], K["hhi"][:, k, t0:t0 + SEG],
                                 K["hlo"][:, k, t0:t0 + SEG]) for k in range(KD)])
                        last.then_inc(ab_ps, 1)
                pe.wait_ge(tap_ok, NCT * TAPS)

                def mean(n):
                    if n >= 2:
                        pe.wait_ge(xc_ok, NCT * (n - 1))
                    for c in range(NCT):
                        last = nc.tensor.matmul(pmu[n % 2][:], K["mean_cw"][:], co[:, c, n * SEG:(n + 1) * SEG],
                                                start=(c == 0), stop=(c == NCT - 1))
                    last.then_inc(mu_ps, 1)

                mean(0)
                for n in range(NSEG):
                    if n + 1 < NSEG:
                        mean(n + 1)
                    if n >= 2:
                        pe.wait_ge(sd_ok, n - 1)
                    for c in range(NCT):
                        q = n * NCT + c
                        pe.wait_ge(sq_ok, q + 1)
                        nc.tensor.matmul(pva[n % 2][:], K["mean_cw"][:], sq[:, q % 2], start=(c == 0),
                                         stop=(c == NCT - 1)).then_inc(va_ps, 1)


def heads_stage(nc, K, I, scr):
    UNITS = [(0, -1), (1, -1), (0, 0), (1, 3), (0, 1), (1, 2), (0, 2), (1, 1), (0, 3), (1, 0)]
    NU = len(UNITS)
    NX = NU - 2
    CS = SEG // CH
    BLK = P // CH
    CHAIN = 2 * (TC // CH) + NX * CS + NX
    SLABS = [COL_Q, COL_I, COL_FF, COL_FB, COL_G]
    EARLY = 4

    def size(i):
        return TC if UNITS[i][1] < 0 else SEG

    def tok0(i):
        return 0 if UNITS[i][1] < 0 else TC + SEG * UNITS[i][1]

    def xs(i):
        return max(0, i - 2)

    def order(i):
        n = size(i) // CH
        return range(n) if UNITS[i][0] == 0 else range(n - 1, -1, -1)

    chain_at, total = [], 0
    for i in range(NU):
        chain_at.append(total)
        total += size(i) // CH + (1 if UNITS[i][1] >= 0 else 0)
    assert total == CHAIN
    seen, first = set(), []
    for d, s in UNITS:
        first.append(s not in seen)
        seen.add(s)

    with nc.cleanup_on_exit(), ExitStack() as ctx:
        m = Mem(nc, ctx)
        wst = m.sb("hwst", [P, 5, KD, P])
        whi = m.sb("hwhi", [P, 5, KD, P], BF16)
        wlo = m.sb("hwlo", [P, 5, KD, P], BF16)
        qT = m.sb("qT", [P, T])
        oT = m.sb("oT", [P, T])
        sgT = m.sb("sgT", [P, T])
        v = m.sb("v", [P, 2 + NT, P])
        G = m.sb("G", [P, 2, SEG])
        KK = m.sb("KK", [P, 2, SEG])
        B = m.sb("B", [P, 2, SEG])
        E = m.sb("E", [P, 2, SEG])
        QI = m.sb("QI", [P, 2, SEG])
        KT = m.sb("KT", [P, 2, SEG])
        AT = m.sb("AT", [P, 2, SEG])
        S = m.sb("S", [P, 2, CS + 1, P])
        sm = m.sb("sm", [P, 2, 3, CS])
        se = m.sb("se", [P, 2, 3, CS])
        lbr = m.sb("lbr", [P, 2, 2, HEADS])
        lbd = m.sb("lbd", [P, 2, HEADS])
        gh = m.sb("gh", [P, 2, HEADS])
        gb = m.sb("gb", [P, 2, HEADS])
        lh = m.sb("lh", [P, 2, 2])
        ng = m.sb("ng", [P, HEADS])
        ngh = m.sb("ngh", [P, 1])
        segm = m.sb("segm", [P, SEG])
        msk = m.sb("msk", [P, 2, SEG])
        mh = m.sb("hmh", [P, 2, SEG], BF16)
        ml = m.sb("hml", [P, 2, SEG], BF16)
        pu = [m.ps(f"pu{i}", [P, SEG]) for i in range(4)]
        pj, pk, pat, po = m.ps("pj", [P, SEG]), m.ps("pk", [P, SEG]), m.ps("pat", [P, SEG]), m.ps("po", [P, SEG])

        flag = m.sb("hflag", [1, 1])
        pflag = m.sb("hpflag", [1, 1])

        hpar_in, lb_ok, msk_ok, zero_ok = m.sem("hpar_in"), m.sem("lb_ok"), m.sem("msk_ok"), m.sem("zero_ok")
        hd_ok = m.sem("hd_ok")
        pf_ok = m.sem("pf_ok")
        w_in, w_hi, w_lo = m.sems("hw_in", 5), m.sem("hw_hi"), m.sem("hw_lo")
        qv_ps, qv_ok = m.sem("qv_ps"), m.sem("qv_ok")
        pj_ps, th_ok, f_ok, kk_ok, lf_ok, b_ok = (m.sem("pj_ps"), m.sem("hth_ok"), m.sem("f_ok"), m.sem("kk_ok"),
                                                  m.sem("lf_ok"), m.sem("b_ok"))
        sm_ok, d_ok, ex_ok, qh_ok, qi_ok, kh_ok, kd_ok = (m.sem("sm_ok"), m.sem("d_ok"), m.sem("ex_ok"), m.sem("qh_ok"),
                                                          m.sem("qi_ok"), m.sem("kh_ok"), m.sem("kd_ok"))
        kt_ps, kt_ok, at_ps, at_ok, u_ps, ch_ok, o_ps, o_ok = (
            m.sem("kt_ps"), m.sem("kt_ok"), m.sem("at_ps"), m.sem("at_ok"), m.sem("u_ps"), m.sem("ch_ok"),
            m.sem("o_ps"), m.sem("ho_ok"))
        osq_ok, ms_ps, g_ps, sd_ok, rs_ok, g_th = (m.sem("osq_ok"), m.sem("ms_ps"), m.sem("g_ps"), m.sem("hsd_ok"),
                                                   m.sem("hrs_ok"), m.sem("g_th"))
        y_ok, sg_ok, hm_ok, hmh_ok, hml_ok = (m.sem("hy_ok"), m.sem("sg_ok"), m.sem("hm_ok"), m.sem("hmh_ok"),
                                              m.sem("hml_ok"))
        m_out = m.sems("hm_out", 2)
        wv = I["w_in"][0].rearrange("(k p) n -> p k n", p=P)
        ms_bank = [pk, pat, pj, po]
        sq_buf = [KT[:, 0], KT[:, 1], G[:, 0], G[:, 1]]
        rs_buf = [KK[:, 0], KK[:, 1], E[:, 0], E[:, 1]]

        with nc.Block() as block:
            @block.sync
            def _(sp):
                with nc.allow_non_contiguous_dma(reason="per-channel constants into columns"):
                    sp.dma_start(ng[:], I["hgrn_norm_g"][0].rearrange("(h p) -> p h", p=P)).then_inc(m_out[0], 16)
                    sp.dma_start(lbr[:, 0, 0, :], I["hgrn_lb_logits"][0, 0].rearrange("(h p) -> p h", p=P))\
                        .then_inc(m_out[1], 16)

                def store(r):
                    for n in range(NSEG):
                        wait(sp, hml_ok, r * NSEG + n + 1)
                        for part, buf in ((0, mh), (1, ml)):
                            dst = scr["mixed"][4 * n:4 * n + 4, :, part, bass.ds(r + NCT, 1), :]
                            sp.dma_start(dst.rearrange("t p a j -> p t (a j)"),
                                         buf[:, n % 2, :].rearrange("p (t j) -> p t j", j=P)).then_inc(m_out[n % 2], 16)

                def one(h, store_before=True):
                    for j, col in enumerate(SLABS):
                        if j == 0:
                            wait(sp, w_lo, h * 5)
                        sp.dma_start(wst[:, j], wv[:, :, bass.ds(h * P + col, P)]).then_inc(w_in[j], 16)
                    if store_before:
                        store(h - 1)

                one(0, False)
                with sp.Fori(1, HEADS) as h:
                    one(h)
                store(HEADS - 1)
                for s in range(2):
                    wait(sp, m_out[s], 16 + 32 * (HEADS * NSEG // 2))

            @block.gpsimd
            def _(pool):
                with nc.allow_non_contiguous_dma(reason="per-channel constants into columns"):
                    for l in range(2):
                        for d in range(2):
                            if (l, d) == (0, 0):
                                continue
                            pool.dma_start(lbr[:, l, d, :], I["hgrn_lb_logits"][l, d].rearrange("(h p) -> p h", p=P))\
                                .then_inc(hpar_in, 16)
                nc.gpsimd.memset(segm[:], 1.0).then_inc(msk_ok, 1)
                nc.gpsimd.memset(msk[:], 1.0).then_inc(msk_ok, 1)
                wait(pool, msk_ok, 2)
                nc.gpsimd.memset(segm[:, 0:SEG:CH], 0.0).then_inc(msk_ok, 1)
                pat4 = [[0, SEG // P], [-CH, BLK], [0, CH]]
                for d in range(2):
                    mv = msk[:, d, :].rearrange("p (r b i) -> p r b i", r=SEG // P, b=BLK)
                    conds = [(0, 1, pat4), (CH - 1, -1, [[0, SEG // P], [CH, BLK], [0, CH]]),
                             (0, -1 if d == 0 else 1,
                              [[0, SEG // P], [CH if d == 0 else -CH, BLK], [1 if d == 0 else -1, CH]])]
                    for n, (base, mult, pattern) in enumerate(conds):
                        wait(pool, msk_ok, 3 + 3 * d + n)
                        nc.gpsimd.affine_select(out=mv, in_=mv, compare_op=ALU.is_ge, fill=0.0, base=base,
                                                pattern=pattern, channel_multiplier=mult).then_inc(msk_ok, 1)
                nc.gpsimd.memset(pflag[:], 0.0).then_inc(pf_ok, 1)
                nc.gpsimd.memset(AT[:], 0.0).then_inc(zero_ok, 1)
                wait(pool, zero_ok, 1)
                def one(h):
                    def keep(i):
                        p, n = i % 2, size(i)
                        wait(pool, f_ok, h * NU + i + 1)
                        wait(pool, kt_ps, h * NU + max(0, i - 1))
                        if i < 2:
                            wait(pool, hml_ok, h * NSEG)
                        wait(pool, pf_ok, h * NU + i + 1)
                        nc.gpsimd.tensor_tensor(pflag[:], pflag[:], pflag[:], ALU.mult).then_inc(pf_ok, 1)
                        nc.gpsimd.tensor_scalar(KK[:, p, 0:n], G[:, p, 0:n], -1.0, 1.0, ALU.mult, ALU.add)\
                            .then_inc(kk_ok, 1)

                    def decay_k(i):
                        p, n = i % 2, size(i)
                        wait(pool, ex_ok, h * NU + i + 1)
                        wait(pool, kk_ok, h * NU + i + 1)
                        nc.gpsimd.tensor_tensor(B[:, p, 0:n], KK[:, p, 0:n], B[:, p, 0:n], ALU.mult).then_inc(kh_ok, 1)
                        wait(pool, kh_ok, h * NU + i + 1)
                        c3 = lambda t: t[:, p, 0:n].rearrange("p (c j) -> p c j", j=CH)
                        nc.gpsimd.tensor_tensor(c3(KK), c3(B), se[:, p, 1, 0:n // CH].unsqueeze(2)
                                                .broadcast_to([P, n // CH, CH]), ALU.mult).then_inc(kd_ok, 1)

                    keep(0)
                    keep(1)
                    decay_k(0)
                    for i in range(NU):
                        if i + 1 < NU:
                            decay_k(i + 1)
                        if i + 2 < NU:
                            keep(i + 2)

                peeled(pool, HEADS, one)

            @block.scalar
            def _(act):
                wait(act, lb_ok, 1)
                nc.scalar.activation(lbd[:], lbd[:], ACT.Tanh, scale=0.5).then_inc(lb_ok, 1)

                def split(h, j):
                    wait(act, w_in[j], h * 16 + 16)
                    wait(act, pj_ps, h * NU)
                    nc.scalar.activation(whi[:, j], wst[:, j], ACT.Copy).then_inc(w_hi, 1)

                def squares(r):
                    wait(act, o_ok, r * NX + NX)
                    wait(act, u_ps, r * NU + NU)
                    wait(act, kk_ok, r * NU + NU)
                    for n in range(NSEG):
                        nc.scalar.activation(sq_buf[n], oT[:, n * SEG:(n + 1) * SEG], ACT.Square).then_inc(osq_ok, 1)

                def deviations(r):
                    for n in range(NSEG):
                        wait(act, ms_ps, r * NSEG + n + 1)
                        nc.scalar.activation(rs_buf[n], ms_bank[n][:], ACT.Sqrt, bias=K["eps"][:, 0:1])\
                            .then_inc(sd_ok, 1)

                def cast(r):
                    for n in range(NSEG):
                        wait(act, hm_ok, r * NSEG + n + 1)
                        wait(act, m_out[n % 2], r * 64 + 32 * (n // 2) + 16)
                        nc.scalar.activation(mh[:, n % 2], oT[:, n * SEG:(n + 1) * SEG], ACT.Copy).then_inc(hmh_ok, 1)

                def one(h, readout=True):
                    split(h, 0)
                    if readout:
                        squares(h - 1)
                    for j in (1, 4, 2, 3):
                        split(h, j)
                    for n in range(4):
                        wait(act, qv_ps, h * 9 + n + 1)
                        wait(act, qi_ok, h * NX)
                        nc.scalar.activation(qT[:, n * SEG:(n + 1) * SEG], pu[n][:], ACT.Copy).then_inc(qv_ok, 1)
                        if n == 0 and readout:
                            deviations(h - 1)
                    if readout:
                        cast(h - 1)
                    for n in range(5):
                        wait(act, qv_ps, h * 9 + n + 5)
                        t0, k = (0, 2) if n == 4 else (2 + 4 * n, 4)
                        bank = pj if n == 4 else pu[n]
                        wait(act, o_ps, h * NX)
                        nc.scalar.activation(v[:, t0:t0 + k, :], bank[:, 0:k * P].rearrange("p (t j) -> p t j", j=P),
                                             ACT.Copy).then_inc(qv_ok, 1)
                    for n in range(NSEG):
                        wait(act, g_ps, h * NSEG + n + 1)
                        wait(act, hm_ok, h * NSEG)
                        nc.scalar.activation(sgT[:, n * SEG:(n + 1) * SEG], pu[n][:], ACT.Tanh, scale=0.5)\
                            .then_inc(g_th, 1)

                    def gate(i):
                        p, n = i % 2, size(i)
                        wait(act, pj_ps, h * NU + i + 1)
                        wait(act, kk_ok, h * NU + max(0, i - 1))
                        wait(act, lf_ok, h * NU + max(0, i - 1))
                        if i < 2:
                            wait(act, hml_ok, h * NSEG)
                        nc.scalar.activation(G[:, p, 0:n], pj[:, 0:n], ACT.Tanh, scale=0.5).then_inc(th_ok, 1)

                    def logs(i):
                        p, n = i % 2, size(i)
                        wait(act, f_ok, h * NU + i + 1)
                        wait(act, at_ps, h * NX + (xs(i - 1) if i >= 2 else 0))
                        wait(act, qi_ok, h * NX + (xs(i - 1) if i >= 2 else 0))
                        nc.scalar.activation(E[:, p, 0:n], G[:, p, 0:n], ACT.Ln).then_inc(lf_ok, 1)

                    def exps(i):
                        p, n = i % 2, size(i)
                        wait(act, d_ok, h * NU + i + 1)
                        wait(act, kd_ok, h * NU + max(0, i - 1))
                        wait(act, qi_ok, h * NX + (xs(i - 1) if i >= 2 else 0))
                        wait(act, ch_ok, h * CHAIN + (chain_at[i - 1] if i >= 2 else 0))
                        nc.scalar.activation(se[:, p, :, 0:n // CH], sm[:, p, :, 0:n // CH], ACT.Exp).then_inc(sm_ok, 1)
                        if UNITS[i][1] >= 0:
                            nc.scalar.activation(E[:, p, 0:n], B[:, p, 0:n], ACT.Exp).then_inc(sm_ok, 1)
                        nc.scalar.activation(B[:, p, 0:n], B[:, p, 0:n], ACT.Exp, scale=-1.0).then_inc(ex_ok, 1)

                    def turn(i):
                        p, n = i % 2, size(i)
                        wait(act, kt_ps, h * NU + i + 1)
                        wait(act, u_ps, h * NU + max(0, i - 1))
                        if i < 2:
                            wait(act, hml_ok, h * NSEG)
                        nc.scalar.activation(KT[:, p, 0:n], pk[:, 0:n], ACT.Copy).then_inc(kt_ok, 1)

                    gate(0)
                    logs(0)
                    gate(1)
                    exps(0)
                    logs(1)
                    turn(0)
                    for i in range(NU):
                        if i + 1 < NU:
                            exps(i + 1)
                        if i + 1 < NU:
                            turn(i + 1)
                        if i + 2 < NU:
                            gate(i + 2)
                            logs(i + 2)

                one(0, False)
                with act.Fori(1, HEADS) as h:
                    one(h)
                squares(HEADS - 1)
                deviations(HEADS - 1)
                cast(HEADS - 1)

            @block.vector
            def _(dve):
                wait(dve, hpar_in, 48)
                wait(dve, m_out[0], 16)
                wait(dve, m_out[1], 16)
                nc.vector.tensor_tensor(lbd[:], lbr[:, 0], lbr[:, 1], ALU.subtract).then_inc(lb_ok, 1)
                wait(dve, lb_ok, 2)
                nc.vector.tensor_scalar(gh[:], lbd[:], -0.25, 0.25, ALU.mult, ALU.add).then_inc(lb_ok, 1)
                nc.vector.tensor_scalar(gb[:], lbd[:], 0.25, 0.75, ALU.mult, ALU.add).then_inc(lb_ok, 1)
                nc.vector.tensor_scalar(ng[:], ng[:], 0.5, None, ALU.mult).then_inc(lb_ok, 1)
                wait(dve, lb_ok, 5)
                wait(dve, msk_ok, 9)
                wait(dve, zero_ok, 1)

                def split(h, j):
                    wait(dve, w_hi, h * 5 + (0, 2, 4, 5, 3)[j] if j else h * 5 + 1)
                    nc.vector.tensor_tensor(wlo[:, j], wst[:, j], whi[:, j], ALU.subtract).then_inc(w_lo, 1)

                def readout(r):
                    for n in range(NSEG):
                        wait(dve, sd_ok, r * NSEG + n + 1)
                        nc.vector.reciprocal(rs_buf[n], rs_buf[n]).then_inc(rs_ok, 1)
                        sl = oT[:, n * SEG:(n + 1) * SEG]
                        wait(dve, rs_ok, r * NSEG + n + 1)
                        nc.vector.tensor_tensor(sl, sl, rs_buf[n], ALU.mult).then_inc(y_ok, 1)
                        wait(dve, y_ok, r * NSEG + n + 1)
                        nc.vector.scalar_tensor_tensor(sl, sl, ngh[:, 0:1], sgT[:, n * SEG:(n + 1) * SEG], ALU.mult,
                                                       ALU.mult).then_inc(hm_ok, 1)
                        wait(dve, hmh_ok, r * NSEG + n + 1)
                        wait(dve, m_out[n % 2], r * 64 + 32 * (n // 2) + 16)
                        nc.vector.tensor_tensor(ml[:, n % 2], sl, mh[:, n % 2], ALU.subtract).then_inc(hml_ok, 1)

                def one(h, finish=True):
                    for j in (0, 1, 4, 2, 3):
                        split(h, j)
                    if finish:
                        readout(h - 1)
                    wait(dve, hml_ok, h * NSEG)
                    for d in range(2):
                        nc.vector.tensor_copy(lh[:, d, 0:1], gh[:, d, bass.ds(h, 1)]).then_inc(hd_ok, 1)
                        nc.vector.tensor_copy(lh[:, d, 1:2], gb[:, d, bass.ds(h, 1)]).then_inc(hd_ok, 1)
                    nc.vector.tensor_copy(ngh[:], ng[:, bass.ds(h, 1)]).then_inc(hd_ok, 1)
                    wait(dve, o_ps, h * NX)
                    nc.vector.memset(S[:, :, 0, :], 0.0).then_inc(hd_ok, 1)
                    wait(dve, hd_ok, h * 6 + 6)
                    for n in range(NSEG):
                        sl = sgT[:, n * SEG:(n + 1) * SEG]
                        wait(dve, g_th, h * NSEG + n + 1)
                        nc.vector.scalar_tensor_tensor(sl, sl, 1.0, pu[n][:], ALU.add, ALU.mult).then_inc(sg_ok, 1)

                    def forget(i):
                        p, n, d = i % 2, size(i), UNITS[i][0]
                        wait(dve, th_ok, h * NU + i + 1)
                        nc.vector.tensor_scalar(G[:, p, 0:n], G[:, p, 0:n], lh[:, d, 0:1], lh[:, d, 1:2], ALU.mult,
                                                ALU.add).then_inc(f_ok, 1)

                    def sums(i):
                        p, n, d = i % 2, size(i), UNITS[i][0]
                        nch = n // CH
                        mid, end = (CH // 2 - 1, CH - 1) if d == 0 else (CH // 2, 0)
                        wait(dve, lf_ok, h * NU + i + 1)
                        wait(dve, kd_ok, h * NU + max(0, i - 1))
                        way = slice(0, n) if d == 0 else slice(n - 1, None, -1)
                        nc.vector.tensor_tensor_scan(B[:, p, way], segm[:, 0:n], E[:, p, way], 0.0, ALU.mult, ALU.add)\
                            .then_inc(b_ok, 1)
                        b3 = B[:, p, 0:n].rearrange("p (c j) -> p c j", j=CH)
                        wait(dve, b_ok, h * 3 * NU + 3 * i + 1)
                        wait(dve, ex_ok, h * NU + max(0, i - 1))
                        nc.vector.tensor_copy(sm[:, p, 0, 0:nch], b3[:, :, mid]).then_inc(b_ok, 1)
                        nc.vector.tensor_copy(sm[:, p, 2, 0:nch], b3[:, :, end]).then_inc(b_ok, 1)
                        wait(dve, b_ok, h * 3 * NU + 3 * i + 3)
                        nc.vector.tensor_tensor(sm[:, p, 1, 0:nch], sm[:, p, 2, 0:nch], sm[:, p, 0, 0:nch],
                                                ALU.subtract)
                        nc.vector.tensor_tensor(b3, b3, sm[:, p, 0, 0:nch].unsqueeze(2).broadcast_to([P, nch, CH]),
                                                ALU.subtract).then_inc(d_ok, 1)

                    def decay_q(i):
                        if UNITS[i][1] < 0:
                            return
                        t0 = UNITS[i][1] * SEG
                        wait(dve, ex_ok, h * NU + i + 1)
                        wait(dve, qv_ok, h * 9 + 4)
                        nc.vector.tensor_tensor(E[:, i % 2], qT[:, t0:t0 + SEG], E[:, i % 2], ALU.mult)\
                            .then_inc(qh_ok, 1)

                    def decay_q_start(i):
                        p = i % 2
                        if UNITS[i][1] < 0:
                            return
                        wait(dve, qh_ok, h * NX + xs(i) + 1)
                        wait(dve, o_ps, h * NX + xs(i - 1))
                        c3 = lambda t: t[:, p].rearrange("p (c j) -> p c j", j=CH)
                        nc.vector.tensor_tensor(c3(QI), c3(E), se[:, p, 0].unsqueeze(2).broadcast_to([P, CS, CH]),
                                                ALU.mult).then_inc(qi_ok, 1)

                    def mask(i):
                        if UNITS[i][1] < 0:
                            return
                        wait(dve, at_ps, h * NX + xs(i) + 1)
                        wait(dve, o_ps, h * NX + xs(i - 1))
                        nc.vector.memset(flag[:], 0.0)
                        nc.vector.copy_predicated(AT[:, i % 2], msk[:, UNITS[i][0]].bitcast(U32), pat[:])\
                            .then_inc(at_ok, 1)

                    def chain(i, part):
                        p, d = i % 2, UNITS[i][0]
                        done = chain_at[i]
                        if UNITS[i][1] >= 0:
                            if part == 0:
                                wait(dve, o_ps, h * NX + xs(i - 1))
                                prev = size(i - 2) // CH
                                wait(dve, ch_ok, h * CHAIN + chain_at[i])
                                nc.vector.tensor_copy(S[:, d, 0, :], S[:, d, prev, :]).then_inc(ch_ok, 1)
                            done += 1
                        if part == 0:
                            wait(dve, u_ps, h * NU + i + 1)
                        for n, c in enumerate(order(i)):
                            if (n < EARLY) == (part == 0):
                                wait(dve, ch_ok, h * CHAIN + done + n)
                                nc.vector.scalar_tensor_tensor(S[:, d, n + 1, :], S[:, d, n, :], se[:, p, 2, c:c + 1],
                                                               pu[c % BLK][:, (c // BLK) * P:(c // BLK + 1) * P],
                                                               ALU.mult, ALU.add).then_inc(ch_ok, 1)

                    def collect(i):
                        if i < 2:
                            return
                        t0 = UNITS[i][1] * SEG
                        wait(dve, o_ps, h * NX + xs(i) + 1)
                        if first[i]:
                            ins = nc.vector.tensor_copy(oT[:, t0:t0 + SEG], po[:])
                        else:
                            wait(dve, o_ok, h * NX + xs(i))
                            ins = nc.vector.tensor_tensor(oT[:, t0:t0 + SEG], oT[:, t0:t0 + SEG], po[:], ALU.add)
                        ins.then_inc(o_ok, 1)

                    forget(0)
                    sums(0)
                    forget(1)
                    for i in range(NU):
                        if i >= 2:
                            collect(i - 2)
                        if i + 1 < NU:
                            sums(i + 1)
                        chain(i, 0)
                        if i + 1 < NU:
                            decay_q(i + 1)
                        chain(i, 1)
                        if i + 1 < NU:
                            decay_q_start(i + 1)
                        if i + 2 < NU:
                            forget(i + 2)
                        if i + 1 < NU:
                            mask(i + 1)
                    collect(NU - 2)
                    collect(NU - 1)

                one(0, False)
                with dve.Fori(1, HEADS) as h:
                    one(h)
                readout(HEADS - 1)

            @block.tensor
            def _(pe):
                def means(r):
                    for n in range(NSEG):
                        wait(pe, osq_ok, r * NSEG + n + 1)
                        nc.tensor.matmul(ms_bank[n][:], K["mean_p"][:], sq_buf[n], start=True, stop=True)\
                            .then_inc(ms_ps, 1)

                def one(h, readout=True):
                    def pairs(j, t0, n):
                        return [(whi[:, j, k, :], wlo[:, j, k, :], K["hhi"][:, k, t0:t0 + n], K["hlo"][:, k, t0:t0 + n])
                                for k in range(KD)]

                    wait(pe, w_lo, h * 5 + 1)
                    wait(pe, ch_ok, h * CHAIN)
                    for n in range(4):
                        triple(nc, pu[n][:], pairs(0, TC + n * SEG, SEG)).then_inc(qv_ps, 1)
                        if n == 0 and readout:
                            means(h - 1)
                    wait(pe, w_lo, h * 5 + 2)
                    for n in range(5):
                        t0, cnt = (0, 2) if n == 4 else (2 + 4 * n, 4)
                        bank = pj if n == 4 else pu[n]
                        if n < 4:
                            wait(pe, qv_ok, h * 9 + n + 1)
                        else:
                            wait(pe, sd_ok, h * NSEG)
                        for t in range(t0, t0 + cnt):
                            last = triple(nc, bank[:, (t - t0) * P:(t - t0 + 1) * P], [
                                (K["hhi"][:, k, t * P:(t + 1) * P], K["hlo"][:, k, t * P:(t + 1) * P],
                                 whi[:, 1, k, :], wlo[:, 1, k, :]) for k in range(KD)])
                        last.then_inc(qv_ps, 1)
                    wait(pe, w_lo, h * 5 + 3)
                    for n in range(NSEG):
                        wait(pe, qv_ok, h * 9 + n + 5)
                        triple(nc, pu[n][:], pairs(4, TC + n * SEG, SEG)).then_inc(g_ps, 1)

                    def project(i, first=0, end=3 * KD):
                        j, n = 2 + UNITS[i][0], size(i)
                        for mm in range(first, end):
                            if mm == 0:
                                if i == 0:
                                    wait(pe, w_lo, h * 5 + 5)
                                    wait(pe, qv_ok, h * 9 + 9)
                                wait(pe, th_ok, h * NU + i)
                            lh, ll, rh, rl = pairs(j, tok0(i), n)[mm // 3]
                            w, x = ((lh, rh), (lh, rl), (ll, rh))[mm % 3]
                            ins = nc.tensor.matmul(pj[:, 0:n], w, x, start=(mm == 0), stop=(mm == 3 * KD - 1))
                        if end == 3 * KD:
                            ins.then_inc(pj_ps, 1)

                    def scores(i):
                        p, tiles = i % 2, size(i) // P
                        wait(pe, kd_ok, h * NU + i + 1)
                        wait(pe, kt_ok, h * NU + i)
                        for t in range(tiles):
                            last = nc.tensor.transpose(pk[:, t * P:(t + 1) * P], KK[:, p, t * P:(t + 1) * P],
                                                       K["ident"][:])
                        last.then_inc(kt_ps, 1)
                        if UNITS[i][1] >= 0:
                            wait(pe, qh_ok, h * NX + xs(i) + 1)
                            wait(pe, at_ok, h * NX + xs(i))
                            for t in range(tiles):
                                last = nc.tensor.matmul(pat[:, t * P:(t + 1) * P], B[:, p, t * P:(t + 1) * P],
                                                        E[:, p, t * P:(t + 1) * P], start=True, stop=True)
                            last.then_inc(at_ps, 1)

                    def updates(i):
                        p, tiles, v0 = i % 2, size(i) // P, tok0(i) // P
                        wait(pe, kt_ok, h * NU + i + 1)
                        wait(pe, ch_ok, h * CHAIN + chain_at[i])
                        if i == 0:
                            wait(pe, sg_ok, h * NSEG + NSEG)
                        for t in range(tiles):
                            for j in range(BLK):
                                rows = slice(CH * j, CH * (j + 1))
                                last = nc.tensor.matmul(pu[j][:, t * P:(t + 1) * P], KT[rows, p, t * P:(t + 1) * P],
                                                        v[rows, v0 + t, :], start=True, stop=True)
                        last.then_inc(u_ps, 1)

                    def output(i, mm):
                        p, d, v0 = i % 2, UNITS[i][0], tok0(i) // P
                        if mm == 0:
                            wait(pe, at_ok, h * NX + xs(i) + 1)
                            wait(pe, qi_ok, h * NX + xs(i) + 1)
                            wait(pe, o_ok, h * NX + xs(i))
                            wait(pe, ch_ok, h * CHAIN + (chain_at[i + 1] if i + 1 < NU else CHAIN))
                        if mm < SEG // P:
                            nc.tensor.matmul(po[:, mm * P:(mm + 1) * P], v[:, v0 + mm, :], AT[:, p, mm * P:(mm + 1) * P],
                                             start=(mm == 0), stop=False, skip_group_check=True)
                        else:
                            n = mm - SEG // P
                            c = order(i)[n]
                            ins = nc.tensor.matmul(po[:, c * CH:(c + 1) * CH], S[:, d, n, :], QI[:, p, c * CH:(c + 1) * CH],
                                                   start=False, stop=(n == CS - 1), skip_group_check=True)
                            if n == CS - 1:
                                ins.then_inc(o_ps, 1)

                    def project_and_output(i, first, end):
                        for mm in range(first, end):
                            if i + 2 < NU:
                                project(i + 2, mm, mm + 1)
                            if i >= 3 and mm < SEG // P + CS:
                                output(i - 1, mm)

                    project(0)
                    project(1)
                    scores(0)
                    for i in range(NU + 1):
                        if i < NU:
                            updates(i)
                        project_and_output(i, 0, 2 * KD)
                        if i + 1 < NU:
                            scores(i + 1)
                        project_and_output(i, 2 * KD, 3 * KD)

                one(0, False)
                with pe.Fori(1, HEADS) as h:
                    one(h)
                means(HEADS - 1)


def outproj_stage(nc, K, I, scr):
    with nc.cleanup_on_exit(), ExitStack() as ctx:
        m = Mem(nc, ctx)
        wst = m.sb("owst", [P, 2, KD, SEG])
        whi = m.sb("owhi", [P, KD, D], BF16)
        wlo = m.sb("owlo", [P, KD, D], BF16)
        rw = m.sb("rw", [P, KD, NE])
        mrow = m.sb("mrow", [P, 3, D])
        xt = m.sb("xt", [P, 2, D])
        mx = m.sb("mx", [P, 2, 2, KD, P], BF16)
        t1 = m.sb("t1", [P, 2, D])
        x1 = m.sb("x1", [P, 2, D])
        junk = m.sb("ojunk", [P, D])
        st = m.sb("st", [P, 2, 4])
        h2 = m.sb("h2", [P, 2, D])
        row32 = m.sb("row", [P, 2, ROWW], I32)
        row = row32[:].bitcast(BF16)
        prob = row32[:, :, D:ROWW].bitcast(F32)
        h2T = m.sb("h2T", [P, D])
        nm = m.sb("nm", [P, 2, 4])
        pe_ = m.sb("pexp", [P, 2, NE])
        pT = m.sb("pT", [NE, T])
        pout = [m.ps(f"pout{i}", [P, 2, SEG]) for i in range(2)]
        ptp = m.ps("ptp", [P, 2, SEG])
        plg = m.ps("plg", [P, SEG])[:, 0:NE]
        ppt = m.ps("ppt", [P, SEG])[0:NE, 0:P]

        w_in, w_hi, w_lo, r_in = m.sems("ow_in", 2), m.sem("ow_hi"), m.sem("ow_lo"), m.sem("or_in")
        x_in, m_in = m.sems("ox_in", 2), m.sems("om_in", 2)
        out_ps, t1_ok, x1_ok, ss_ok, sd_ok, rs_ok, hn_ok, h2_ok = (
            m.sems("oo_ps", 2), m.sems("ot1", 2), m.sems("ox1", 2), m.sems("oss", 2), m.sems("osd", 2),
            m.sems("ors", 2), m.sems("ohn", 2), m.sems("oh2", 2))
        hi_ok, lo_ok, tp_ps, tp_ok, lg_ps, mx_ok, ex_ok, ri_ok, pr_ok, pt_ps, pt_ok = (
            m.sems("ohi", 2), m.sems("olo", 2), m.sems("otp", 2), m.sems("otc", 2), m.sems("olg", 2), m.sems("omx", 2),
            m.sems("oex", 2), m.sems("ori", 2), m.sems("opr", 2), m.sems("oppt", 2), m.sems("optc", 2))
        x1_out, row_out = m.sems("x1_out", 2), m.sems("orow_out", 2)
        pT_out = m.sem("pT_out")
        wv = I["w_out"][0].rearrange("(k p) n -> p k n", p=P)

        def steps(engine, step):
            def two(i):
                step(i * 2 + 2, 0, i + 1, (True, True, True))
                step(i * 2 + 3, 1, i + 1, (True, True, True))

            step(0, 0, 0, (True, False, False))
            step(1, 1, 0, (True, True, False))
            peeled(engine, NT // 2 - 1, two)
            step(NT, 0, NT // 2, (False, True, True))
            step(NT + 1, 1, NT // 2, (False, False, True))

        def tile_rows(ap, t):
            return ap[bass.ds(t * P, P), :]

        with nc.Block() as block:
            @block.sync
            def _(sp):
                for c in range(2):
                    sp.dma_start(wst[:, c], wv[:, :, c * SEG:(c + 1) * SEG]).then_inc(w_in[c], 16)
                sp.dma_start(rw[:], I["router_w"][0].rearrange("(k p) e -> p k e", p=P)).then_inc(r_in, 16)
                for j, r in enumerate((0, 2, 1)):
                    sp.dma_start(mrow[:, j], scr["modrows"][2 * r:2 * r + 2, :].rearrange("a n -> (a n)")
                                 .partition_broadcast(P)).then_inc(r_in, 16)

                def load(t, p, n):
                    wait(sp, x1_ok[p], n)
                    sp.dma_start(xt[:, p], tile_rows(I["x"][0], t)).then_inc(x_in[p], 16)
                    wait(sp, out_ps[p], n)
                    sp.dma_start(mx[:, p], scr["mixed"][bass.ds(t, 1), :, :, :, :].rearrange("t p a c j -> (t p) a c j"))\
                        .then_inc(m_in[p], 16)

                def store(t, p, n):
                    wait(sp, x1_ok[p], n + 1)
                    sp.dma_start(tile_rows(scr["y"], t), x1[:, p]).then_inc(x1_out[p], 16)
                    wait(sp, pr_ok[p], n + 1)
                    wait(sp, lo_ok[p], n + 1)
                    sp.dma_start(tile_rows(scr["rows"], t), row32[:, p]).then_inc(row_out[p], 16)

                load(0, 0, 0)
                load(1, 1, 0)

                def two(i):
                    load(i * 2 + 2, 0, i + 1)
                    store(i * 2, 0, i)
                    load(i * 2 + 3, 1, i + 1)
                    store(i * 2 + 1, 1, i)

                peeled(sp, NT // 2 - 1, two)
                store(NT - 2, 0, NT // 2 - 1)
                store(NT - 1, 1, NT // 2 - 1)
                wait(sp, pt_ok[0], NT // 2)
                wait(sp, pt_ok[1], NT // 2)
                sp.dma_start(scr["pT"], pT[:]).then_inc(pT_out, 16)
                for s in range(2):
                    wait(sp, x1_out[s], 16 * NT // 2)
                    wait(sp, row_out[s], 16 * NT // 2)
                wait(sp, pT_out, 16)

            @block.gpsimd
            def _(pool):
                wait(pool, r_in, 64)

                def front(t, p, n):
                    wait(pool, x_in[p], n * 16 + 16)
                    wait(pool, t1_ok[p], n + 1)
                    wait(pool, x1_out[p], n * 16)
                    wait(pool, hn_ok[p], n)
                    nc.gpsimd.tensor_tensor(x1[:, p], xt[:, p], t1[:, p], ALU.add).then_inc(x1_ok[p], 1)
                    wait(pool, hn_ok[p], n + 1)
                    nc.gpsimd.tensor_tensor(h2[:, p], h2[:, p], mrow[:, 2], ALU.add).then_inc(h2_ok[p], 1)

                steps(pool, lambda t, p, n, have: front(t, p, n) if have[0] else None)

            @block.scalar
            def _(act):
                for c in range(2):
                    wait(act, w_in[c], 16)
                    nc.scalar.activation(whi[:, :, c * SEG:(c + 1) * SEG], wst[:, c], ACT.Copy).then_inc(w_hi, 1)

                def front(t, p, n):
                    wait(act, x1_ok[p], n + 1)
                    nc.scalar.activation(junk[:], x1[:, p], ACT.Square, accum_out=st[:, p, 0:1]).then_inc(ss_ok[p], 1)
                    wait(act, ss_ok[p], n + 1)
                    nc.scalar.activation(st[:, p, 1:2], st[:, p, 0:1], ACT.Sqrt, bias=K["eps"][:, 0:1], scale=1.0 / D)\
                        .then_inc(sd_ok[p], 1)
                    wait(act, h2_ok[p], n + 1)
                    wait(act, row_out[p], n * 16)
                    nc.scalar.activation(row[:, p, 0:D], h2[:, p], ACT.Copy).then_inc(hi_ok[p], 1)

                def turn(p, n):
                    wait(act, tp_ps[p], n + 1)
                    wait(act, lg_ps[1 - p], n + p)
                    nc.scalar.activation(h2T[:], ptp[:].rearrange("p a j -> p (a j)"), ACT.Copy).then_inc(tp_ok[p], 1)

                def route(p, n):
                    wait(act, mx_ok[p], n + 1)
                    nc.scalar.activation(pe_[:, p], plg, ACT.Exp, bias=nm[:, p, 0:1], accum_out=nm[:, p, 1:2])\
                        .then_inc(ex_ok[p], 1)

                def step(t, p, n, have):
                    if have[2]:
                        route(p, n - 1)
                    if have[1]:
                        turn(1 - p, n - 1 + p)
                    if have[0]:
                        front(t, p, n)

                steps(act, step)

            @block.vector
            def _(dve):
                for c in range(2):
                    wait(dve, w_hi, c + 1)
                    nc.vector.tensor_tensor(wlo[:, :, c * SEG:(c + 1) * SEG], wst[:, c], whi[:, :, c * SEG:(c + 1) * SEG],
                                            ALU.subtract).then_inc(w_lo, 1)
                wait(dve, r_in, 64)

                def front(t, p, n):
                    wait(dve, out_ps[p], n + 1)
                    wait(dve, x1_ok[p], n)
                    nc.vector.tensor_tensor(t1[:, p], pout[p][:].rearrange("p a j -> p (a j)"), mrow[:, 0], ALU.mult)\
                        .then_inc(t1_ok[p], 1)
                    wait(dve, sd_ok[p], n + 1)
                    nc.vector.reciprocal(st[:, p, 2:3], st[:, p, 1:2]).then_inc(rs_ok[p], 1)
                    wait(dve, rs_ok[p], n + 1)
                    wait(dve, x1_ok[p], n + 1)
                    wait(dve, tp_ps[p], n)
                    nc.vector.scalar_tensor_tensor(h2[:, p], x1[:, p], st[:, p, 2:3], mrow[:, 1], ALU.mult, ALU.mult)\
                        .then_inc(hn_ok[p], 1)
                    wait(dve, hi_ok[p], n + 1)
                    nc.vector.tensor_tensor(row[:, p, D:2 * D], h2[:, p], row[:, p, 0:D], ALU.subtract).then_inc(lo_ok[p], 1)

                def route(t, p, n):
                    wait(dve, lg_ps[p], n + 1)
                    nc.vector.tensor_reduce(nm[:, p, 0:1], plg, AX.X, ALU.max, negate=True).then_inc(mx_ok[p], 1)
                    wait(dve, ex_ok[p], n + 1)
                    nc.vector.reciprocal(nm[:, p, 2:3], nm[:, p, 1:2]).then_inc(ri_ok[p], 1)
                    wait(dve, ri_ok[p], n + 1)
                    nc.vector.tensor_scalar(prob[:, p, :], pe_[:, p], nm[:, p, 2:3], None, ALU.mult)\
                        .then_inc(pr_ok[p], 1)
                    wait(dve, pt_ps[p], n + 1)
                    nc.vector.tensor_copy(pT[:, bass.ds(t * P, P)], ppt).then_inc(pt_ok[p], 1)

                def step(t, p, n, have):
                    if have[2]:
                        route(t - 2, p, n - 1)
                    if have[0]:
                        front(t, p, n)

                steps(dve, step)

            @block.tensor
            def _(pe):
                wait(pe, w_lo, 2)
                wait(pe, r_in, 64)

                def project(p, n, c):
                    if c == 0:
                        wait(pe, m_in[p], n * 16 + 16)
                        wait(pe, t1_ok[p], n)
                    last = triple(nc, pout[p][:, c, :], [
                        (mx[:, p, 0, k, :], mx[:, p, 1, k, :], whi[:, k, c * SEG:(c + 1) * SEG],
                         wlo[:, k, c * SEG:(c + 1) * SEG]) for k in range(KD)])
                    if c == 1:
                        last.then_inc(out_ps[p], 1)

                def turn(p, n):
                    wait(pe, h2_ok[p], n + 1)
                    wait(pe, tp_ok[1 - p], n + p)
                    for k in range(KD):
                        last = nc.tensor.transpose(ptp[:, k // 4, (k % 4) * P:(k % 4 + 1) * P], h2[:, p, k * P:(k + 1) * P],
                                                   K["ident"][:])
                    last.then_inc(tp_ps[p], 1)

                def logits(p, n):
                    wait(pe, tp_ok[p], n + 1)
                    wait(pe, ex_ok[1 - p], n + p)
                    for k in range(KD):
                        last = nc.tensor.matmul(plg, h2T[:, k * P:(k + 1) * P], rw[:, k, :], start=(k == 0),
                                                stop=(k == KD - 1))
                    last.then_inc(lg_ps[p], 1)

                def spread(p, n):
                    wait(pe, pr_ok[p], n + 1)
                    wait(pe, pt_ok[1 - p], n + p)
                    nc.tensor.transpose(ppt, prob[:, p, :], K["ident"][:]).then_inc(pt_ps[p], 1)

                def step(t, p, n, have):
                    if have[0]:
                        project(p, n, 0)
                    if have[2]:
                        logits(p, n - 1)
                    if have[0]:
                        project(p, n, 1)
                    if have[2]:
                        spread(p, n - 1)
                    if have[1]:
                        turn(1 - p, n - 1 + p)

                steps(pe, step)


def topk_stage(nc, K, I, scr):
    NCK = P // NE
    W = T // NCK
    BITS = 30
    with nc.cleanup_on_exit(), ExitStack() as ctx:
        m = Mem(nc, ctx)
        pr = m.sb("pr", [P, W])
        tmp = m.sb("tmp", [P, W])
        gt = m.sb("gt", [P, W])
        eq = m.sb("eq", [P, W])
        cg = m.sb("cg", [P, W])
        ce = m.sb("ce", [P, W])
        slot = m.sb("slot", [P, W])
        onesw = m.sb("onesw", [P, W])
        same = m.sb("same", [P, P])
        before = m.sb("before", [P, P])
        thr = m.sb("thr", [P, 1])
        cand = m.sb("cand", [P, 2, 1])
        cnt = m.sb("cnt", [P, 2])
        acc = m.sb("accp", [P, 1])
        base = m.sb("base", [P, 4])
        sT = m.sb("sT", [P, NE, NCK, 2])
        hi = m.sb("thi", [P, NE, NCK, 2])
        pcol = m.sb("pcol", [P, 1])
        tcol = m.sb("tcol", [P, NCK, 2])
        R = K["R"]
        pc = m.ps("pc", [P, SEG])
        pc2 = m.ps("pc2", [P, SEG])
        ptr = m.ps("ptr", [P, 4, P])

        p_in, cst, c_ok, cnt_ok, tot, a_ok, t_ok = (m.sem("tp_in"), m.sem("tcst"), m.sem("tc_ok"), m.sem("tcnt"),
                                                    m.sem("ttot"), m.sem("ta_ok"), m.sem("tt_ok"))
        fin, ofs, slo, trp, ve = m.sem("tfin"), m.sem("tofs"), m.sem("tslo"), m.sem("ttrp"), m.sem("tve")
        with nc.Block() as block:
            @block.sync
            def _(sp):
                sp.dma_start(pr[:], scr["pT"].rearrange("e (c w) -> (e c) w", w=W)).then_inc(p_in, 16)

            @block.gpsimd
            def _(pool):
                nc.gpsimd.memset(same[:], 1.0).then_inc(cst, 1)
                nc.gpsimd.memset(onesw[:], 1.0).then_inc(cst, 1)
                nc.gpsimd.iota(pcol[:], [[0, 1]], base=0, channel_multiplier=1,
                               allow_small_or_imprecise_dtypes=True).then_inc(cst, 1)
                nc.gpsimd.iota(tcol[:], [[2, NCK], [1, 2]], base=0, channel_multiplier=0,
                               allow_small_or_imprecise_dtypes=True).then_inc(cst, 1)
                pool.wait_ge(cst, 4)
                sv = same[:].rearrange("p (e c) -> p e c", c=NCK)
                nc.gpsimd.affine_select(out=sv, in_=sv, compare_op=ALU.is_ge, fill=0.0, base=0,
                                        pattern=[[-NCK, NE], [0, NCK]], channel_multiplier=1).then_inc(cst, 1)
                pool.wait_ge(cst, 5)
                nc.gpsimd.affine_select(out=sv, in_=sv, compare_op=ALU.is_ge, fill=0.0, base=NCK - 1,
                                        pattern=[[NCK, NE], [0, NCK]], channel_multiplier=-1).then_inc(cst, 1)
                pool.wait_ge(cst, 6)
                nc.gpsimd.affine_select(out=before[:], in_=same[:], compare_op=ALU.is_ge, fill=0.0, base=-1,
                                        pattern=[[1, P]], channel_multiplier=-1).then_inc(cst, 1)

            @block.vector
            def _(dve):
                nc.vector.memset(thr[:], 0.0).then_inc(t_ok, 1)
                dve.wait_ge(p_in, 16)
                dve.wait_ge(cst, 7)
                for b in range(BITS):
                    dve.wait_ge(t_ok, b + 1)
                    nc.vector.tensor_scalar(cand[:, b % 2].bitcast(U32), thr[:].bitcast(U32), 1 << (BITS - 1 - b), None,
                                            ALU.bitwise_or).then_inc(c_ok, 1)
                    dve.wait_ge(c_ok, b + 1)
                    nc.vector.tensor_scalar(tmp[:], pr[:], cand[:, b % 2], None, ALU.is_ge, ALU.add,
                                            accum_out=cnt[:, b % 2:b % 2 + 1]).then_inc(cnt_ok, 1)
                    dve.wait_ge(tot, b + 1)
                    nc.vector.scalar_tensor_tensor(acc[:], pc[:, b % 2:b % 2 + 1], float(CAP), cand[:, b % 2], ALU.is_ge,
                                                   ALU.mult).then_inc(a_ok, 1)
                    dve.wait_ge(a_ok, b + 1)
                    nc.vector.tensor_tensor(thr[:], thr[:], acc[:], ALU.max).then_inc(t_ok, 1)
                dve.wait_ge(t_ok, BITS + 1)
                dve.wait_ge(cnt_ok, BITS)
                nc.vector.tensor_scalar(gt[:], pr[:], thr[:, 0:1], None, ALU.is_gt, ALU.add, accum_out=cnt[:, 0:1])\
                    .then_inc(fin, 1)
                nc.vector.tensor_scalar(eq[:], pr[:], thr[:, 0:1], None, ALU.is_equal, ALU.add, accum_out=cnt[:, 1:2])\
                    .then_inc(fin, 1)
                dve.wait_ge(fin, 2)
                nc.vector.tensor_tensor_scan(cg[:], onesw[:], gt[:], 0.0, ALU.mult, ALU.add).then_inc(ve, 1)
                nc.vector.tensor_tensor_scan(ce[:], onesw[:], eq[:], 0.0, ALU.mult, ALU.add).then_inc(ve, 1)
                dve.wait_ge(ofs, 1)
                nc.vector.tensor_copy(base[:, 0:3], pc2[:, 0:3]).then_inc(ve, 1)
                dve.wait_ge(ve, 3)
                nc.vector.tensor_scalar(cg[:], cg[:], base[:, 0:1], None, ALU.add).then_inc(ve, 1)
                nc.vector.tensor_scalar(ce[:], ce[:], base[:, 1:2], base[:, 2:3], ALU.add, ALU.add).then_inc(ve, 1)
                dve.wait_ge(ve, 5)
                nc.vector.tensor_tensor(cg[:], cg[:], gt[:], ALU.mult).then_inc(ve, 1)
                nc.vector.scalar_tensor_tensor(eq[:], ce[:], float(CAP), eq[:], ALU.is_le, ALU.mult).then_inc(ve, 1)
                dve.wait_ge(ve, 7)
                nc.vector.tensor_tensor(ce[:], ce[:], eq[:], ALU.mult).then_inc(ve, 1)
                nc.vector.tensor_tensor(gt[:], gt[:], eq[:], ALU.add).then_inc(ve, 1)
                dve.wait_ge(ve, 9)
                nc.vector.tensor_scalar(gt[:], gt[:], -(NOT_A_SLOT + 1.0), NOT_A_SLOT, ALU.mult, ALU.add).then_inc(ve, 1)
                nc.vector.tensor_tensor(cg[:], cg[:], ce[:], ALU.add).then_inc(ve, 1)
                dve.wait_ge(ve, 11)
                nc.vector.tensor_tensor(slot[:], cg[:], gt[:], ALU.add).then_inc(slo, 1)
                dve.wait_ge(trp, 1)
                for half in range(2):
                    nc.vector.tensor_copy(sT[:, :, :, half], ptr[:, half, :].rearrange("p (e c) -> p e c", c=NCK))\
                        .then_inc(ve, 1)
                dve.wait_ge(ve, 13)
                nc.vector.tensor_scalar(hi[:], sT[:], float(P), None, ALU.is_ge).then_inc(ve, 1)
                dve.wait_ge(ve, 14)
                nc.vector.scalar_tensor_tensor(K["place"][:], hi[:].rearrange("p e c h -> p e (c h)"), -float(P),
                                               sT[:].rearrange("p e c h -> p e (c h)"), ALU.mult, ALU.add).then_inc(ve, 1)
                hv = hi[:].rearrange("p e c h -> p e (c h)")
                tv = tcol[:].rearrange("p c h -> p (c h)").unsqueeze(1).broadcast_to([P, NE, NT])
                nc.vector.tensor_scalar(R[:, :, :, 2], hv, pcol[:, 0:1], None, ALU.mult).then_inc(ve, 1)
                nc.vector.tensor_tensor(R[:, :, :, 3], hv, tv, ALU.mult).then_inc(ve, 1)
                dve.wait_ge(ve, 17)
                nc.vector.tensor_scalar(R[:, :, :, 0], R[:, :, :, 2], -1.0, pcol[:, 0:1], ALU.mult, ALU.add).then_inc(ve, 1)
                nc.vector.scalar_tensor_tensor(R[:, :, :, 1], R[:, :, :, 3], -1.0, tv, ALU.mult, ALU.add).then_inc(ve, 1)

            @block.tensor
            def _(pe):
                pe.wait_ge(cst, 7)
                for b in range(BITS):
                    pe.wait_ge(cnt_ok, b + 1)
                    nc.tensor.matmul(pc[:, b % 2:b % 2 + 1], same[:], cnt[:, b % 2:b % 2 + 1], start=True,
                                     stop=True).then_inc(tot, 1)
                pe.wait_ge(fin, 2)
                nc.tensor.matmul(pc2[:, 0:2], before[:], cnt[:], start=True, stop=True)
                nc.tensor.matmul(pc2[:, 2:3], same[:], cnt[:, 0:1], start=True, stop=True).then_inc(ofs, 1)
                pe.wait_ge(slo, 1)
                for half in range(2):
                    last = nc.tensor.transpose(ptr[:, half, :], slot[:, half * P:(half + 1) * P], K["ident"][:])
                last.then_inc(trp, 1)


def moe_stage(nc, K, I, scr):
    FH = SEG
    NB = 6
    NS = 3
    HALVES = 2 * NB
    HEAD_START = 6
    KH = KD // 2
    with nc.cleanup_on_exit(), ExitStack() as ctx:
        m = Mem(nc, ctx)
        wst = m.sb("mwst", [P, NS, KD, FH])
        whi = m.sb("mwhi", [P, NB, KD, FH], BF16)
        wlo = m.sb("mwlo", [P, NB, KD, FH], BF16)
        rows32 = m.sb("mrows", [P, 2, ROWW], I32)
        rows = rows32[:].bitcast(BF16)
        probs = rows32[:].bitcast(F32)
        xhi = m.sb("xhi", [P, KD, CAP], BF16)
        xlo = m.sb("xlo", [P, KD, CAP], BF16)
        thb = m.sb("thb", [P, 2, CAP])
        hb = m.sb("hb", [P, 2, CAP])
        fhi = m.sb("fhi", [P, KD, CAP], BF16)
        flo = m.sb("flo", [P, KD, CAP], BF16)
        ysb = m.sb("ysb", [P, 2, D])
        g2 = m.sb("g2", [P, D])
        oneh = m.sb("oneh", [P, NT, P], BF16)
        Re = m.sb("Re", [P, NT, 4], BF16)
        iot = m.sb("iot", [P, P])
        idf = m.sb("idf", [P, 4])
        idn = m.sb("idn", [P, 2], I32)
        idc = m.sb("idc", [P, 2], I32)
        gate = m.sb("gate", [P, 2])
        pflag = m.sb("mpflag", [1, 1])
        pgu = [m.ps(f"pgu{i}", [P, 2, CAP]) for i in range(2)]
        pd = [m.ps(f"pd{i}", [P, SEG]) for i in range(2)]
        pid = m.ps("pid", [P, SEG])[:, 0:4]
        ptx = [m.ps(f"ptx{i}", [P, 4, CAP], BF16) for i in range(2)]

        g2_in, iot_ok, fl_ok = m.sem("g2_in"), m.sem("iot_ok"), m.sem("fl_ok")
        w_in, w_hi, w_lo = m.sems("mw_in", NS), m.sem("mw_hi"), m.sems("mw_lo", NS)
        oh_ok, id_ps, idf_ok, id_ok, idc_ok, gt_ok = (m.sem("oh_ok"), m.sem("id_ps"), m.sem("idf_ok"), m.sem("id_ok"),
                                                      m.sem("idc_ok"), m.sem("gt_ok"))
        got, tx_ps, tx_ok = m.sem("got"), m.sem("tx_ps"), m.sem("tx_ok")
        gu_ps, mth_ok, sg_ok, hid_ok, fhi_ok, flo_ok = (m.sem("gu_ps"), m.sem("mth_ok"), m.sem("msg_ok"), m.sem("hid_ok"),
                                                        m.sem("fhi_ok"), m.sem("flo_ok"))
        d_ps, y_ok, put = m.sem("d_ps"), m.sem("my_ok"), m.sem("put")
        mats = [I["w_gate"], I["w_up"], I["w_gate"], I["w_up"], I["w_down"], I["w_down"]]
        half_of = [0, 0, 1, 1, 0, 1]

        def experts(engine, prep, body):
            prep(0)
            peeled(engine, NE - 1, lambda e: body(e, True))
            body(NE - 1, False)

        with nc.Block() as block:
            @block.sync
            def _(sp):
                def one(e):
                    for b in range(NB):
                        wait(sp, w_lo[b % NS], 2 * (e * 2 + b // NS))
                        src = mats[b][0, bass.ds(e, 1), :, :].rearrange("e (k p) n -> p (e k) n", p=P)
                        sp.dma_start(wst[:, b % NS], src[:, :, half_of[b] * FH:(half_of[b] + 1) * FH])\
                            .then_inc(w_in[b % NS], 16)
                peeled(sp, NE, one)

            @block.gpsimd
            def _(pool):
                pool.dma_start(g2[:], scr["modrows"][6:8, :].rearrange("a n -> (a n)").partition_broadcast(P))\
                    .then_inc(g2_in, 16)
                nc.gpsimd.memset(pflag[:], 0.0).then_inc(fl_ok, 1)
                wait(pool, fl_ok, 1)
                nc.gpsimd.iota(iot[:], [[1, P]], base=0, channel_multiplier=0,
                               allow_small_or_imprecise_dtypes=True).then_inc(iot_ok, 1)

                def carrier():
                    nc.gpsimd.tensor_tensor(pflag[:], pflag[:], pflag[:], ALU.mult).then_inc(fl_ok, 1)

                def prep(e, first=False):
                    wait(pool, fl_ok, 1 if first else e * 3 - 1)
                    wait(pool, id_ok, e + 1)
                    wait(pool, tx_ps, e * 4)
                    wait(pool, gt_ok, e)
                    carrier()
                    for s in range(2):
                        pool.indirect_dma_start(out=rows32[:, s, :], out_offset=None, in_=scr["rows"],
                                                in_offset=bass.IndirectOffsetOnAxis(ap=idn[:, s:s + 1], axis=0))\
                            .then_inc(got, 16)

                def body(e, nxt):
                    if nxt:
                        prep(e + 1)
                    wait(pool, put, e * 32)
                    for s in range(2):
                        wait(pool, y_ok, e * 4 + 2 * s + 2)
                        wait(pool, fl_ok, e * 3 + s + (3 if nxt else 2))
                        carrier()
                        pool.indirect_dma_start(out=scr["y"], out_offset=bass.IndirectOffsetOnAxis(ap=idc[:, s:s + 1], axis=0),
                                                in_=ysb[:, s, :], in_offset=None, compute_op=ALU.add).then_inc(put, 16)

                experts(pool, lambda e: prep(e, True), body)
                wait(pool, put, NE * 32)

            @block.scalar
            def _(act):
                def turn(e, j):
                    wait(act, tx_ps, e * 4 + 2 * j + 1)
                    wait(act, gu_ps, e * 8)
                    nc.scalar.activation(xhi[:, 4 * j:4 * j + 4, :], ptx[0][:], ACT.Copy).then_inc(tx_ok, 1)

                def split(e, r):
                    e, b, ks = e + r // HALVES, r % HALVES // 2, slice(r % 2 * KH, (r % 2 + 1) * KH)
                    wait(act, w_in[b % NS], e * 32 + 16 * (b // NS) + 16)
                    if b < 2:
                        if not (isinstance(e, int) and e == 0):
                            wait(act, gu_ps, e * 8 - 4)
                    elif b < 4:
                        wait(act, gu_ps, e * 8)
                    else:
                        wait(act, d_ps, e * 4)
                    nc.scalar.activation(whi[:, b, ks], wst[:, b % NS, ks], ACT.Copy).then_inc(w_hi, 1)

                def hidden(e, j, nxt):
                    wait(act, gu_ps, e * 8 + j + 1)
                    if j < 2:
                        wait(act, sg_ok, e * 8)
                    else:
                        wait(act, sg_ok, e * 8 + j - 1)
                    nc.scalar.activation(thb[:, j % 2], pgu[j % 2][:, 0, :], ACT.Tanh, scale=0.5).then_inc(mth_ok, 1)
                    if nxt or HEAD_START + j < HALVES:
                        split(e, HEAD_START + j)
                    wait(act, hid_ok, e * 8 + j + 1)
                    wait(act, d_ps, e * 4)
                    nc.scalar.activation(fhi[:, j, :], hb[:, j % 2], ACT.Copy).then_inc(fhi_ok, 1)

                def body(e, nxt):
                    for j in range(8):
                        hidden(e, j, nxt)
                    if nxt:
                        for q in range(4):
                            if q < 2:
                                turn(e + 1, q)
                            split(e, HEAD_START + 8 + q)

                def prep0(e):
                    for r in range(HEAD_START):
                        split(0, r)
                    turn(0, 0)
                    turn(0, 1)

                experts(act, prep0, body)

            @block.vector
            def _(dve):
                wait(dve, iot_ok, 1)
                wait(dve, g2_in, 16)

                def token_list(e):
                    wait(dve, id_ps, e)
                    nc.vector.tensor_tensor(oneh[:], iot[:].unsqueeze(1).broadcast_to([P, NT, P]),
                                            K["place"][:, bass.ds(e, 1), :].rearrange("p e t -> p (e t)").unsqueeze(2)
                                            .broadcast_to([P, NT, P]), ALU.is_equal).then_inc(oh_ok, 1)
                    nc.vector.tensor_copy(Re[:], K["R"][:, bass.ds(e, 1), :, :].rearrange("p e t j -> p (e t) j"))\
                        .then_inc(oh_ok, 1)

                def numbers(e):
                    wait(dve, id_ps, e + 1)
                    nc.vector.tensor_copy(idf[:], pid).then_inc(idf_ok, 1)
                    wait(dve, idf_ok, e + 1)
                    wait(dve, got, e * 32)
                    wait(dve, idc_ok, e)
                    f2 = idf[:].rearrange("p (s a) -> p s a", a=2)
                    nc.vector.scalar_tensor_tensor(idn[:], f2[:, :, 1], float(P), f2[:, :, 0], ALU.mult, ALU.add)\
                        .then_inc(id_ok, 1)

                def turn(e, j):
                    wait(dve, tx_ps, e * 4 + 2 * j + 2)
                    wait(dve, gu_ps, e * 8)
                    nc.vector.tensor_copy(xlo[:, 4 * j:4 * j + 4, :], ptx[1][:]).then_inc(tx_ok, 1)

                def split(e, r):
                    e, b, ks = e + r // HALVES, r % HALVES // 2, slice(r % 2 * KH, (r % 2 + 1) * KH)
                    wait(dve, w_hi, e * HALVES + r % HALVES + 1)
                    nc.vector.tensor_tensor(wlo[:, b, ks], wst[:, b % NS, ks], whi[:, b, ks], ALU.subtract)\
                        .then_inc(w_lo[b % NS], 1)

                def hidden(e, j, nxt):
                    p = j % 2
                    wait(dve, mth_ok, e * 8 + j + 1)
                    if j < 2:
                        wait(dve, flo_ok, e * 8)
                    else:
                        wait(dve, flo_ok, e * 8 + j - 1)
                    nc.vector.scalar_tensor_tensor(thb[:, p], thb[:, p], 1.0, pgu[p][:, 0, :], ALU.add, ALU.mult)\
                        .then_inc(sg_ok, 1)
                    wait(dve, sg_ok, e * 8 + j + 1)
                    nc.vector.tensor_tensor(hb[:, p], thb[:, p], pgu[p][:, 1, :], ALU.mult).then_inc(hid_ok, 1)
                    if nxt or HEAD_START - 1 + j < HALVES:
                        split(e, HEAD_START - 1 + j)
                    wait(dve, hid_ok, e * 8 + j + 1)
                    wait(dve, fhi_ok, e * 8 + j + 1)
                    nc.vector.tensor_tensor(flo[:, j, :], hb[:, p], fhi[:, j, :], ALU.subtract).then_inc(flo_ok, 1)

                def weigh(e, s, c):
                    q = 2 * s + c
                    wait(dve, d_ps, e * 4 + q + 1)
                    wait(dve, put, e * 32)
                    nc.vector.scalar_tensor_tensor(ysb[:, s, c * SEG:(c + 1) * SEG], pd[q % 2][:], gate[:, s:s + 1],
                                                   g2[:, c * SEG:(c + 1) * SEG], ALU.mult, ALU.mult).then_inc(y_ok, 1)

                def body(e, nxt):
                    wait(dve, got, e * 32 + 32)
                    wait(dve, y_ok, e * 4)
                    nc.vector.tensor_scalar(gate[:], probs[:, :, bass.ds(e + D, 1)]
                                            .rearrange("p s a -> p (s a)"), 0.5, None, ALU.mult).then_inc(gt_ok, 1)
                    for j in range(8):
                        hidden(e, j, nxt)
                        if j == 0 and nxt:
                            token_list(e + 1)
                        if j == 2:
                            wait(dve, put, e * 32)
                            nc.vector.tensor_copy(idc[:], idn[:]).then_inc(idc_ok, 1)
                            if nxt:
                                numbers(e + 1)
                    wait(dve, gt_ok, e + 1)
                    for q in range(4):
                        if nxt:
                            if q < 2:
                                turn(e + 1, q)
                            split(e, HEAD_START - 1 + 8 + q)
                        weigh(e, q // 2, q % 2)

                def prep0(e):
                    token_list(0)
                    numbers(0)
                    for r in range(HEAD_START - 1):
                        split(0, r)
                    turn(0, 0)
                    turn(0, 1)

                experts(dve, prep0, body)

            @block.tensor
            def _(pe):
                def token_list(e):
                    wait(pe, oh_ok, e * 2 + 2)
                    wait(pe, idf_ok, e)
                    for t in range(NT):
                        last = nc.tensor.matmul(pid, oneh[:, t, :], Re[:, t, :], start=(t == 0), stop=(t == NT - 1))
                    last.then_inc(id_ps, 1)

                def turn(e, j):
                    wait(pe, got, e * 32 + 32)
                    wait(pe, tx_ok, e * 4 + 2 * j)
                    for part in range(2):
                        for k in range(4):
                            for s in range(2):
                                c = part * D + (4 * j + k) * P
                                last = nc.tensor.transpose(ptx[part][:, k, s * P:(s + 1) * P], rows[:, s, c:c + P],
                                                           K["identb"][:])
                        last.then_inc(tx_ps, 1)

                def body(e, nxt):
                    wait(pe, tx_ok, e * 4 + 4)
                    for f in range(8):
                        h, jj = f // 4, f % 4
                        if jj == 0:
                            for b in (2 * h, 2 * h + 1):
                                wait(pe, w_lo[b % NS], 2 * (e * 2 + b // NS + 1))
                        if f < 2:
                            wait(pe, hid_ok, e * 8)
                        else:
                            wait(pe, hid_ok, e * 8 + f - 1)
                        for part in range(2):
                            b = 2 * h + part
                            last = triple(nc, pgu[f % 2][:, part, :], [
                                (whi[:, b, k, jj * P:(jj + 1) * P], wlo[:, b, k, jj * P:(jj + 1) * P], xhi[:, k, :],
                                 xlo[:, k, :]) for k in range(KD)])
                        last.then_inc(gu_ps, 1)
                        if nxt and f == 2:
                            token_list(e + 1)
                        if nxt and f == 6:
                            turn(e + 1, 0)
                    wait(pe, flo_ok, e * 8 + 7)
                    for b in (4, 5):
                        wait(pe, w_lo[b % NS], 2 * (e * 2 + b // NS + 1))
                    for q in range(4):
                        s, c = q // 2, q % 2
                        wait(pe, y_ok, e * 4 + max(0, q - 1))
                        for k in range(KD):
                            if q == 0 and k == KD - 1:
                                wait(pe, flo_ok, e * 8 + 8)
                            fh, fl = fhi[:, k, s * P:(s + 1) * P], flo[:, k, s * P:(s + 1) * P]
                            nc.tensor.matmul(pd[q % 2][:], fh, whi[:, 4 + c, k, :], start=(k == 0), stop=False)
                            nc.tensor.matmul(pd[q % 2][:], fh, wlo[:, 4 + c, k, :], start=False, stop=False)
                            last = nc.tensor.matmul(pd[q % 2][:], fl, whi[:, 4 + c, k, :], start=False,
                                                    stop=(k == KD - 1))
                        last.then_inc(d_ps, 1)
                        if nxt and q == 0:
                            turn(e + 1, 1)

                def prep0(e):
                    token_list(0)
                    turn(0, 0)
                    turn(0, 1)

                experts(pe, prep0, body)


def finish_stage(nc, K, I, scr, out):
    with nc.cleanup_on_exit(), ExitStack() as ctx:
        m = Mem(nc, ctx)
        NBUF = 4
        yt = m.sb("yt", [P, NBUF, D])
        junk = m.sb("fjunk", [P, D])
        fg = m.sb("fg", [P, D])
        st = m.sb("fst", [P, NBUF, 4])
        fg_in, y_in, y_out = m.sem("fg_in"), m.sems("fy_in", NBUF), m.sems("fy_out", NBUF)
        ss, sd, rs, ok = m.sem("fss"), m.sem("fsd"), m.sem("frs"), m.sem("fok")
        with nc.Block() as block:
            @block.sync
            def _(sp):
                sp.dma_start(fg[:], I["final_g"].partition_broadcast(P)).then_inc(fg_in, 16)
                def one(i):
                    for b in range(NBUF):
                        wait(sp, y_out[b], i * 16)
                        sp.dma_start(yt[:, b], scr["y"][bass.ds((i * NBUF + b) * P, P), :]).then_inc(y_in[b], 16)
                peeled(sp, NT // NBUF, one)

            @block.gpsimd
            def _(pool):
                def one(i):
                    for b in range(NBUF):
                        wait(pool, ok, i * NBUF + b + 1)
                        pool.dma_start(out[0, bass.ds((i * NBUF + b) * P, P), :], yt[:, b]).then_inc(y_out[b], 16)
                peeled(pool, NT // NBUF, one)
                for b in range(NBUF):
                    wait(pool, y_out[b], 16 * NT // NBUF)

            @block.scalar
            def _(act):
                def one(i):
                    for b in range(NBUF):
                        wait(act, y_in[b], i * 16 + 16)
                        nc.scalar.activation(junk[:], yt[:, b], ACT.Square, accum_out=st[:, b, 0:1]).then_inc(ss, 1)
                        wait(act, ss, i * NBUF + b + 1)
                        nc.scalar.activation(st[:, b, 1:2], st[:, b, 0:1], ACT.Sqrt, bias=K["eps"][:, 0:1], scale=1.0 / D)\
                            .then_inc(sd, 1)
                peeled(act, NT // NBUF, one)

            @block.vector
            def _(dve):
                wait(dve, fg_in, 16)
                def one(i):
                    for b in range(NBUF):
                        wait(dve, sd, i * NBUF + b + 1)
                        nc.vector.reciprocal(st[:, b, 2:3], st[:, b, 1:2]).then_inc(rs, 1)
                        wait(dve, rs, i * NBUF + b + 1)
                        nc.vector.scalar_tensor_tensor(yt[:, b], yt[:, b], st[:, b, 2:3], fg[:], ALU.mult, ALU.mult)\
                            .then_inc(ok, 1)
                peeled(dve, NT // NBUF, one)


def build(nc, I, out, debug=False):
    kind = "ExternalOutput" if debug else "Internal"
    scr = {
        "modrows": nc.dram_tensor("s_modrows", [8, SEG], F32, kind=kind).ap(),
        "mixed": nc.dram_tensor("s_mixed", [NT, P, 2, KD, P], BF16, kind=kind).ap(),
        "rows": nc.dram_tensor("s_rows", [T, ROWW], I32, kind=kind).ap(),
        "pT": nc.dram_tensor("s_pT", [NE, T], F32, kind=kind).ap(),
        "y": nc.dram_tensor("s_y", [T, D], F32, kind=kind).ap(),
    }
    with ExitStack() as whole:
        m = Mem(nc, whole)
        K = {"ident": m.sb("ident", [P, P]), "identb": m.sb("identb", [P, P], BF16), "ones": m.sb("ones", [P, P]),
             "mean_cw": m.sb("mean_cw", [P, P]), "mean_p": m.sb("mean_p", [P, P]), "eps": m.sb("eps", [P, 1]),
             "const_ok": m.sem("const_ok"), "n_const": 8}
        with nc.Block() as block:
            @block.gpsimd
            def _(pool):
                for t, val in (("ident", 0.0), ("identb", 0.0), ("ones", 1.0), ("mean_cw", 1.0 / CW),
                               ("mean_p", 1.0 / P), ("eps", EPS)):
                    nc.gpsimd.memset(K[t][:], val).then_inc(K["const_ok"], 1)
                wait(pool, K["const_ok"], 6)
                for t in ("ident", "identb"):
                    nc.gpsimd.affine_select(out=K[t][:], in_=K[t][:], compare_op=ALU.not_equal, fill=1.0, base=0,
                                            pattern=[[-1, P]], channel_multiplier=1).then_inc(K["const_ok"], 1)
        with ExitStack() as mixer:
            mm = Mem(nc, mixer)
            K["hhi"] = mm.sb("hhi", [P, KD, TC + T], BF16)
            K["hlo"] = mm.sb("hlo", [P, KD, TC + T], BF16)
            modulate_stage(nc, K, I, scr)
            conv_stage(nc, K, I, scr)
            heads_stage(nc, K, I, scr)
        outproj_stage(nc, K, I, scr)
        K["place"] = m.sb("place", [P, NE, NT])
        K["R"] = m.sb("R", [P, NE, NT, 4], BF16)
        topk_stage(nc, K, I, scr)
        moe_stage(nc, K, I, scr)
        finish_stage(nc, K, I, scr, out)


_INS = ["x", "c", "ctx", "c_ctx", "ada_w", "ada_b", "norm1_g", "w_in", "conv_taps", "conv_bias", "conv_ln_g",
        "conv_ln_b", "hgrn_lb_logits", "hgrn_norm_g", "w_out", "norm2_g", "router_w", "w_gate", "w_up", "w_down",
        "final_g"]
DEBUG = False


def kernel(**inputs):
    import numpy as np
    import concourse.bacc as bacc
    from concourse.bass_utils import run_bass_kernel_spmd as run

    nc = bacc.Bacc("TRN2", target_bir_lowering=False, num_devices=1)
    arrays, aps = {}, {}
    for name in _INS:
        a = np.ascontiguousarray(inputs[name])
        arrays[f"in_{name}"] = a
        aps[name] = nc.dram_tensor(f"in_{name}", a.shape, mybir.dt.from_np(a.dtype), kind="ExternalInput").ap()
    o = nc.dram_tensor("out_0", (1, T, D), F32, kind="ExternalOutput").ap()
    build(nc, aps, o, debug=DEBUG)
    r = run(nc, [arrays], core_ids=[0])
    return r.results[0]["out_0"]
```

```python
from contextlib import ExitStack

import concourse.bass as bass
from concourse import mybir

F32 = mybir.dt.float32
BF16 = mybir.dt.bfloat16
I32 = mybir.dt.int32
U32 = mybir.dt.uint32
ACT = mybir.ActivationFunctionType
ALU = mybir.AluOpType
AX = mybir.AxisListType

P = 128
D = 1024
KD = D // P
T = 2048
TC = 256
NT = T // P
SEG = 512
NSEG = T // SEG
CW = 512
NCT = CW // P
HEADS = 4
TAPS = 31
PAD = (TAPS - 1) // 2
GW = 64
GH = T // GW
CH = 32
NE = 16
CAP = 2 * T // NE
EPS = 1e-6
COL_A, COL_B, COL_Q, COL_I, COL_FF, COL_FB, COL_G = [512 * j for j in range(7)]
ROWW = D + NE
NOT_A_SLOT = 1000.0


class Mem:

    def __init__(self, nc, ctx):
        self.nc, self.ctx = nc, ctx

    def sb(self, name, shape, dt=F32):
        return self.ctx.enter_context(self.nc.sbuf_tensor(name, shape, dt))

    def ps(self, name, shape, dt=F32):
        return self.ctx.enter_context(self.nc.psum_tensor(name, shape, dt))

    def sem(self, name):
        return self.nc.alloc_semaphore(name)

    def sems(self, name, n):
        return [self.sem(f"{name}{i}") for i in range(n)]


def wait(engine, sem, value):
    if not (isinstance(value, int) and value <= 0):
        engine.wait_ge(sem, value)


def peeled(engine, n, one):
    one(0)
    with engine.Fori(1, n) as i:
        one(i)


def triple(nc, out, pairs):
    n = len(pairs)
    for k, (lh, ll, rh, rl) in enumerate(pairs):
        nc.tensor.matmul(out, lh, rh, start=(k == 0), stop=False)
        nc.tensor.matmul(out, lh, rl, start=False, stop=False)
        last = nc.tensor.matmul(out, ll, rh, start=False, stop=(k == n - 1))
    return last


def modulate_stage(nc, K, I, scr):
    NCH = 12
    groups = [(0, 2)] + [(2 + 4 * s, 4) for s in range(NSEG)]
    with nc.cleanup_on_exit(), ExitStack() as ctx:
        m = Mem(nc, ctx)
        cc = m.sb("cc", [P, 2, KD])
        cth = m.sb("cth", [P, 2, KD])
        csil = m.sb("csil", [P, 2, KD])
        crep = m.sb("crep", [P, KD, P])
        cmix = m.sb("cmix", [P, KD, P])
        ada = m.sb("ada", [P, 2, KD, SEG])
        adab = m.sb("adab", [1, 2, SEG])
        modrow = m.sb("modrow", [P, 2 * D])
        modc = m.sb("modc", [P, 2 * KD, 2])
        n1c = m.sb("n1c", [P, KD])
        A1 = m.sb("A1", [P, KD, 2])
        n2r = m.sb("n2r", [P, D])
        rows = m.sb("rows", [P, 2, SEG])
        xb = m.sb("xb", [P, 2, 4, D])
        junk = m.sb("junk", [P, D])
        ss = m.sb("ss", [P, 5, 4])
        rstd = m.sb("rstd", [P, 5, 4])
        hf = m.sb("hf", [P, 2, SEG])
        pm = [m.ps(f"pm{i}", [P, SEG]) for i in range(2)]
        pt = [m.ps(f"pt{i}", [P, SEG]) for i in range(4)]

        c_in, col_in, n2_in = m.sem("c_in"), m.sem("col_in"), m.sem("n2_in")
        ada_in, x_in = m.sems("ada_in", 2), m.sems("x_in", 2)
        c_th, c_sil, c_rep = m.sem("c_th"), m.sem("c_sil"), m.sem("c_rep")
        mod_ps, mod_sb, modc_ps, modc_sb = m.sem("mod_ps"), m.sem("mod_sb"), m.sem("modc_ps"), m.sem("modc_sb")
        row_out = m.sems("row_out", 2)
        a1_ok, ss_ok, std_ok, rstd_ok, xn_ok = m.sem("a1_ok"), m.sem("ss_ok"), m.sem("std_ok"), m.sem("rstd_ok"), m.sem("xn_ok")
        tp_ps, hi_ok, hf_ok, lo_ok = m.sem("tp_ps"), m.sem("hi_ok"), m.sem("hf_ok"), m.sem("lo_ok")

        ada_v = I["ada_w"][0].rearrange("(p k) e -> p k e", k=KD)
        def chunks_with(g):
            return [] if g == 0 else [2 + 2 * g, 3 + 2 * g]

        with nc.Block() as block:
            @block.sync
            def _(sp):
                sp.dma_start(cc[:, 0, :], I["c"].rearrange("a (p k) -> (a p) k", k=KD)).then_inc(c_in, 16)
                sp.dma_start(cc[:, 1, :], I["c_ctx"].rearrange("(p k) -> p k", k=KD)).then_inc(c_in, 16)

                def load_ada(n):
                    if n >= 2:
                        sp.wait_ge(mod_ps, n - 1)
                    sp.dma_start(ada[:, n % 2], ada_v[:, :, n * SEG:(n + 1) * SEG]).then_inc(ada_in[n % 2], 16)
                    sp.dma_start(adab[:, n % 2], I["ada_b"][:, n * SEG:(n + 1) * SEG]).then_inc(ada_in[n % 2], 16)

                def load_x(g):
                    t0, n = groups[g]
                    src = I["ctx"][0] if g == 0 else I["x"][0, (t0 - 2) * P:(t0 - 2 + n) * P, :]
                    if g >= 2:
                        sp.wait_ge(tp_ps, KD * (g - 1))
                    sp.dma_start(xb[:, g % 2, 0:n, :], src.rearrange("(n p) d -> p n d", p=P)).then_inc(x_in[g % 2], 16)

                load_ada(0)
                load_ada(1)
                load_x(0)
                load_x(1)
                load_ada(2)
                load_ada(3)
                for g in range(1, 5):
                    for n in chunks_with(g):
                        load_ada(n)
                    if g + 1 < 5:
                        load_x(g + 1)

            @block.gpsimd
            def _(pool):
                with nc.allow_non_contiguous_dma(reason="1024 single norm weights into columns"):
                    pool.dma_start(n1c[:], I["norm1_g"][0].rearrange("(k p) -> p k", p=P)).then_inc(col_in, 16)
                pool.dma_start(n2r[:], I["norm2_g"][0].partition_broadcast(P)).then_inc(n2_in, 16)
                for n in range(4, NCH):
                    pool.wait_ge(mod_sb, n + 1)
                    pool.dma_start(scr["modrows"][n - 4:n - 3, :], rows[0:1, n % 2, :]).then_inc(row_out[n % 2], 16)
                for s in range(2):
                    pool.wait_ge(row_out[s], 16 * (NCH - 4) // 2)

            @block.scalar
            def _(act):
                act.wait_ge(c_in, 32)
                nc.scalar.activation(cth[:], cc[:], ACT.Tanh, scale=0.5).then_inc(c_th, 1)

                def square(g, j):
                    t0, n = groups[g]
                    if j == 0:
                        act.wait_ge(x_in[g % 2], 16 * (g // 2 + 1))
                    if t0 + j:
                        act.wait_ge(ss_ok, t0 + j)
                    nc.scalar.activation(junk[:], xb[:, g % 2, j, :], ACT.Square, accum_out=ss[:, g, j:j + 1])\
                        .then_inc(ss_ok, 1)
                    if j == n - 1:
                        act.wait_ge(ss_ok, t0 + n)
                        act.wait_ge(K["const_ok"], K["n_const"])
                        nc.scalar.activation(ss[:, g, 0:n], ss[:, g, 0:n], ACT.Sqrt, bias=K["eps"][:, 0:1],
                                             scale=1.0 / D).then_inc(std_ok, 1)

                for j in range(groups[0][1]):
                    square(0, j)
                for g, (t0, n) in enumerate(groups):
                    if g == 0:
                        act.wait_ge(a1_ok, 1)
                    s = 0 if g else 1
                    for k in range(KD):
                        q = g * KD + k
                        act.wait_ge(tp_ps, q + 1)
                        nc.scalar.activation(K["hhi"][:, k, t0 * P:(t0 + n) * P], pt[q % 4][:, 0:n * P], ACT.Identity,
                                             bias=modc[:, k, s:s + 1], scale=A1[:, k, s:s + 1]).then_inc(hi_ok, 1)
                        if k < 4 and g + 1 < len(groups):
                            square(g + 1, k)

            @block.vector
            def _(dve):
                dve.wait_ge(c_th, 1)
                nc.vector.scalar_tensor_tensor(csil[:], cth[:], 1.0, cc[:], ALU.add, ALU.mult).then_inc(c_sil, 1)
                dve.wait_ge(c_sil, 1)
                nc.vector.tensor_scalar(crep[:], csil[:, 0, :].unsqueeze(2).broadcast_to([P, KD, P]), 0.5, None,
                                        ALU.mult).then_inc(c_rep, 1)
                for s in range(2):
                    nc.vector.tensor_scalar(cmix[:, :, 64 * s:64 * s + 64],
                                            csil[:, s, :].unsqueeze(2).broadcast_to([P, KD, 64]), 0.5, None,
                                            ALU.mult).then_inc(c_rep, 1)

                def mod_out(n):
                    dve.wait_ge(mod_ps, n + 1)
                    src = pm[n % 2][:]
                    if n < 4:
                        ins = nc.vector.tensor_copy(modrow[:, n * SEG:(n + 1) * SEG], src)
                    else:
                        if n >= 6:
                            dve.wait_ge(row_out[n % 2], 16 * ((n - 4) // 2))
                        if n in (8, 9):
                            dve.wait_ge(n2_in, 16)
                            ins = nc.vector.scalar_tensor_tensor(rows[:, n % 2, :], src, 1.0,
                                                                 n2r[:, (n - 8) * SEG:(n - 7) * SEG], ALU.add, ALU.mult)
                        else:
                            ins = nc.vector.tensor_copy(rows[:, n % 2, :], src)
                    ins.then_inc(mod_sb, 1)

                for n in range(4):
                    mod_out(n)
                for q in range(4):
                    dve.wait_ge(modc_ps, q + 1)
                    nc.vector.tensor_copy(modc[:, 4 * q:4 * q + 4, :],
                                          pt[q][:].rearrange("p (a s j) -> p a s j", a=4, s=2)[:, :, :, 0])\
                        .then_inc(modc_sb, 1)
                dve.wait_ge(modc_sb, 4)
                dve.wait_ge(col_in, 16)
                nc.vector.scalar_tensor_tensor(A1[:], modc[:, KD:2 * KD, :], 1.0,
                                               n1c[:].unsqueeze(2).broadcast_to([P, KD, 2]), ALU.add, ALU.mult)\
                    .then_inc(a1_ok, 1)
                dve.wait_ge(a1_ok, 1)

                def inverse(g):
                    n = groups[g][1]
                    dve.wait_ge(std_ok, g + 1)
                    nc.vector.reciprocal(rstd[:, g, 0:n], ss[:, g, 0:n]).then_inc(rstd_ok, 1)
                    dve.wait_ge(rstd_ok, g + 1)

                def normed(g, j):
                    nc.vector.tensor_scalar(xb[:, g % 2, j, :], xb[:, g % 2, j, :], rstd[:, g, j:j + 1], None,
                                            ALU.mult).then_inc(xn_ok, 1)

                inverse(0)
                for j in range(groups[0][1]):
                    normed(0, j)
                for g, (t0, n) in enumerate(groups):
                    s = 0 if g else 1
                    for k in range(KD):
                        q = g * KD + k
                        dve.wait_ge(hi_ok, q + 1)
                        nc.vector.tensor_scalar(hf[:, q % 2, 0:n * P], pt[q % 4][:, 0:n * P], A1[:, k, s:s + 1],
                                                modc[:, k, s:s + 1], ALU.mult, ALU.add).then_inc(hf_ok, 1)
                        dve.wait_ge(hf_ok, q + 1)
                        nc.vector.tensor_tensor(K["hlo"][:, k, t0 * P:(t0 + n) * P], hf[:, q % 2, 0:n * P],
                                                K["hhi"][:, k, t0 * P:(t0 + n) * P], ALU.subtract).then_inc(lo_ok, 1)
                        if k >= KD - 4 and g + 1 < len(groups):
                            if k == KD - 4:
                                inverse(g + 1)
                            normed(g + 1, k - (KD - 4))
                    for c in chunks_with(g):
                        mod_out(c)

            @block.tensor
            def _(pe):
                pe.wait_ge(K["const_ok"], K["n_const"])
                pe.wait_ge(c_rep, 3)

                def mod_mm(n, ks=range(KD)):
                    if 0 in ks:
                        pe.wait_ge(ada_in[n % 2], 32 * (n // 2 + 1))
                        if n >= 2:
                            pe.wait_ge(mod_sb, n - 1)
                    w = cmix if n < 4 else crep
                    for k in ks:
                        nc.tensor.matmul(pm[n % 2][:], w[:, k, :], ada[:, n % 2, k, :], start=(k == 0), stop=False)
                    if KD - 1 in ks:
                        nc.tensor.matmul(pm[n % 2][:], K["ones"][0:1, :], adab[0:1, n % 2, :], start=False,
                                         stop=True).then_inc(mod_ps, 1)

                for n in range(4):
                    mod_mm(n)
                pe.wait_ge(mod_sb, 4)
                for q in range(4):
                    for a in range(4):
                        j = 4 * q + a
                        last = nc.tensor.transpose(pt[q][:, a * P:(a + 1) * P], modrow[:, j * P:(j + 1) * P], K["ident"][:])
                    last.then_inc(modc_ps, 1)
                tiles = 0
                for g, (t0, n) in enumerate(groups):
                    tiles += n
                    pe.wait_ge(xn_ok, tiles)
                    for k in range(KD):
                        q = g * KD + k
                        if q >= 4:
                            pe.wait_ge(hf_ok, q - 3)
                        else:
                            pe.wait_ge(modc_sb, 4)
                        for j in range(n):
                            last = nc.tensor.transpose(pt[q % 4][:, j * P:(j + 1) * P],
                                                       xb[:, g % 2, j, k * P:(k + 1) * P], K["ident"][:])
                        last.then_inc(tp_ps, 1)
                        for c in chunks_with(g)[2 * k // KD:2 * k // KD + 1]:
                            first = 2 * k % KD
                            mod_mm(c, range(first, first + 2))


def conv_stage(nc, K, I, scr):
    SLAB = [(COL_A, 0), (COL_B, 1), (COL_A + P, 2), (COL_B + P, 3)]
    SLAB += [(COL_I + h * P, 4 + h) for h in range(HEADS)]
    SLAB += [(COL_A + 2 * P, 0), (COL_B + 2 * P, 1), (COL_A + 3 * P, 2), (COL_B + 3 * P, 3)]
    SLAB += [(COL_Q + h * P, h) for h in range(HEADS)] + [(COL_G + h * P, 4 + h) for h in range(HEADS)]
    JV = 2 + NT
    JOBS = JV + 2 * HEADS * NSEG
    WITH_U = 3 * NSEG
    WITH_TAPS = 17
    WITH_LN = 5
    with nc.cleanup_on_exit(), ExitStack() as ctx:
        m = Mem(nc, ctx)
        wst = m.sb("wst", [P, 4, KD, P])
        whi = m.sb("whi", [P, 8, KD, P], BF16)
        wlo = m.sb("wlo", [P, 8, KD, P], BF16)
        jb = m.sb("jb", [P, 2, SEG])
        th = m.sb("th", [P, 2, SEG])
        u = m.sb("u", [P, 2, T])
        co = m.sb("co", [P, NCT, T])
        taps = m.sb("taps", [P, NCT, TAPS])
        cb = m.sb("cb", [P, NCT])
        lg = m.sb("lg", [P, 2, NCT])
        sq = m.sb("sq", [P, 2, SEG])
        rs = m.sb("rs", [P, 2, SEG])
        y = m.sb("y", [P, 2, SEG])
        tl = m.sb("tl", [P, 2, SEG])
        mh = m.sb("mh", [P, 2, SEG], BF16)
        ml = m.sb("ml", [P, 2, SEG], BF16)
        pa = [m.ps(f"pa{i}", [P, SEG]) for i in range(2)]
        pb = [m.ps(f"pb{i}", [P, SEG]) for i in range(2)]
        pmu, pva = pa, pb
        pjob = [m.ps(f"pjob{i}", [P, SEG]) for i in range(4)]

        job_ps, job_ok, job_out = m.sem("job_ps"), m.sem("job_ok"), m.sems("job_out", 2)
        par_in, par_ok = m.sem("par_in"), m.sem("par_ok")
        w_in, w_hi, w_lo = m.sems("cw_in", 4), m.sem("cw_hi"), m.sem("cw_lo")
        ab_ps, b_th, u_ok, tap_ok = m.sem("ab_ps"), m.sem("b_th"), m.sem("u_ok"), m.sem("tap_ok")
        mu_ps, xc_ok, sq_ok, va_ps, sd_ok, rs_ok = (m.sem("mu_ps"), m.sem("xc_ok"), m.sem("sq_ok"), m.sem("va_ps"),
                                                    m.sem("sd_ok"), m.sem("rs_ok"))
        y_ok, yh_ok, t_ok, o_ok, mh_ok, ml_ok = (m.sem("y_ok"), m.sem("yh_ok"), m.sem("t_ok"), m.sem("o_ok"),
                                                 m.sem("mh_ok"), m.sem("ml_ok"))
        m_out = m.sems("m_out", 2)
        wv = I["w_in"][0].rearrange("(k p) n -> p k n", p=P)

        def ln_job(n, j):
            return WITH_U + WITH_TAPS + n * WITH_LN + j

        with nc.Block() as block:
            @block.sync
            def _(sp):
                for s, (col, _) in enumerate(SLAB):
                    if s >= 4:
                        sp.wait_ge(w_lo, s - 3)
                    sp.dma_start(wst[:, s % 4], wv[:, :, col:col + P]).then_inc(w_in[s % 4], 16)
                for n in range(NSEG):
                    for c in range(NCT):
                        q = n * NCT + c
                        sp.wait_ge(ml_ok, q + 1)
                        for part, buf in ((0, mh), (1, ml)):
                            dst = scr["mixed"][4 * n:4 * n + 4, :, part, c, :]
                            sp.dma_start(dst.rearrange("t p j -> p t j"),
                                         buf[:, q % 2, :].rearrange("p (t j) -> p t j", j=P)).then_inc(m_out[q % 2], 16)
                for s in range(2):
                    sp.wait_ge(m_out[s], 32 * (NSEG * NCT // 2))

            @block.gpsimd
            def _(pool):
                with nc.allow_non_contiguous_dma(reason="per-channel constants into columns"):
                    for c in range(NCT):
                        pool.dma_start(taps[:, c, :], I["conv_taps"][0, :, c * P:(c + 1) * P].rearrange("k p -> p k"))\
                            .then_inc(par_in, 16)
                    pool.dma_start(cb[:], I["conv_bias"][0].rearrange("(c p) -> p c", p=P)).then_inc(par_in, 16)
                    pool.dma_start(lg[:, 0, :], I["conv_ln_g"][0].rearrange("(c p) -> p c", p=P)).then_inc(par_in, 16)
                    pool.dma_start(lg[:, 1, :], I["conv_ln_b"][0].rearrange("(c p) -> p c", p=P)).then_inc(par_in, 16)
                for j in range(JOBS):
                    pool.wait_ge(job_ok, j + 1)
                    if j < JV:
                        dst = scr["v"][:, :, j, :].rearrange("h p d -> p h d")
                        src = jb[:, j % 2].rearrange("p (h d) -> p h d", h=HEADS)
                    else:
                        what, r = ("q", j - JV) if j < JV + HEADS * NSEG else ("g", j - JV - HEADS * NSEG)
                        dst = scr[what][r // NSEG, :, r % NSEG * SEG:(r % NSEG + 1) * SEG]
                        src = jb[:, j % 2]
                    pool.dma_start(dst, src).then_inc(job_out[j % 2], 16)
                for i in range(2):
                    pool.wait_ge(job_out[i], 16 * (JOBS // 2))

            @block.scalar
            def _(act):
                def w_split(s):
                    act.wait_ge(w_in[s % 4], 16 * (s // 4 + 1))
                    if 8 <= s < 12:
                        act.wait_ge(ab_ps, NSEG * ((s - 8) // 2 + 1))
                    elif 12 <= s < 16:
                        act.wait_ge(ab_ps, NSEG * NCT)
                    elif s >= 16:
                        act.wait_ge(job_ps, JV)
                    nc.scalar.activation(whi[:, SLAB[s][1]], wst[:, s % 4], ACT.Copy).then_inc(w_hi, 1)

                def job(j):
                    act.wait_ge(job_ps, j + 1)
                    if j >= 2:
                        act.wait_ge(job_out[j % 2], 16 * (j // 2))
                    nc.scalar.activation(jb[:, j % 2], pjob[j % 4][:], ACT.Copy).then_inc(job_ok, 1)

                for s in range(4):
                    w_split(s)
                for c in range(NCT):
                    for n in range(NSEG):
                        q = c * NSEG + n
                        act.wait_ge(ab_ps, q + 1)
                        if q >= 2:
                            act.wait_ge(u_ok, q - 1)
                        nc.scalar.activation(th[:, q % 2], pb[q % 2][:], ACT.Tanh, scale=0.5).then_inc(b_th, 1)
                        if c == 0:
                            w_split(4 + n)
                        else:
                            job(q - NSEG)
                    if c < 2:
                        w_split(8 + 2 * c)
                        w_split(9 + 2 * c)
                for j in range(WITH_U, WITH_U + WITH_TAPS):
                    job(j)
                    for s in {WITH_U: (12, 13, 14, 15), JV: (16, 17, 18, 19)}.get(j, ()):
                        w_split(s)
                for n in range(NSEG):
                    for c in range(NCT):
                        q = n * NCT + c
                        act.wait_ge(xc_ok, q + 1)
                        if q >= 2:
                            act.wait_ge(va_ps, q - 1)
                        nc.scalar.activation(sq[:, q % 2], co[:, c, n * SEG:(n + 1) * SEG], ACT.Square).then_inc(sq_ok, 1)
                        if c == 1 and n >= 1:
                            job(ln_job(n - 1, 4))
                        if c == 2:
                            job(ln_job(n, 0))
                    act.wait_ge(va_ps, NCT * (n + 1))
                    if n >= 2:
                        act.wait_ge(y_ok, NCT * (n - 1))
                    nc.scalar.activation(rs[:, n % 2], pva[n % 2][:], ACT.Sqrt, bias=K["eps"][:, 0:1]).then_inc(sd_ok, 1)
                    job(ln_job(n, 1))

                    def cast(q):
                        act.wait_ge(o_ok, q + 1)
                        if q >= 2:
                            act.wait_ge(m_out[q % 2], 32 * (q // 2))
                        nc.scalar.activation(mh[:, q % 2], y[:, q % 2], ACT.Copy).then_inc(mh_ok, 1)

                    for c in range(NCT):
                        q = n * NCT + c
                        act.wait_ge(y_ok, q + 1)
                        sl = co[:, c, n * SEG:(n + 1) * SEG]
                        if q >= 2:
                            act.wait_ge(ml_ok, q - 1)
                        nc.scalar.activation(y[:, q % 2], sl, ACT.Identity, bias=lg[:, 1, c:c + 1],
                                             scale=lg[:, 0, c:c + 1]).then_inc(yh_ok, 1)
                        act.wait_ge(yh_ok, q + 1)
                        nc.scalar.activation(tl[:, q % 2], y[:, q % 2], ACT.Tanh).then_inc(t_ok, 1)
                        if c >= 1:
                            cast(q - 1)
                    cast(n * NCT + NCT - 1)
                    job(ln_job(n, 2))
                    job(ln_job(n, 3))
                job(ln_job(NSEG - 1, 4))
                for j in range(ln_job(NSEG, 0), JOBS):
                    job(j)

            @block.vector
            def _(dve):
                def w_split(s):
                    dve.wait_ge(w_hi, s + 1)
                    w = SLAB[s][1]
                    nc.vector.tensor_tensor(wlo[:, w], wst[:, s % 4], whi[:, w], ALU.subtract).then_inc(w_lo, 1)

                for s in range(4):
                    w_split(s)
                dve.wait_ge(par_in, 16 * (NCT + 3))
                nc.vector.tensor_scalar(taps[:], taps[:], 0.5, None, ALU.mult).then_inc(par_ok, 1)
                nc.vector.tensor_scalar(lg[:], lg[:], 0.5, None, ALU.mult).then_inc(par_ok, 1)

                def gated(c, n):
                    q = c * NSEG + n
                    dve.wait_ge(b_th, q + 1)
                    nc.vector.scalar_tensor_tensor(u[:, c % 2, n * SEG:(n + 1) * SEG], th[:, q % 2], 1.0, pa[q % 2][:],
                                                   ALU.add, ALU.mult).then_inc(u_ok, 1)

                for n in range(NSEG):
                    gated(0, n)
                    w_split(4 + n)
                w_split(8)
                w_split(9)
                steps = 0
                for c in range(NCT):
                    dve.wait_ge(u_ok, NSEG * (c + 1))
                    dve.wait_ge(par_ok, 2)
                    acc, up = co[:, c, :], u[:, c % 2, :]
                    nc.vector.tensor_scalar(acc, up, taps[:, c, PAD:PAD + 1], cb[:, c:c + 1], ALU.mult, ALU.add)\
                        .then_inc(tap_ok, 1)
                    steps += 1
                    a3, u3 = acc.rearrange("p (r w) -> p r w", w=GW), up.rearrange("p (r w) -> p r w", w=GW)
                    for k in range(TAPS):
                        off = k - PAD
                        if off == 0:
                            continue
                        if c < NCT // 2:
                            lo, hi = max(0, -off), GW - max(0, off)
                            o, i = a3[:, :, lo:hi], u3[:, :, lo + off:hi + off]
                        else:
                            lo, hi = max(0, -off), GH - max(0, off)
                            o, i = acc[:, lo * GW:hi * GW], up[:, (lo + off) * GW:(hi + off) * GW]
                        dve.wait_ge(tap_ok, steps)
                        nc.vector.scalar_tensor_tensor(o, i, taps[:, c, k:k + 1], o, ALU.mult, ALU.add).then_inc(tap_ok, 1)
                        steps += 1
                        if k % 7 == 6:
                            n = k // 7
                            if c + 1 < NCT:
                                gated(c + 1, n)
                                if c == 0 and n == NSEG - 1:
                                    w_split(10)
                                    w_split(11)
                            else:
                                w_split(12 + 2 * n)
                                w_split(13 + 2 * n)
                dve.wait_ge(tap_ok, steps)

                def centre(n):
                    dve.wait_ge(mu_ps, n + 1)
                    for c in range(NCT):
                        sl = co[:, c, n * SEG:(n + 1) * SEG]
                        nc.vector.tensor_tensor(sl, sl, pmu[n % 2][:], ALU.subtract).then_inc(xc_ok, 1)

                centre(0)
                for n in range(NSEG):
                    if n + 1 < NSEG:
                        centre(n + 1)
                    dve.wait_ge(sd_ok, n + 1)
                    nc.vector.reciprocal(rs[:, n % 2], rs[:, n % 2]).then_inc(rs_ok, 1)
                    dve.wait_ge(rs_ok, n + 1)
                    for c in range(NCT):
                        sl = co[:, c, n * SEG:(n + 1) * SEG]
                        nc.vector.tensor_tensor(sl, sl, rs[:, n % 2], ALU.mult).then_inc(y_ok, 1)

                    def low(q):
                        dve.wait_ge(mh_ok, q + 1)
                        if q >= 2:
                            dve.wait_ge(m_out[q % 2], 32 * (q // 2))
                        nc.vector.tensor_tensor(ml[:, q % 2], y[:, q % 2], mh[:, q % 2], ALU.subtract).then_inc(ml_ok, 1)

                    for c in range(NCT):
                        q = n * NCT + c
                        dve.wait_ge(t_ok, q + 1)
                        nc.vector.scalar_tensor_tensor(y[:, q % 2], tl[:, q % 2], 1.0, y[:, q % 2], ALU.add, ALU.mult)\
                            .then_inc(o_ok, 1)
                        if c >= 1:
                            low(q - 1)
                    low(n * NCT + NCT - 1)

            @block.tensor
            def _(pe):
                def job(j):
                    if j >= 4:
                        pe.wait_ge(job_ok, j - 3)
                    bank = pjob[j % 4]
                    if j < JV:
                        pe.wait_ge(w_lo, 8)
                        tok = slice(j * P, (j + 1) * P)
                        last = triple(nc, bank[:].rearrange("p (h d) -> p h d", h=HEADS), [
                            (K["hhi"][:, k, tok], K["hlo"][:, k, tok], whi[:, 4:8, k, :], wlo[:, 4:8, k, :])
                            for k in range(KD)])
                    else:
                        r, n = divmod(j - JV, NSEG)
                        pe.wait_ge(w_lo, 13 + r)
                        w, t0 = SLAB[12 + r][1], TC + n * SEG
                        last = triple(nc, bank[:], [
                            (whi[:, w, k, :], wlo[:, w, k, :], K["hhi"][:, k, t0:t0 + SEG], K["hlo"][:, k, t0:t0 + SEG])
                            for k in range(KD)])
                    last.then_inc(job_ps, 1)

                for c in range(NCT):
                    pe.wait_ge(w_lo, (2, 4, 10, 12)[c])
                    for n in range(NSEG):
                        q = c * NSEG + n
                        if q >= 2:
                            pe.wait_ge(u_ok, q - 1)
                        t0 = TC + n * SEG
                        for s, bank in ((2 * c % 4, pa), (2 * c % 4 + 1, pb)):
                            last = triple(nc, bank[q % 2][:], [
                                (whi[:, s, k, :], wlo[:, s, k, :], K["hhi"][:, k, t0:t0 + SEG],
                                 K["hlo"][:, k, t0:t0 + SEG]) for k in range(KD)])
                        last.then_inc(ab_ps, 1)
                        if c >= 1:
                            job(q - NSEG)
                for j in range(WITH_U, WITH_U + WITH_TAPS):
                    job(j)
                pe.wait_ge(tap_ok, NCT * TAPS)

                def mean(n):
                    if n >= 2:
                        pe.wait_ge(xc_ok, NCT * (n - 1))
                    for c in range(NCT):
                        last = nc.tensor.matmul(pmu[n % 2][:], K["mean_cw"][:], co[:, c, n * SEG:(n + 1) * SEG],
                                                start=(c == 0), stop=(c == NCT - 1))
                    last.then_inc(mu_ps, 1)

                mean(0)
                for n in range(NSEG):
                    if n + 1 < NSEG:
                        mean(n + 1)
                    if n >= 2:
                        pe.wait_ge(sd_ok, n - 1)
                    for c in range(NCT):
                        q = n * NCT + c
                        pe.wait_ge(sq_ok, q + 1)
                        nc.tensor.matmul(pva[n % 2][:], K["mean_cw"][:], sq[:, q % 2], start=(c == 0),
                                         stop=(c == NCT - 1)).then_inc(va_ps, 1)
                        if c == 1:
                            job(ln_job(n, 0))
                    for j in range(1, WITH_LN):
                        job(ln_job(n, j))
                for j in range(ln_job(NSEG, 0), JOBS):
                    job(j)


def heads_stage(nc, K, I, scr):
    UNITS = [(0, -1), (1, -1), (0, 0), (1, 3), (0, 1), (1, 2), (0, 2), (1, 1), (0, 3), (1, 0)]
    NU = len(UNITS)
    NX = NU - 2
    CS = SEG // CH
    BLK = P // CH
    CHAIN = 2 * (TC // CH) + NX * CS + NU
    READ = [0, 3, 1, 2]
    EARLY = 4
    assert NU % 2 == 0

    def size(i):
        return TC if UNITS[i][1] < 0 else SEG

    def tok0(i):
        return 0 if UNITS[i][1] < 0 else TC + SEG * UNITS[i][1]

    def order(i):
        n = size(i) // CH
        return range(n) if UNITS[i][0] == 0 else range(n - 1, -1, -1)

    def U(h, i):
        return h * NU + i

    def X(h, i):
        return h * NX + (max(0, i - 2) if i >= 0 else i)

    def C(h, i):
        return h * CHAIN + (sum(size(j) // CH + 1 for j in range(i)) if i >= 0 else -(CS + 1))

    def at(h, i):
        return h + i // NU, i % NU

    assert C(0, NU) == CHAIN
    first, seen = [], set()
    for d, s in UNITS:
        first.append(s not in seen)
        seen.add(s)

    with nc.cleanup_on_exit(), ExitStack() as ctx:
        m = Mem(nc, ctx)
        wst = m.sb("hwst", [P, 2, KD, P])
        whi = m.sb("hwhi", [P, 2, KD, P], BF16)
        wlo = m.sb("hwlo", [P, 2, KD, P], BF16)
        qT = m.sb("qT", [P, T])
        oT = m.sb("oT", [P, T])
        gT = m.sb("gT", [P, T])
        v = m.sb("v", [P, TC // P + NT, P])
        G = m.sb("G", [P, 2, SEG])
        KK = m.sb("KK", [P, 2, SEG])
        B = m.sb("B", [P, 2, SEG])
        E = m.sb("E", [P, 2, SEG])
        QI = m.sb("QI", [P, 2, SEG])
        KT = m.sb("KT", [P, 2, SEG])
        AT = m.sb("AT", [P, 2, SEG])
        S = m.sb("S", [P, 2, CS + 1, P])
        sm = m.sb("sm", [P, 2, 3, CS])
        se = m.sb("se", [P, 2, 3, CS])
        lbr = m.sb("lbr", [P, 2, 2, HEADS])
        lbd = m.sb("lbd", [P, 2, HEADS])
        gh = m.sb("gh", [P, 2, HEADS])
        gb = m.sb("gb", [P, 2, HEADS])
        lh = m.sb("lh", [P, 2, 2])
        ng = m.sb("ng", [P, HEADS])
        ngh = m.sb("ngh", [P, 1])
        segm = m.sb("segm", [P, SEG])
        msk = m.sb("msk", [P, 2, SEG])
        sqb = m.sb("sqb", [P, 2, SEG])
        rsb = m.sb("rsb", [P, NSEG, SEG])
        tg = m.sb("tg", [P, 2, SEG])
        mh = m.sb("hmh", [P, 2, SEG], BF16)
        ml = m.sb("hml", [P, 2, SEG], BF16)
        flag = m.sb("hflag", [1, 1])
        pflag = m.sb("hpflag", [1, 1])
        pu = [m.ps(f"pu{i}", [P, SEG]) for i in range(4)]
        pj, pk, pat, po = m.ps("pj", [P, SEG]), m.ps("pk", [P, SEG]), m.ps("pat", [P, SEG]), m.ps("po", [P, SEG])

        hpar_in, lb_ok, msk_ok, zero_ok = m.sem("hpar_in"), m.sem("lb_ok"), m.sem("msk_ok"), m.sem("zero_ok")
        hd_ok, pf_ok, ng_ok = m.sem("hd_ok"), m.sem("pf_ok"), m.sem("ng_ok")
        w_in, w_hi, w_lo = m.sems("hw_in", 2), m.sem("hw_hi"), m.sem("hw_lo")
        vc_in, qv_in, g_in = m.sem("vc_in"), m.sems("qv_in", NSEG), m.sem("g_in")
        pj_ps, th_ok, f_ok, kk_ok, lf_ok, b_ok = (m.sem("pj_ps"), m.sem("hth_ok"), m.sem("f_ok"), m.sem("kk_ok"),
                                                  m.sem("lf_ok"), m.sem("b_ok"))
        sm_ok, d_ok, ex_ok, qh_ok, qi_ok, kh_ok, kd_ok = (m.sem("sm_ok"), m.sem("d_ok"), m.sem("ex_ok"), m.sem("qh_ok"),
                                                          m.sem("qi_ok"), m.sem("kh_ok"), m.sem("kd_ok"))
        kt_ps, kt_ok, at_ps, at_ok, u_ps, ch_ok, o_ps, o_ok = (
            m.sem("kt_ps"), m.sem("kt_ok"), m.sem("at_ps"), m.sem("at_ok"), m.sem("u_ps"), m.sem("ch_ok"),
            m.sem("o_ps"), m.sem("ho_ok"))
        osq_ok, ms_ps, sd_ok, rs_ok = m.sem("osq_ok"), m.sem("ms_ps"), m.sem("hsd_ok"), m.sem("hrs_ok")
        y_ok, tg_ok, sg_ok, hm_ok, hmh_ok, hml_ok = (m.sem("hy_ok"), m.sem("tg_ok"), m.sem("sg_ok"), m.sem("hm_ok"),
                                                     m.sem("hmh_ok"), m.sem("hml_ok"))
        m_out = m.sems("hm_out", 2)
        wv = I["w_in"][0].rearrange("(k p) n -> p k n", p=P)

        def seg(j):
            return slice(READ[j] * SEG, (READ[j] + 1) * SEG)

        def heads(engine, one):
            one(0, False, True)
            with engine.Fori(1, HEADS - 1) as h:
                one(h, True, True)
            one(HEADS - 1, True, False)

        with nc.Block() as block:
            @block.sync
            def _(sp):
                with nc.allow_non_contiguous_dma(reason="per-channel constants into columns"):
                    sp.dma_start(ng[:], I["hgrn_norm_g"][0].rearrange("(h p) -> p h", p=P)).then_inc(m_out[0], 16)
                    sp.dma_start(lbr[:, 0, 0, :], I["hgrn_lb_logits"][0, 0].rearrange("(h p) -> p h", p=P))\
                        .then_inc(m_out[1], 16)

                def load(h):
                    for d, col in enumerate((COL_FF, COL_FB)):
                        wait(sp, w_lo, h * 2 - 1 + d)
                        sp.dma_start(wst[:, d], wv[:, :, bass.ds(h * P + col, P)]).then_inc(w_in[d], 16)
                    wait(sp, u_ps, U(h, 2 - NU))
                    hv = scr["v"][bass.ds(h, 1)].rearrange("h p t d -> p (h t) d")
                    hq = scr["q"][bass.ds(h, 1)].rearrange("h p t -> p (h t)")
                    sp.dma_start(v[:, 0:TC // P, :], hv[:, 0:TC // P, :]).then_inc(vc_in, 16)
                    segs = (0, 3, 1, 2) if isinstance(h, int) and h == 0 else (2, 1, 3, 0)
                    for n, s in enumerate(segs):
                        wait(sp, o_ps, h * NX - 3 + n if segs[0] == 2 else 0)
                        t0 = TC // P + s * (SEG // P)
                        sp.dma_start(v[:, t0:t0 + SEG // P, :], hv[:, t0:t0 + SEG // P, :]).then_inc(qv_in[s], 16)
                        sp.dma_start(qT[:, s * SEG:(s + 1) * SEG], hq[:, s * SEG:(s + 1) * SEG]).then_inc(qv_in[s], 16)

                def store(r):
                    for j in range(NSEG):
                        wait(sp, hml_ok, r * NSEG + j + 1)
                        for part, buf in ((0, mh), (1, ml)):
                            n = READ[j]
                            dst = scr["mixed"][4 * n:4 * n + 4, :, part, bass.ds(r + NCT, 1), :]
                            sp.dma_start(dst.rearrange("t p a j -> p t (a j)"),
                                         buf[:, j % 2, :].rearrange("p (t j) -> p t j", j=P)).then_inc(m_out[j % 2], 16)

                load(0)

                def one(h, prev, nxt):
                    if prev:
                        store(h - 1)
                    wait(sp, sg_ok, h * NSEG)
                    sp.dma_start(gT[:], scr["g"][bass.ds(h, 1)].rearrange("h p t -> p (h t)")).then_inc(g_in, 16)
                    if nxt:
                        load(h + 1)

                heads(sp, one)
                store(HEADS - 1)
                for s in range(2):
                    wait(sp, m_out[s], 16 + 32 * (HEADS * NSEG // 2))

            @block.gpsimd
            def _(pool):
                with nc.allow_non_contiguous_dma(reason="per-channel constants into columns"):
                    for l in range(2):
                        for d in range(2):
                            if (l, d) == (0, 0):
                                continue
                            pool.dma_start(lbr[:, l, d, :], I["hgrn_lb_logits"][l, d].rearrange("(h p) -> p h", p=P))\
                                .then_inc(hpar_in, 16)
                nc.gpsimd.memset(segm[:], 1.0).then_inc(msk_ok, 1)
                nc.gpsimd.memset(msk[:], 1.0).then_inc(msk_ok, 1)
                wait(pool, msk_ok, 2)
                nc.gpsimd.memset(segm[:, 0:SEG:CH], 0.0).then_inc(msk_ok, 1)
                pat4 = [[0, SEG // P], [-CH, BLK], [0, CH]]
                for d in range(2):
                    mv = msk[:, d, :].rearrange("p (r b i) -> p r b i", r=SEG // P, b=BLK)
                    conds = [(0, 1, pat4), (CH - 1, -1, [[0, SEG // P], [CH, BLK], [0, CH]]),
                             (0, -1 if d == 0 else 1,
                              [[0, SEG // P], [CH if d == 0 else -CH, BLK], [1 if d == 0 else -1, CH]])]
                    for n, (base, mult, pattern) in enumerate(conds):
                        wait(pool, msk_ok, 3 + 3 * d + n)
                        nc.gpsimd.affine_select(out=mv, in_=mv, compare_op=ALU.is_ge, fill=0.0, base=base,
                                                pattern=pattern, channel_multiplier=mult).then_inc(msk_ok, 1)
                nc.gpsimd.memset(pflag[:], 0.0).then_inc(pf_ok, 1)
                nc.gpsimd.memset(AT[:], 0.0).then_inc(zero_ok, 1)
                wait(pool, zero_ok, 1)

                def keep(h, i):
                    h, i = at(h, i)
                    p, n = i % 2, size(i)
                    wait(pool, f_ok, U(h, i) + 1)
                    wait(pool, kt_ps, U(h, i - 1))
                    wait(pool, pf_ok, U(h, i) + 1)
                    nc.gpsimd.tensor_tensor(pflag[:], pflag[:], pflag[:], ALU.mult).then_inc(pf_ok, 1)
                    nc.gpsimd.tensor_scalar(KK[:, p, 0:n], G[:, p, 0:n], -1.0, 1.0, ALU.mult, ALU.add).then_inc(kk_ok, 1)

                def decay_k(h, i):
                    h, i = at(h, i)
                    p, n = i % 2, size(i)
                    wait(pool, ex_ok, U(h, i) + 1)
                    wait(pool, kk_ok, U(h, i) + 1)
                    nc.gpsimd.tensor_tensor(B[:, p, 0:n], KK[:, p, 0:n], B[:, p, 0:n], ALU.mult).then_inc(kh_ok, 1)
                    wait(pool, kh_ok, U(h, i) + 1)
                    c3 = lambda t: t[:, p, 0:n].rearrange("p (c j) -> p c j", j=CH)
                    nc.gpsimd.tensor_tensor(c3(KK), c3(B), se[:, p, 1, 0:n // CH].unsqueeze(2)
                                            .broadcast_to([P, n // CH, CH]), ALU.mult).then_inc(kd_ok, 1)

                def normed(r, j):
                    wait(pool, rs_ok, r * NSEG + j + 1)
                    wait(pool, o_ok, r * NX + NX)
                    nc.gpsimd.tensor_tensor(oT[:, seg(j)], oT[:, seg(j)], rsb[:, j], ALU.mult).then_inc(y_ok, 1)

                def low(r, j):
                    wait(pool, hmh_ok, r * NSEG + j + 1)
                    wait(pool, m_out[j % 2], r * 64 + 32 * (j // 2) + 16)
                    nc.gpsimd.tensor_tensor(ml[:, j % 2], oT[:, seg(j)], mh[:, j % 2], ALU.subtract).then_inc(hml_ok, 1)

                keep(0, 0)
                keep(0, 1)
                decay_k(0, 0)

                def one(h, prev, nxt):
                    for i in range(NU):
                        if nxt or i + 1 < NU:
                            decay_k(h, i + 1)
                        if prev and 2 <= i < 2 + NSEG:
                            normed(h - 1, i - 2)
                        if nxt or i + 2 < NU:
                            keep(h, i + 2)
                        if prev and 3 <= i < 3 + NSEG:
                            low(h - 1, i - 3)

                heads(pool, one)
                for j in range(NSEG + 1):
                    if j < NSEG:
                        normed(HEADS - 1, j)
                    if j >= 1:
                        low(HEADS - 1, j - 1)

            @block.scalar
            def _(act):
                wait(act, lb_ok, 1)
                nc.scalar.activation(lbd[:], lbd[:], ACT.Tanh, scale=0.5).then_inc(lb_ok, 1)

                def split(h, d):
                    wait(act, w_in[d], h * 16 + 16)
                    wait(act, pj_ps, U(h, d - 1))
                    nc.scalar.activation(whi[:, d], wst[:, d], ACT.Copy).then_inc(w_hi, 1)

                def gate(h, i):
                    h, i = at(h, i)
                    p, n = i % 2, size(i)
                    wait(act, pj_ps, U(h, i) + 1)
                    wait(act, kk_ok, U(h, i - 1))
                    wait(act, lf_ok, U(h, i - 1))
                    nc.scalar.activation(G[:, p, 0:n], pj[:, 0:n], ACT.Tanh, scale=0.5).then_inc(th_ok, 1)

                def logs(h, i):
                    h, i = at(h, i)
                    p, n = i % 2, size(i)
                    wait(act, f_ok, U(h, i) + 1)
                    wait(act, at_ps, X(h, i - 1))
                    wait(act, qi_ok, X(h, i - 1))
                    nc.scalar.activation(E[:, p, 0:n], G[:, p, 0:n], ACT.Ln).then_inc(lf_ok, 1)

                def exps(h, i):
                    h, i = at(h, i)
                    p, n = i % 2, size(i)
                    wait(act, d_ok, U(h, i) + 1)
                    wait(act, kd_ok, U(h, i - 1))
                    wait(act, qi_ok, X(h, i - 1))
                    wait(act, ch_ok, C(h, i - 1))
                    nc.scalar.activation(se[:, p, :, 0:n // CH], sm[:, p, :, 0:n // CH], ACT.Exp).then_inc(sm_ok, 1)
                    if UNITS[i][1] >= 0:
                        nc.scalar.activation(E[:, p, 0:n], B[:, p, 0:n], ACT.Exp).then_inc(sm_ok, 1)
                    nc.scalar.activation(B[:, p, 0:n], B[:, p, 0:n], ACT.Exp, scale=-1.0).then_inc(ex_ok, 1)

                def turn(h, i):
                    h, i = at(h, i)
                    p, n = i % 2, size(i)
                    wait(act, kt_ps, U(h, i) + 1)
                    wait(act, u_ps, U(h, i - 1))
                    nc.scalar.activation(KT[:, p, 0:n], pk[:, 0:n], ACT.Copy).then_inc(kt_ok, 1)

                def squares(r, j):
                    wait(act, o_ok, r * NX + NX)
                    if j >= 2:
                        wait(act, ms_ps, r * NSEG + j - 1)
                    nc.scalar.activation(sqb[:, j % 2], oT[:, seg(j)], ACT.Square).then_inc(osq_ok, 1)

                def deviation(r, j):
                    wait(act, ms_ps, r * NSEG + j + 1)
                    nc.scalar.activation(rsb[:, j], po[:], ACT.Sqrt, bias=K["eps"][:, 0:1]).then_inc(sd_ok, 1)

                def half_tanh(r, j):
                    wait(act, g_in, r * 16 + 16)
                    if j >= 2:
                        wait(act, hm_ok, r * NSEG + j - 1)
                    nc.scalar.activation(tg[:, j % 2], gT[:, seg(j)], ACT.Tanh, scale=0.5).then_inc(tg_ok, 1)

                def cast(r, j):
                    wait(act, hm_ok, r * NSEG + j + 1)
                    wait(act, m_out[j % 2], r * 64 + 32 * (j // 2) + 16)
                    nc.scalar.activation(mh[:, j % 2], oT[:, seg(j)], ACT.Copy).then_inc(hmh_ok, 1)

                split(0, 0)
                split(0, 1)
                gate(0, 0)
                logs(0, 0)
                gate(0, 1)
                exps(0, 0)
                logs(0, 1)
                turn(0, 0)

                def one(h, prev, nxt):
                    for i in range(NU):
                        if prev and 3 <= i < 3 + NSEG:
                            cast(h - 1, i - 3)
                        if prev and i in (1, 2):
                            squares(h - 1, 2 * i - 2)
                            squares(h - 1, 2 * i - 1)
                        if nxt or i + 1 < NU:
                            exps(h, i + 1)
                        if prev and i in (1, 2):
                            deviation(h - 1, 2 * i - 2)
                        if nxt or i + 1 < NU:
                            turn(h, i + 1)
                        if nxt or i + 2 < NU:
                            gate(h, i + 2)
                            logs(h, i + 2)
                        if prev and i in (1, 2):
                            deviation(h - 1, 2 * i - 1)
                        if prev and 1 <= i < 1 + NSEG:
                            half_tanh(h - 1, i - 1)
                        if nxt and i in (7, 8):
                            split(h + 1, i - 7)

                heads(act, one)
                last = HEADS - 1
                for j in range(NSEG):
                    squares(last, j)
                    deviation(last, j)
                for j in range(NSEG + 2):
                    if j < NSEG:
                        half_tanh(last, j)
                    if j >= 1 and j <= NSEG:
                        cast(last, j - 1)

            @block.vector
            def _(dve):
                wait(dve, hpar_in, 48)
                wait(dve, m_out[0], 16)
                wait(dve, m_out[1], 16)
                nc.vector.tensor_tensor(lbd[:], lbr[:, 0], lbr[:, 1], ALU.subtract).then_inc(lb_ok, 1)
                wait(dve, lb_ok, 2)
                nc.vector.tensor_scalar(gh[:], lbd[:], -0.25, 0.25, ALU.mult, ALU.add).then_inc(lb_ok, 1)
                nc.vector.tensor_scalar(gb[:], lbd[:], 0.25, 0.75, ALU.mult, ALU.add).then_inc(lb_ok, 1)
                nc.vector.tensor_scalar(ng[:], ng[:], 0.5, None, ALU.mult).then_inc(lb_ok, 1)
                wait(dve, lb_ok, 5)
                wait(dve, msk_ok, 9)
                wait(dve, zero_ok, 1)

                def split(h, d):
                    wait(dve, w_hi, h * 2 + d + 1)
                    nc.vector.tensor_tensor(wlo[:, d], wst[:, d], whi[:, d], ALU.subtract).then_inc(w_lo, 1)

                def constants(h, d):
                    nc.vector.tensor_copy(lh[:, d, 0:1], gh[:, d, bass.ds(h, 1)]).then_inc(hd_ok, 1)
                    nc.vector.tensor_copy(lh[:, d, 1:2], gb[:, d, bass.ds(h, 1)]).then_inc(hd_ok, 1)

                def forget(h, i):
                    h, i = at(h, i)
                    p, n, d = i % 2, size(i), UNITS[i][0]
                    wait(dve, th_ok, U(h, i) + 1)
                    if i < 2:
                        wait(dve, hd_ok, h * 4 + 2 * i + 2)
                    nc.vector.tensor_scalar(G[:, p, 0:n], G[:, p, 0:n], lh[:, d, 0:1], lh[:, d, 1:2], ALU.mult,
                                            ALU.add).then_inc(f_ok, 1)

                def sums(h, i):
                    h, i = at(h, i)
                    p, n, d = i % 2, size(i), UNITS[i][0]
                    nch = n // CH
                    mid, end = (CH // 2 - 1, CH - 1) if d == 0 else (CH // 2, 0)
                    wait(dve, lf_ok, U(h, i) + 1)
                    wait(dve, kd_ok, U(h, i - 1))
                    way = slice(0, n) if d == 0 else slice(n - 1, None, -1)
                    nc.vector.tensor_tensor_scan(B[:, p, way], segm[:, 0:n], E[:, p, way], 0.0, ALU.mult, ALU.add)\
                        .then_inc(b_ok, 1)
                    b3 = B[:, p, 0:n].rearrange("p (c j) -> p c j", j=CH)
                    wait(dve, b_ok, 3 * U(h, i) + 1)
                    wait(dve, ex_ok, U(h, i - 1))
                    nc.vector.tensor_copy(sm[:, p, 0, 0:nch], b3[:, :, mid]).then_inc(b_ok, 1)
                    nc.vector.tensor_copy(sm[:, p, 2, 0:nch], b3[:, :, end]).then_inc(b_ok, 1)
                    wait(dve, b_ok, 3 * U(h, i) + 3)
                    nc.vector.tensor_tensor(sm[:, p, 1, 0:nch], sm[:, p, 2, 0:nch], sm[:, p, 0, 0:nch], ALU.subtract)
                    nc.vector.tensor_tensor(b3, b3, sm[:, p, 0, 0:nch].unsqueeze(2).broadcast_to([P, nch, CH]),
                                            ALU.subtract).then_inc(d_ok, 1)

                def decay_q(h, i):
                    h, i = at(h, i)
                    s = UNITS[i][1]
                    if s < 0:
                        return
                    wait(dve, ex_ok, U(h, i) + 1)
                    wait(dve, qv_in[s], h * 32 + 32)
                    nc.vector.tensor_tensor(E[:, i % 2], qT[:, s * SEG:(s + 1) * SEG], E[:, i % 2], ALU.mult)\
                        .then_inc(qh_ok, 1)

                def decay_q_start(h, i):
                    h, i = at(h, i)
                    p = i % 2
                    if UNITS[i][1] < 0:
                        return
                    wait(dve, qh_ok, X(h, i) + 1)
                    wait(dve, o_ps, X(h, i - 1))
                    c3 = lambda t: t[:, p].rearrange("p (c j) -> p c j", j=CH)
                    nc.vector.tensor_tensor(c3(QI), c3(E), se[:, p, 0].unsqueeze(2).broadcast_to([P, CS, CH]),
                                            ALU.mult).then_inc(qi_ok, 1)

                def mask(h, i):
                    h, i = at(h, i)
                    if UNITS[i][1] < 0:
                        return
                    wait(dve, at_ps, X(h, i) + 1)
                    wait(dve, o_ps, X(h, i - 1))
                    nc.vector.memset(flag[:], 0.0)
                    nc.vector.copy_predicated(AT[:, i % 2], msk[:, UNITS[i][0]].bitcast(U32), pat[:]).then_inc(at_ok, 1)

                def chain(h, i, part):
                    p, d = i % 2, UNITS[i][0]
                    done = C(h, i) + 1
                    if part == 0:
                        wait(dve, o_ps, X(h, i - 1))
                        wait(dve, ch_ok, C(h, i))
                        if UNITS[i][1] < 0:
                            nc.vector.memset(S[:, d, 0, :], 0.0).then_inc(ch_ok, 1)
                        else:
                            nc.vector.tensor_copy(S[:, d, 0, :], S[:, d, size(i - 2) // CH, :]).then_inc(ch_ok, 1)
                        wait(dve, u_ps, U(h, i) + 1)
                    for n, c in enumerate(order(i)):
                        if (n < EARLY) == (part == 0):
                            wait(dve, ch_ok, done + n)
                            nc.vector.scalar_tensor_tensor(S[:, d, n + 1, :], S[:, d, n, :], se[:, p, 2, c:c + 1],
                                                           pu[c % BLK][:, (c // BLK) * P:(c // BLK + 1) * P],
                                                           ALU.mult, ALU.add).then_inc(ch_ok, 1)

                def collect(h, i):
                    if UNITS[i][1] < 0:
                        return
                    t0 = UNITS[i][1] * SEG
                    wait(dve, o_ps, X(h, i) + 1)
                    if first[i]:
                        wait(dve, hml_ok, h * NSEG - NSEG + READ.index(UNITS[i][1]) + 1)
                        ins = nc.vector.tensor_copy(oT[:, t0:t0 + SEG], po[:])
                    else:
                        wait(dve, o_ok, X(h, i))
                        ins = nc.vector.tensor_tensor(oT[:, t0:t0 + SEG], oT[:, t0:t0 + SEG], po[:], ALU.add)
                    ins.then_inc(o_ok, 1)

                def inverse(r, j):
                    wait(dve, sd_ok, r * NSEG + j + 1)
                    nc.vector.reciprocal(rsb[:, j], rsb[:, j]).then_inc(rs_ok, 1)

                def read(r, j):
                    if j == 0:
                        nc.vector.tensor_copy(ngh[:], ng[:, bass.ds(r, 1)]).then_inc(ng_ok, 1)
                    n = r * NSEG + j + 1
                    sl = oT[:, seg(j)]
                    wait(dve, tg_ok, n)
                    nc.vector.scalar_tensor_tensor(tg[:, j % 2], tg[:, j % 2], 1.0, gT[:, seg(j)], ALU.add, ALU.mult)\
                        .then_inc(sg_ok, 1)
                    wait(dve, y_ok, n)
                    wait(dve, sg_ok, n)
                    wait(dve, ng_ok, r + 1)
                    nc.vector.scalar_tensor_tensor(sl, sl, ngh[:, 0:1], tg[:, j % 2], ALU.mult, ALU.mult).then_inc(hm_ok, 1)

                for d in range(2):
                    constants(0, d)
                    split(0, d)
                forget(0, 0)
                sums(0, 0)
                forget(0, 1)

                def one(h, prev, nxt):
                    for i in range(NU):
                        if i >= 2:
                            collect(h, i - 2)
                        elif i == 0 and prev:
                            collect(h - 1, NU - 2)
                        if nxt or i + 1 < NU:
                            sums(h, i + 1)
                        chain(h, i, 0)
                        if nxt or i + 1 < NU:
                            decay_q(h, i + 1)
                        chain(h, i, 1)
                        if prev and 1 <= i < 1 + NSEG:
                            inverse(h - 1, i - 1)
                        if nxt or i + 1 < NU:
                            decay_q_start(h, i + 1)
                        if nxt or i + 2 < NU:
                            forget(h, i + 2)
                        if nxt or i + 1 < NU:
                            mask(h, i + 1)
                        if i == 0 and prev:
                            collect(h - 1, NU - 1)
                        if prev and 2 <= i < 2 + NSEG:
                            read(h - 1, i - 2)
                        if nxt and i in (7, 8):
                            constants(h + 1, i - 7)
                            split(h + 1, i - 7)

                heads(dve, one)
                last = HEADS - 1
                collect(last, NU - 2)
                collect(last, NU - 1)
                inverse(last, 0)
                for j in range(NSEG):
                    if j + 1 < NSEG:
                        inverse(last, j + 1)
                    read(last, j)

            @block.tensor
            def _(pe):
                def project(h, i, first=0, end=3 * KD):
                    h, i = at(h, i)
                    d, n, t0 = UNITS[i][0], size(i), tok0(i)
                    for mm in range(first, end):
                        k = mm // 3
                        if mm == 0:
                            wait(pe, w_lo, h * 2 + d + 1)
                            wait(pe, th_ok, U(h, i))
                        w = (whi, whi, wlo)[mm % 3][:, d, k, :]
                        x = K[("hhi", "hlo", "hhi")[mm % 3]][:, k, t0:t0 + n]
                        ins = nc.tensor.matmul(pj[:, 0:n], w, x, start=(mm == 0), stop=(mm == 3 * KD - 1))
                    if end == 3 * KD:
                        ins.then_inc(pj_ps, 1)

                def scores(h, i):
                    h, i = at(h, i)
                    p, tiles = i % 2, size(i) // P
                    wait(pe, kd_ok, U(h, i) + 1)
                    wait(pe, kt_ok, U(h, i))
                    for t in range(tiles):
                        last = nc.tensor.transpose(pk[:, t * P:(t + 1) * P], KK[:, p, t * P:(t + 1) * P], K["ident"][:])
                    last.then_inc(kt_ps, 1)
                    if UNITS[i][1] >= 0:
                        wait(pe, qh_ok, X(h, i) + 1)
                        wait(pe, at_ok, X(h, i))
                        for t in range(tiles):
                            last = nc.tensor.matmul(pat[:, t * P:(t + 1) * P], B[:, p, t * P:(t + 1) * P],
                                                    E[:, p, t * P:(t + 1) * P], start=True, stop=True)
                        last.then_inc(at_ps, 1)

                def updates(h, i):
                    p, tiles, v0 = i % 2, size(i) // P, tok0(i) // P
                    wait(pe, kt_ok, U(h, i) + 1)
                    wait(pe, ch_ok, C(h, i))
                    if UNITS[i][1] < 0:
                        wait(pe, vc_in, h * 16 + 16)
                    else:
                        wait(pe, qv_in[UNITS[i][1]], h * 32 + 32)
                    for t in range(tiles):
                        for j in range(BLK):
                            rows = slice(CH * j, CH * (j + 1))
                            last = nc.tensor.matmul(pu[j][:, t * P:(t + 1) * P], KT[rows, p, t * P:(t + 1) * P],
                                                    v[rows, v0 + t, :], start=True, stop=True)
                    last.then_inc(u_ps, 1)

                def output(h, i, mm):
                    p, d, v0 = i % 2, UNITS[i][0], tok0(i) // P
                    if mm == 0:
                        wait(pe, at_ok, X(h, i) + 1)
                        wait(pe, qi_ok, X(h, i) + 1)
                        wait(pe, o_ok, X(h, i))
                        if i == 2:
                            wait(pe, sd_ok, h * NSEG)
                        wait(pe, ch_ok, C(h, i + 1))
                    if mm < SEG // P:
                        nc.tensor.matmul(po[:, mm * P:(mm + 1) * P], v[:, v0 + mm, :], AT[:, p, mm * P:(mm + 1) * P],
                                         start=(mm == 0), stop=False, skip_group_check=True)
                    else:
                        n = mm - SEG // P
                        c = order(i)[n]
                        ins = nc.tensor.matmul(po[:, c * CH:(c + 1) * CH], S[:, d, n, :], QI[:, p, c * CH:(c + 1) * CH],
                                               start=False, stop=(n == CS - 1), skip_group_check=True)
                        if n == CS - 1:
                            ins.then_inc(o_ps, 1)

                def project_and_output(h, i, prev, nxt, first, end):
                    for mm in range(first, end):
                        if nxt or i + 2 < NU:
                            project(h, i + 2, mm, mm + 1)
                        if mm < SEG // P + CS:
                            if i >= 3:
                                output(h, i - 1, mm)
                            elif i == 0 and prev:
                                output(h - 1, NU - 1, mm)

                def mean(r, j):
                    wait(pe, osq_ok, r * NSEG + j + 1)
                    if j >= 1:
                        wait(pe, sd_ok, r * NSEG + j)
                    nc.tensor.matmul(po[:], K["mean_p"][:], sqb[:, j % 2], start=True, stop=True).then_inc(ms_ps, 1)

                project(0, 0)
                project(0, 1)
                scores(0, 0)

                def one(h, prev, nxt):
                    for i in range(NU):
                        updates(h, i)
                        if prev and i in (1, 2):
                            mean(h - 1, 2 * i - 2)
                        project_and_output(h, i, prev, nxt, 0, 2 * KD)
                        if prev and i in (1, 2):
                            mean(h - 1, 2 * i - 1)
                        if nxt or i + 1 < NU:
                            scores(h, i + 1)
                        project_and_output(h, i, prev, nxt, 2 * KD, 3 * KD)

                heads(pe, one)
                for mm in range(SEG // P + CS):
                    output(HEADS - 1, NU - 1, mm)
                for j in range(NSEG):
                    mean(HEADS - 1, j)


def outproj_stage(nc, K, I, scr):
    with nc.cleanup_on_exit(), ExitStack() as ctx:
        m = Mem(nc, ctx)
        wst = m.sb("owst", [P, 2, KD, SEG])
        whi = m.sb("owhi", [P, KD, D], BF16)
        wlo = m.sb("owlo", [P, KD, D], BF16)
        rw = m.sb("rw", [P, KD, NE])
        mrow = m.sb("mrow", [P, 3, D])
        xt = m.sb("xt", [P, 2, D])
        mx = m.sb("mx", [P, 2, 2, KD, P], BF16)
        t1 = m.sb("t1", [P, 2, D])
        x1 = m.sb("x1", [P, 2, D])
        junk = m.sb("ojunk", [P, D])
        st = m.sb("st", [P, 2, 4])
        h2 = m.sb("h2", [P, 2, D])
        row32 = m.sb("row", [P, 2, ROWW], I32)
        row = row32[:].bitcast(BF16)
        prob = row32[:, :, D:ROWW].bitcast(F32)
        h2T = m.sb("h2T", [P, D])
        nm = m.sb("nm", [P, 2, 4])
        pe_ = m.sb("pexp", [P, 2, NE])
        pT = m.sb("pT", [NE, T])
        pout = [m.ps(f"pout{i}", [P, 2, SEG]) for i in range(2)]
        ptp = m.ps("ptp", [P, 2, SEG])
        plg = m.ps("plg", [P, SEG])[:, 0:NE]
        ppt = m.ps("ppt", [P, SEG])[0:NE, 0:P]

        w_in, w_hi, w_lo, r_in = m.sems("ow_in", 4), m.sem("ow_hi"), m.sem("ow_lo"), m.sem("or_in")
        x_in, m_in = m.sems("ox_in", 2), m.sems("om_in", 2)
        out_ps, t1_ok, x1_ok, ss_ok, sd_ok, rs_ok, hn_ok, h2_ok = (
            m.sems("oo_ps", 2), m.sems("ot1", 2), m.sems("ox1", 2), m.sems("oss", 2), m.sems("osd", 2),
            m.sems("ors", 2), m.sems("ohn", 2), m.sems("oh2", 2))
        hi_ok, lo_ok, tp_ps, tp_ok, lg_ps, mx_ok, ex_ok, ri_ok, pr_ok, pt_ps, pt_ok = (
            m.sems("ohi", 2), m.sems("olo", 2), m.sems("otp", 2), m.sems("otc", 2), m.sems("olg", 2), m.sems("omx", 2),
            m.sems("oex", 2), m.sems("ori", 2), m.sems("opr", 2), m.sems("oppt", 2), m.sems("optc", 2))
        x1_out, row_out = m.sems("x1_out", 2), m.sems("orow_out", 2)
        pT_out = m.sem("pT_out")
        wv = I["w_out"][0].rearrange("(k p) n -> p k n", p=P)

        def piece(w):
            return w // 2, slice(w % 2 * KD // 2, (w % 2 + 1) * KD // 2)

        def steps(engine, step):
            def two(i):
                step(i * 2 + 2, 0, i + 1, (True, True, True))
                step(i * 2 + 3, 1, i + 1, (True, True, True))

            step(0, 0, 0, (True, False, False))
            step(1, 1, 0, (True, True, False))
            peeled(engine, NT // 2 - 1, two)
            step(NT, 0, NT // 2, (False, True, True))
            step(NT + 1, 1, NT // 2, (False, False, True))

        def tile_rows(ap, t):
            return ap[bass.ds(t * P, P), :]

        with nc.Block() as block:
            @block.sync
            def _(sp):
                def load_mixed(t, p, n):
                    wait(sp, out_ps[p], n)
                    sp.dma_start(mx[:, p], scr["mixed"][bass.ds(t, 1), :, :, :, :].rearrange("t p a c j -> (t p) a c j"))\
                        .then_inc(m_in[p], 16)

                for w in range(4):
                    c, ks = piece(w)
                    sp.dma_start(wst[:, c, ks], wv[:, ks, c * SEG:(c + 1) * SEG]).then_inc(w_in[w], 16)
                    if w == 1:
                        for t in range(2):
                            load_mixed(t, t, 0)
                sp.dma_start(rw[:], I["router_w"][0].rearrange("(k p) e -> p k e", p=P)).then_inc(r_in, 16)
                for j, r in enumerate((0, 2, 1)):
                    sp.dma_start(mrow[:, j], scr["modrows"][2 * r:2 * r + 2, :].rearrange("a n -> (a n)")
                                 .partition_broadcast(P)).then_inc(r_in, 16)

                def load_x(t, p, n):
                    wait(sp, x1_ok[p], n)
                    sp.dma_start(xt[:, p], tile_rows(I["x"][0], t)).then_inc(x_in[p], 16)

                def store_x1(t, p, n):
                    wait(sp, x1_ok[p], n + 1)
                    sp.dma_start(tile_rows(scr["y"], t), x1[:, p]).then_inc(x1_out[p], 16)

                def store_row(t, p, n):
                    wait(sp, pr_ok[p], n + 1)
                    wait(sp, lo_ok[p], n + 1)
                    sp.dma_start(tile_rows(scr["rows"], t), row32[:, p]).then_inc(row_out[p], 16)

                for t in range(2):
                    load_x(t, t, 0)

                def two(i):
                    for p in range(2):
                        t = i * 2 + p
                        load_mixed(t + 2, p, i + 1)
                        load_x(t + 2, p, i + 1)
                        store_x1(t, p, i)
                        if p == 1:
                            store_row(t - 1, 0, i)
                        elif not (isinstance(i, int) and i == 0):
                            store_row(t - 1, 1, i - 1)

                peeled(sp, NT // 2 - 1, two)
                store_x1(NT - 2, 0, NT // 2 - 1)
                store_row(NT - 3, 1, NT // 2 - 2)
                store_x1(NT - 1, 1, NT // 2 - 1)
                store_row(NT - 2, 0, NT // 2 - 1)
                store_row(NT - 1, 1, NT // 2 - 1)
                wait(sp, pt_ok[0], NT // 2)
                wait(sp, pt_ok[1], NT // 2)
                sp.dma_start(scr["pT"], pT[:]).then_inc(pT_out, 16)
                for s in range(2):
                    wait(sp, x1_out[s], 16 * NT // 2)
                    wait(sp, row_out[s], 16 * NT // 2)
                wait(sp, pT_out, 16)

            @block.gpsimd
            def _(pool):
                wait(pool, r_in, 64)

                def front(t, p, n):
                    wait(pool, x_in[p], n * 16 + 16)
                    wait(pool, t1_ok[p], n + 1)
                    wait(pool, x1_out[p], n * 16)
                    wait(pool, hn_ok[p], n)
                    nc.gpsimd.tensor_tensor(x1[:, p], xt[:, p], t1[:, p], ALU.add).then_inc(x1_ok[p], 1)
                    wait(pool, hn_ok[p], n + 1)
                    nc.gpsimd.tensor_tensor(h2[:, p], h2[:, p], mrow[:, 2], ALU.add).then_inc(h2_ok[p], 1)

                steps(pool, lambda t, p, n, have: front(t, p, n) if have[0] else None)

            @block.scalar
            def _(act):
                for w in range(4):
                    c, ks = piece(w)
                    wait(act, w_in[w], 16)
                    nc.scalar.activation(whi[:, ks, c * SEG:(c + 1) * SEG], wst[:, c, ks], ACT.Copy).then_inc(w_hi, 1)

                def front(t, p, n):
                    wait(act, x1_ok[p], n + 1)
                    nc.scalar.activation(junk[:], x1[:, p], ACT.Square, accum_out=st[:, p, 0:1]).then_inc(ss_ok[p], 1)
                    wait(act, ss_ok[p], n + 1)
                    nc.scalar.activation(st[:, p, 1:2], st[:, p, 0:1], ACT.Sqrt, bias=K["eps"][:, 0:1], scale=1.0 / D)\
                        .then_inc(sd_ok[p], 1)
                    wait(act, h2_ok[p], n + 1)
                    wait(act, row_out[p], n * 16)
                    nc.scalar.activation(row[:, p, 0:D], h2[:, p], ACT.Copy).then_inc(hi_ok[p], 1)

                def turn(p, n):
                    wait(act, tp_ps[p], n + 1)
                    wait(act, lg_ps[1 - p], n + p)
                    nc.scalar.activation(h2T[:], ptp[:].rearrange("p a j -> p (a j)"), ACT.Copy).then_inc(tp_ok[p], 1)

                def route(p, n):
                    wait(act, mx_ok[p], n + 1)
                    nc.scalar.activation(pe_[:, p], plg, ACT.Exp, bias=nm[:, p, 0:1], accum_out=nm[:, p, 1:2])\
                        .then_inc(ex_ok[p], 1)

                def step(t, p, n, have):
                    if have[2]:
                        route(p, n - 1)
                    if have[1]:
                        turn(1 - p, n - 1 + p)
                    if have[0]:
                        front(t, p, n)

                steps(act, step)

            @block.vector
            def _(dve):
                for w in range(4):
                    c, ks = piece(w)
                    wait(dve, w_hi, w + 1)
                    nc.vector.tensor_tensor(wlo[:, ks, c * SEG:(c + 1) * SEG], wst[:, c, ks],
                                            whi[:, ks, c * SEG:(c + 1) * SEG], ALU.subtract).then_inc(w_lo, 1)
                wait(dve, r_in, 64)

                def gated(t, p, n):
                    wait(dve, out_ps[p], n + 1)
                    wait(dve, x1_ok[p], n)
                    nc.vector.tensor_tensor(t1[:, p], pout[p][:].rearrange("p a j -> p (a j)"), mrow[:, 0], ALU.mult)\
                        .then_inc(t1_ok[p], 1)

                def front(t, p, n):
                    wait(dve, sd_ok[p], n + 1)
                    nc.vector.reciprocal(st[:, p, 2:3], st[:, p, 1:2]).then_inc(rs_ok[p], 1)
                    wait(dve, rs_ok[p], n + 1)
                    wait(dve, x1_ok[p], n + 1)
                    wait(dve, tp_ps[p], n)
                    nc.vector.scalar_tensor_tensor(h2[:, p], x1[:, p], st[:, p, 2:3], mrow[:, 1], ALU.mult, ALU.mult)\
                        .then_inc(hn_ok[p], 1)
                    wait(dve, hi_ok[p], n + 1)
                    nc.vector.tensor_tensor(row[:, p, D:2 * D], h2[:, p], row[:, p, 0:D], ALU.subtract).then_inc(lo_ok[p], 1)

                def route(t, p, n):
                    wait(dve, lg_ps[p], n + 1)
                    nc.vector.tensor_reduce(nm[:, p, 0:1], plg, AX.X, ALU.max, negate=True).then_inc(mx_ok[p], 1)
                    wait(dve, ex_ok[p], n + 1)
                    nc.vector.reciprocal(nm[:, p, 2:3], nm[:, p, 1:2]).then_inc(ri_ok[p], 1)
                    wait(dve, ri_ok[p], n + 1)
                    nc.vector.tensor_scalar(prob[:, p, :], pe_[:, p], nm[:, p, 2:3], None, ALU.mult)\
                        .then_inc(pr_ok[p], 1)

                def collect(t, p, n):
                    wait(dve, pt_ps[p], n + 1)
                    nc.vector.tensor_copy(pT[:, bass.ds(t * P, P)], ppt).then_inc(pt_ok[p], 1)

                def step(t, p, n, have):
                    if have[2]:
                        route(t - 2, p, n - 1)
                    if have[0]:
                        gated(t, p, n)
                    if have[2]:
                        collect(t - 2, p, n - 1)
                    if have[0]:
                        front(t, p, n)

                steps(dve, step)

            @block.tensor
            def _(pe):
                def project(p, n, c):
                    if isinstance(n, int) and n == 0:
                        wait(pe, w_lo, 2 * c + 2)
                    if c == 0:
                        wait(pe, m_in[p], n * 16 + 16)
                        wait(pe, t1_ok[p], n)
                    last = triple(nc, pout[p][:, c, :], [
                        (mx[:, p, 0, k, :], mx[:, p, 1, k, :], whi[:, k, c * SEG:(c + 1) * SEG],
                         wlo[:, k, c * SEG:(c + 1) * SEG]) for k in range(KD)])
                    if c == 1:
                        last.then_inc(out_ps[p], 1)

                def turn(p, n):
                    wait(pe, h2_ok[p], n + 1)
                    wait(pe, tp_ok[1 - p], n + p)
                    for k in range(KD):
                        last = nc.tensor.transpose(ptp[:, k // 4, (k % 4) * P:(k % 4 + 1) * P], h2[:, p, k * P:(k + 1) * P],
                                                   K["ident"][:])
                    last.then_inc(tp_ps[p], 1)

                def logits(p, n):
                    if isinstance(n, int) and n == 0:
                        wait(pe, r_in, 64)
                    wait(pe, tp_ok[p], n + 1)
                    wait(pe, ex_ok[1 - p], n + p)
                    for k in range(KD):
                        last = nc.tensor.matmul(plg, h2T[:, k * P:(k + 1) * P], rw[:, k, :], start=(k == 0),
                                                stop=(k == KD - 1))
                    last.then_inc(lg_ps[p], 1)

                def spread(p, n):
                    wait(pe, pr_ok[p], n + 1)
                    wait(pe, pt_ok[1 - p], n + p)
                    nc.tensor.transpose(ppt, prob[:, p, :], K["ident"][:]).then_inc(pt_ps[p], 1)

                def step(t, p, n, have):
                    if have[0]:
                        project(p, n, 0)
                    if have[2]:
                        logits(p, n - 1)
                    if have[0]:
                        project(p, n, 1)
                    if have[1]:
                        turn(1 - p, n - 1 + p)
                    if have[2]:
                        spread(p, n - 1)

                steps(pe, step)


class ExpertWeights:
    FH = SEG
    NB = 6
    NS = 3
    HALVES = 2 * NB
    HEAD_START = 6
    HALF_OF = [0, 0, 1, 1, 0, 1]

    def __init__(self, m, I):
        self.mats = [I["w_gate"], I["w_up"], I["w_gate"], I["w_up"], I["w_down"], I["w_down"]]
        self.st = m.sb("mwst", [P, self.NS, KD, self.FH])
        self.hi = m.sb("mwhi", [P, self.NB, KD, self.FH], BF16)
        self.lo = m.sb("mwlo", [P, self.NB, KD, self.FH], BF16)
        self.loaded, self.hi_ok, self.lo_ok = m.sems("mw_in", self.NS), m.sem("mw_hi"), m.sems("mw_lo", self.NS)

    def load(self, sp, e, b):
        src = self.mats[b][0, bass.ds(e, 1), :, :].rearrange("e (k p) n -> p (e k) n", p=P)
        c = self.HALF_OF[b] * self.FH
        sp.dma_start(self.st[:, b % self.NS], src[:, :, c:c + self.FH]).then_inc(self.loaded[b % self.NS], 16)

    def half(self, r):
        return r // 2, slice(r % 2 * KD // 2, (r % 2 + 1) * KD // 2)


def topk_stage(nc, K, I, scr, EW):
    NCK = P // NE
    W = T // NCK
    STEPS = 15
    with nc.cleanup_on_exit(), ExitStack() as ctx:
        m = Mem(nc, ctx)
        pr = m.sb("pr", [P, W])
        tmp = m.sb("tmp", [P, 3, W])
        gt = m.sb("gt", [P, W])
        eq = m.sb("eq", [P, W])
        cg = m.sb("cg", [P, W])
        ce = m.sb("ce", [P, W])
        slot = m.sb("slot", [P, W])
        onesw = m.sb("onesw", [P, W])
        same = m.sb("same", [P, P])
        before = m.sb("before", [P, P])
        cand = m.sb("cand", [P, 2, 3])
        cnt3 = m.sb("cnt3", [P, 2, 3])
        acc = m.sb("accp", [P, 2, 4])
        cnt = m.sb("cnt", [P, 2])
        base = m.sb("base", [P, 4])
        sT = m.sb("sT", [P, NE, NCK, 2])
        hi = m.sb("thi", [P, NE, NCK, 2])
        pcol = m.sb("pcol", [P, 1])
        tcol = m.sb("tcol", [P, NCK, 2])
        R = K["R"]
        pc = m.ps("pc", [P, SEG])
        pc2 = m.ps("pc2", [P, SEG])
        ptr = m.ps("ptr", [P, 4, P])

        p_in, cst, c_ok, cnt_ok, tot, a_ok, t_ok = (m.sem("tp_in"), m.sem("tcst"), m.sem("tc_ok"), m.sem("tcnt"),
                                                    m.sem("ttot"), m.sem("ta_ok"), m.sem("tt_ok"))
        fin, ofs, slo, trp, ve = m.sem("tfin"), m.sem("tofs"), m.sem("tslo"), m.sem("ttrp"), m.sem("tve")
        with nc.Block() as block:
            @block.scalar
            def _(act):
                for r in range(EW.HEAD_START):
                    b, ks = EW.half(r)
                    act.wait_ge(EW.loaded[b], 16)
                    nc.scalar.activation(EW.hi[:, b, ks], EW.st[:, b, ks], ACT.Copy).then_inc(EW.hi_ok, 1)

            @block.sync
            def _(sp):
                sp.dma_start(pr[:], scr["pT"].rearrange("e (c w) -> (e c) w", w=W)).then_inc(p_in, 16)
                for b in range(EW.NS):
                    EW.load(sp, 0, b)

            @block.gpsimd
            def _(pool):
                nc.gpsimd.memset(same[:], 1.0).then_inc(cst, 1)
                nc.gpsimd.memset(onesw[:], 1.0).then_inc(cst, 1)
                nc.gpsimd.iota(pcol[:], [[0, 1]], base=0, channel_multiplier=1,
                               allow_small_or_imprecise_dtypes=True).then_inc(cst, 1)
                nc.gpsimd.iota(tcol[:], [[2, NCK], [1, 2]], base=0, channel_multiplier=0,
                               allow_small_or_imprecise_dtypes=True).then_inc(cst, 1)
                pool.wait_ge(cst, 4)
                sv = same[:].rearrange("p (e c) -> p e c", c=NCK)
                nc.gpsimd.affine_select(out=sv, in_=sv, compare_op=ALU.is_ge, fill=0.0, base=0,
                                        pattern=[[-NCK, NE], [0, NCK]], channel_multiplier=1).then_inc(cst, 1)
                pool.wait_ge(cst, 5)
                nc.gpsimd.affine_select(out=sv, in_=sv, compare_op=ALU.is_ge, fill=0.0, base=NCK - 1,
                                        pattern=[[NCK, NE], [0, NCK]], channel_multiplier=-1).then_inc(cst, 1)
                pool.wait_ge(cst, 6)
                nc.gpsimd.affine_select(out=before[:], in_=same[:], compare_op=ALU.is_ge, fill=0.0, base=-1,
                                        pattern=[[1, P]], channel_multiplier=-1).then_inc(cst, 1)
                for r in range(EW.HEAD_START - 1):
                    b, ks = EW.half(r)
                    pool.wait_ge(EW.hi_ok, r + 1)
                    nc.gpsimd.tensor_tensor(EW.lo[:, b, ks], EW.st[:, b, ks], EW.hi[:, b, ks], ALU.subtract)\
                        .then_inc(EW.lo_ok[b], 1)

            @block.vector
            def _(dve):
                nc.vector.memset(acc[:, 0, 3:4], 0.0).then_inc(t_ok, 1)
                dve.wait_ge(p_in, 16)
                dve.wait_ge(cst, 7)
                for b in range(STEPS):
                    p = b % 2
                    dve.wait_ge(t_ok, b + 1)
                    for j in range(3):
                        nc.vector.tensor_scalar(cand[:, p, j:j + 1].bitcast(U32), acc[:, p, 3:4].bitcast(U32),
                                                (j + 1) << (2 * (STEPS - 1 - b)), None, ALU.bitwise_or).then_inc(c_ok, 1)
                    for j in range(3):
                        dve.wait_ge(c_ok, 3 * b + j + 1)
                        if b >= 1:
                            dve.wait_ge(cnt_ok, 3 * b + j - 2)
                        nc.vector.tensor_scalar(tmp[:, j], pr[:], cand[:, p, j:j + 1], None, ALU.is_ge, ALU.add,
                                                accum_out=cnt3[:, p, j:j + 1]).then_inc(cnt_ok, 1)
                    dve.wait_ge(tot, b + 1)
                    nc.vector.scalar_tensor_tensor(acc[:, p, 0:3], pc[:, 4 * p:4 * p + 3], float(CAP), cand[:, p],
                                                   ALU.is_ge, ALU.mult).then_inc(a_ok, 1)
                    dve.wait_ge(a_ok, b + 1)
                    nc.vector.tensor_reduce(acc[:, 1 - p, 3:4], acc[:, p], AX.X, ALU.max).then_inc(t_ok, 1)
                thr = acc[:, STEPS % 2, 3:4]
                dve.wait_ge(t_ok, STEPS + 1)
                nc.vector.tensor_scalar(gt[:], pr[:], thr, None, ALU.is_gt, ALU.add, accum_out=cnt[:, 0:1])\
                    .then_inc(fin, 1)
                nc.vector.tensor_scalar(eq[:], pr[:], thr, None, ALU.is_equal, ALU.add, accum_out=cnt[:, 1:2])\
                    .then_inc(fin, 1)
                dve.wait_ge(fin, 2)
                nc.vector.tensor_tensor_scan(cg[:], onesw[:], gt[:], 0.0, ALU.mult, ALU.add).then_inc(ve, 1)
                nc.vector.tensor_tensor_scan(ce[:], onesw[:], eq[:], 0.0, ALU.mult, ALU.add).then_inc(ve, 1)
                dve.wait_ge(ofs, 1)
                nc.vector.tensor_copy(base[:, 0:3], pc2[:, 0:3]).then_inc(ve, 1)
                dve.wait_ge(ve, 3)
                nc.vector.tensor_scalar(cg[:], cg[:], base[:, 0:1], None, ALU.add).then_inc(ve, 1)
                nc.vector.tensor_scalar(ce[:], ce[:], base[:, 1:2], base[:, 2:3], ALU.add, ALU.add).then_inc(ve, 1)
                dve.wait_ge(ve, 5)
                nc.vector.tensor_tensor(cg[:], cg[:], gt[:], ALU.mult).then_inc(ve, 1)
                nc.vector.scalar_tensor_tensor(eq[:], ce[:], float(CAP), eq[:], ALU.is_le, ALU.mult).then_inc(ve, 1)
                dve.wait_ge(ve, 7)
                nc.vector.tensor_tensor(ce[:], ce[:], eq[:], ALU.mult).then_inc(ve, 1)
                nc.vector.tensor_tensor(gt[:], gt[:], eq[:], ALU.add).then_inc(ve, 1)
                dve.wait_ge(ve, 9)
                nc.vector.tensor_scalar(gt[:], gt[:], -(NOT_A_SLOT + 1.0), NOT_A_SLOT, ALU.mult, ALU.add).then_inc(ve, 1)
                nc.vector.tensor_tensor(cg[:], cg[:], ce[:], ALU.add).then_inc(ve, 1)
                dve.wait_ge(ve, 11)
                nc.vector.tensor_tensor(slot[:], cg[:], gt[:], ALU.add).then_inc(slo, 1)
                dve.wait_ge(trp, 1)
                for half in range(2):
                    nc.vector.tensor_copy(sT[:, :, :, half], ptr[:, half, :].rearrange("p (e c) -> p e c", c=NCK))\
                        .then_inc(ve, 1)
                dve.wait_ge(ve, 13)
                nc.vector.tensor_scalar(hi[:], sT[:], float(P), None, ALU.is_ge).then_inc(ve, 1)
                dve.wait_ge(ve, 14)
                nc.vector.scalar_tensor_tensor(K["place"][:], hi[:].rearrange("p e c h -> p e (c h)"), -float(P),
                                               sT[:].rearrange("p e c h -> p e (c h)"), ALU.mult, ALU.add).then_inc(ve, 1)
                hv = hi[:].rearrange("p e c h -> p e (c h)")
                tv = tcol[:].rearrange("p c h -> p (c h)").unsqueeze(1).broadcast_to([P, NE, NT])
                nc.vector.tensor_scalar(R[:, :, :, 2], hv, pcol[:, 0:1], None, ALU.mult).then_inc(ve, 1)
                nc.vector.tensor_tensor(R[:, :, :, 3], hv, tv, ALU.mult).then_inc(ve, 1)
                dve.wait_ge(ve, 17)
                nc.vector.tensor_scalar(R[:, :, :, 0], R[:, :, :, 2], -1.0, pcol[:, 0:1], ALU.mult, ALU.add).then_inc(ve, 1)
                nc.vector.scalar_tensor_tensor(R[:, :, :, 1], R[:, :, :, 3], -1.0, tv, ALU.mult, ALU.add).then_inc(ve, 1)

            @block.tensor
            def _(pe):
                pe.wait_ge(cst, 7)
                for b in range(STEPS):
                    p = b % 2
                    pe.wait_ge(cnt_ok, 3 * b + 3)
                    nc.tensor.matmul(pc[:, 4 * p:4 * p + 3], same[:], cnt3[:, p], start=True, stop=True).then_inc(tot, 1)
                pe.wait_ge(fin, 2)
                nc.tensor.matmul(pc2[:, 0:2], before[:], cnt[:], start=True, stop=True)
                nc.tensor.matmul(pc2[:, 2:3], same[:], cnt[:, 0:1], start=True, stop=True).then_inc(ofs, 1)
                pe.wait_ge(slo, 1)
                for half in range(2):
                    last = nc.tensor.transpose(ptr[:, half, :], slot[:, half * P:(half + 1) * P], K["ident"][:])
                last.then_inc(trp, 1)


def moe_stage(nc, K, I, scr, EW):
    NB, NS, HALVES, HEAD_START = EW.NB, EW.NS, EW.HALVES, EW.HEAD_START
    wst, whi, wlo, w_in, w_hi, w_lo = EW.st, EW.hi, EW.lo, EW.loaded, EW.hi_ok, EW.lo_ok
    with nc.cleanup_on_exit(), ExitStack() as ctx:
        m = Mem(nc, ctx)
        rows32 = m.sb("mrows", [P, 2, ROWW], I32)
        rows = rows32[:].bitcast(BF16)
        probs = rows32[:].bitcast(F32)
        xhi = m.sb("xhi", [P, KD, CAP], BF16)
        xlo = m.sb("xlo", [P, KD, CAP], BF16)
        thb = m.sb("thb", [P, 2, CAP])
        hb = m.sb("hb", [P, 2, CAP])
        fhi = m.sb("fhi", [P, KD, CAP], BF16)
        flo = m.sb("flo", [P, KD, CAP], BF16)
        ysb = m.sb("ysb", [P, 2, D])
        g2 = m.sb("g2", [P, D])
        oneh = m.sb("oneh", [P, NT, P], BF16)
        Re = m.sb("Re", [P, NT, 4], BF16)
        iot = m.sb("iot", [P, P])
        idf = m.sb("idf", [P, 4])
        idn = m.sb("idn", [P, 2], I32)
        idc = m.sb("idc", [P, 2], I32)
        gate = m.sb("gate", [P, 2])
        pflag = m.sb("mpflag", [1, 1])
        pgu = [m.ps(f"pgu{i}", [P, 2, CAP]) for i in range(2)]
        pd = [m.ps(f"pd{i}", [P, SEG]) for i in range(2)]
        pid = m.ps("pid", [P, SEG])[:, 0:4]
        ptx = [m.ps(f"ptx{i}", [P, 4, CAP], BF16) for i in range(2)]

        g2_in, iot_ok, fl_ok = m.sem("g2_in"), m.sem("iot_ok"), m.sem("fl_ok")
        oh_ok, id_ps, idf_ok, id_ok, idc_ok, gt_ok = (m.sem("oh_ok"), m.sem("id_ps"), m.sem("idf_ok"), m.sem("id_ok"),
                                                      m.sem("idc_ok"), m.sem("gt_ok"))
        got, tx_ps, tx_ok = m.sem("got"), m.sem("tx_ps"), m.sem("tx_ok")
        gu_ps, mth_ok, sg_ok, hid_ok, fhi_ok, flo_ok = (m.sem("gu_ps"), m.sem("mth_ok"), m.sem("msg_ok"), m.sem("hid_ok"),
                                                        m.sem("fhi_ok"), m.sem("flo_ok"))
        d_ps, y_ok, put = m.sem("d_ps"), m.sem("my_ok"), m.sem("put")

        def experts(engine, prep, body):
            prep(0)
            peeled(engine, NE - 1, lambda e: body(e, True))
            body(NE - 1, False)

        with nc.Block() as block:
            @block.sync
            def _(sp):
                def one(e):
                    for b in range(NB):
                        if b < NS and isinstance(e, int) and e == 0:
                            continue
                        if b == NS and isinstance(e, int) and e == 0:
                            wait(sp, got, 32)
                        wait(sp, w_lo[b % NS], 2 * (e * 2 + b // NS))
                        EW.load(sp, e, b)
                peeled(sp, NE, one)

            @block.gpsimd
            def _(pool):
                pool.dma_start(g2[:], scr["modrows"][6:8, :].rearrange("a n -> (a n)").partition_broadcast(P))\
                    .then_inc(g2_in, 16)
                nc.gpsimd.memset(pflag[:], 0.0).then_inc(fl_ok, 1)
                wait(pool, fl_ok, 1)
                nc.gpsimd.iota(iot[:], [[1, P]], base=0, channel_multiplier=0,
                               allow_small_or_imprecise_dtypes=True).then_inc(iot_ok, 1)

                def carrier():
                    nc.gpsimd.tensor_tensor(pflag[:], pflag[:], pflag[:], ALU.mult).then_inc(fl_ok, 1)

                def prep(e, first=False):
                    wait(pool, fl_ok, 1 if first else e * 3 - 1)
                    wait(pool, id_ok, e + 1)
                    wait(pool, tx_ps, e * 4)
                    wait(pool, gt_ok, e)
                    carrier()
                    for s in range(2):
                        pool.indirect_dma_start(out=rows32[:, s, :], out_offset=None, in_=scr["rows"],
                                                in_offset=bass.IndirectOffsetOnAxis(ap=idn[:, s:s + 1], axis=0))\
                            .then_inc(got, 16)

                def body(e, nxt):
                    if nxt:
                        prep(e + 1)
                    wait(pool, put, e * 32)
                    for s in range(2):
                        wait(pool, y_ok, e * 4 + 2 * s + 2)
                        wait(pool, fl_ok, e * 3 + s + (3 if nxt else 2))
                        carrier()
                        pool.indirect_dma_start(out=scr["y"], out_offset=bass.IndirectOffsetOnAxis(ap=idc[:, s:s + 1], axis=0),
                                                in_=ysb[:, s, :], in_offset=None, compute_op=ALU.add).then_inc(put, 16)

                experts(pool, lambda e: prep(e, True), body)
                wait(pool, put, NE * 32)

            @block.scalar
            def _(act):
                def turn(e, j):
                    wait(act, tx_ps, e * 4 + 2 * j + 1)
                    wait(act, gu_ps, e * 8)
                    nc.scalar.activation(xhi[:, 4 * j:4 * j + 4, :], ptx[0][:], ACT.Copy).then_inc(tx_ok, 1)

                def split(e, r):
                    e, (b, ks) = e + r // HALVES, EW.half(r % HALVES)
                    wait(act, w_in[b % NS], e * 32 + 16 * (b // NS) + 16)
                    if b < 2:
                        if not (isinstance(e, int) and e == 0):
                            wait(act, gu_ps, e * 8 - 4)
                    elif b < 4:
                        wait(act, gu_ps, e * 8)
                    else:
                        wait(act, d_ps, e * 4)
                    nc.scalar.activation(whi[:, b, ks], wst[:, b % NS, ks], ACT.Copy).then_inc(w_hi, 1)

                def hidden(e, j, nxt):
                    wait(act, gu_ps, e * 8 + j + 1)
                    if j < 2:
                        wait(act, sg_ok, e * 8)
                    else:
                        wait(act, sg_ok, e * 8 + j - 1)
                    nc.scalar.activation(thb[:, j % 2], pgu[j % 2][:, 0, :], ACT.Tanh, scale=0.5).then_inc(mth_ok, 1)
                    if nxt or HEAD_START + j < HALVES:
                        split(e, HEAD_START + j)
                    wait(act, hid_ok, e * 8 + j + 1)
                    wait(act, d_ps, e * 4)
                    nc.scalar.activation(fhi[:, j, :], hb[:, j % 2], ACT.Copy).then_inc(fhi_ok, 1)

                def body(e, nxt):
                    for j in range(8):
                        hidden(e, j, nxt)
                    if nxt:
                        for q in range(4):
                            if q < 2:
                                turn(e + 1, q)
                            split(e, HEAD_START + 8 + q)

                def prep0(e):
                    turn(0, 0)
                    turn(0, 1)

                experts(act, prep0, body)

            @block.vector
            def _(dve):
                wait(dve, iot_ok, 1)

                def token_list(e):
                    wait(dve, id_ps, e)
                    nc.vector.tensor_tensor(oneh[:], iot[:].unsqueeze(1).broadcast_to([P, NT, P]),
                                            K["place"][:, bass.ds(e, 1), :].rearrange("p e t -> p (e t)").unsqueeze(2)
                                            .broadcast_to([P, NT, P]), ALU.is_equal).then_inc(oh_ok, 1)
                    nc.vector.tensor_copy(Re[:], K["R"][:, bass.ds(e, 1), :, :].rearrange("p e t j -> p (e t) j"))\
                        .then_inc(oh_ok, 1)

                def numbers(e):
                    wait(dve, id_ps, e + 1)
                    nc.vector.tensor_copy(idf[:], pid).then_inc(idf_ok, 1)
                    wait(dve, idf_ok, e + 1)
                    wait(dve, got, e * 32)
                    wait(dve, idc_ok, e)
                    f2 = idf[:].rearrange("p (s a) -> p s a", a=2)
                    nc.vector.scalar_tensor_tensor(idn[:], f2[:, :, 1], float(P), f2[:, :, 0], ALU.mult, ALU.add)\
                        .then_inc(id_ok, 1)

                def turn(e, j):
                    wait(dve, tx_ps, e * 4 + 2 * j + 2)
                    wait(dve, gu_ps, e * 8)
                    nc.vector.tensor_copy(xlo[:, 4 * j:4 * j + 4, :], ptx[1][:]).then_inc(tx_ok, 1)

                def split(e, r):
                    e, (b, ks) = e + r // HALVES, EW.half(r % HALVES)
                    wait(dve, w_hi, e * HALVES + r % HALVES + 1)
                    nc.vector.tensor_tensor(wlo[:, b, ks], wst[:, b % NS, ks], whi[:, b, ks], ALU.subtract)\
                        .then_inc(w_lo[b % NS], 1)

                def hidden(e, j, nxt):
                    p = j % 2
                    wait(dve, mth_ok, e * 8 + j + 1)
                    if j < 2:
                        wait(dve, flo_ok, e * 8)
                    else:
                        wait(dve, flo_ok, e * 8 + j - 1)
                    nc.vector.scalar_tensor_tensor(thb[:, p], thb[:, p], 1.0, pgu[p][:, 0, :], ALU.add, ALU.mult)\
                        .then_inc(sg_ok, 1)
                    wait(dve, sg_ok, e * 8 + j + 1)
                    nc.vector.tensor_tensor(hb[:, p], thb[:, p], pgu[p][:, 1, :], ALU.mult).then_inc(hid_ok, 1)
                    if nxt or HEAD_START - 1 + j < HALVES:
                        split(e, HEAD_START - 1 + j)
                    wait(dve, hid_ok, e * 8 + j + 1)
                    wait(dve, fhi_ok, e * 8 + j + 1)
                    nc.vector.tensor_tensor(flo[:, j, :], hb[:, p], fhi[:, j, :], ALU.subtract).then_inc(flo_ok, 1)

                def weigh(e, s, c):
                    q = 2 * s + c
                    if isinstance(e, int) and e == 0 and q == 0:
                        wait(dve, g2_in, 16)
                    wait(dve, d_ps, e * 4 + q + 1)
                    wait(dve, put, e * 32)
                    nc.vector.scalar_tensor_tensor(ysb[:, s, c * SEG:(c + 1) * SEG], pd[q % 2][:], gate[:, s:s + 1],
                                                   g2[:, c * SEG:(c + 1) * SEG], ALU.mult, ALU.mult).then_inc(y_ok, 1)

                def body(e, nxt):
                    wait(dve, got, e * 32 + 32)
                    wait(dve, y_ok, e * 4)
                    nc.vector.tensor_scalar(gate[:], probs[:, :, bass.ds(e + D, 1)]
                                            .rearrange("p s a -> p (s a)"), 0.5, None, ALU.mult).then_inc(gt_ok, 1)
                    for j in range(8):
                        hidden(e, j, nxt)
                        if j == 0 and nxt:
                            token_list(e + 1)
                        if j == 2:
                            wait(dve, put, e * 32)
                            nc.vector.tensor_copy(idc[:], idn[:]).then_inc(idc_ok, 1)
                            if nxt:
                                numbers(e + 1)
                    wait(dve, gt_ok, e + 1)
                    for q in range(4):
                        if nxt:
                            if q < 2:
                                turn(e + 1, q)
                            split(e, HEAD_START - 1 + 8 + q)
                        weigh(e, q // 2, q % 2)

                def prep0(e):
                    token_list(0)
                    numbers(0)
                    turn(0, 0)
                    turn(0, 1)

                experts(dve, prep0, body)

            @block.tensor
            def _(pe):
                def token_list(e):
                    wait(pe, oh_ok, e * 2 + 2)
                    wait(pe, idf_ok, e)
                    for t in range(NT):
                        last = nc.tensor.matmul(pid, oneh[:, t, :], Re[:, t, :], start=(t == 0), stop=(t == NT - 1))
                    last.then_inc(id_ps, 1)

                def turn(e, j):
                    wait(pe, got, e * 32 + 32)
                    wait(pe, tx_ok, e * 4 + 2 * j)
                    for part in range(2):
                        for k in range(4):
                            for s in range(2):
                                c = part * D + (4 * j + k) * P
                                last = nc.tensor.transpose(ptx[part][:, k, s * P:(s + 1) * P], rows[:, s, c:c + P],
                                                           K["identb"][:])
                        last.then_inc(tx_ps, 1)

                def body(e, nxt):
                    wait(pe, tx_ok, e * 4 + 4)
                    for f in range(8):
                        h, jj = f // 4, f % 4
                        if jj == 0:
                            for b in (2 * h, 2 * h + 1):
                                wait(pe, w_lo[b % NS], 2 * (e * 2 + b // NS + 1))
                        if f < 2:
                            wait(pe, hid_ok, e * 8)
                        else:
                            wait(pe, hid_ok, e * 8 + f - 1)
                        for part in range(2):
                            b = 2 * h + part
                            last = triple(nc, pgu[f % 2][:, part, :], [
                                (whi[:, b, k, jj * P:(jj + 1) * P], wlo[:, b, k, jj * P:(jj + 1) * P], xhi[:, k, :],
                                 xlo[:, k, :]) for k in range(KD)])
                        last.then_inc(gu_ps, 1)
                        if nxt and f == 2:
                            token_list(e + 1)
                        if nxt and f == 6:
                            turn(e + 1, 0)
                    wait(pe, flo_ok, e * 8 + 7)
                    for b in (4, 5):
                        wait(pe, w_lo[b % NS], 2 * (e * 2 + b // NS + 1))
                    for q in range(4):
                        s, c = q // 2, q % 2
                        wait(pe, y_ok, e * 4 + max(0, q - 1))
                        for k in range(KD):
                            if q == 0 and k == KD - 1:
                                wait(pe, flo_ok, e * 8 + 8)
                            fh, fl = fhi[:, k, s * P:(s + 1) * P], flo[:, k, s * P:(s + 1) * P]
                            nc.tensor.matmul(pd[q % 2][:], fh, whi[:, 4 + c, k, :], start=(k == 0), stop=False)
                            nc.tensor.matmul(pd[q % 2][:], fh, wlo[:, 4 + c, k, :], start=False, stop=False)
                            last = nc.tensor.matmul(pd[q % 2][:], fl, whi[:, 4 + c, k, :], start=False,
                                                    stop=(k == KD - 1))
                        last.then_inc(d_ps, 1)
                        if nxt and q == 0:
                            turn(e + 1, 1)

                def prep0(e):
                    token_list(0)
                    turn(0, 0)
                    turn(0, 1)

                experts(pe, prep0, body)


def finish_stage(nc, K, I, scr, out):
    with nc.cleanup_on_exit(), ExitStack() as ctx:
        m = Mem(nc, ctx)
        NBUF = 4
        yt = m.sb("yt", [P, NBUF, D])
        junk = m.sb("fjunk", [P, D])
        fg = m.sb("fg", [P, D])
        st = m.sb("fst", [P, NBUF, 4])
        fg_in, y_in, y_out = m.sem("fg_in"), m.sems("fy_in", NBUF), m.sems("fy_out", NBUF)
        ss, sd, rs, ok = m.sem("fss"), m.sem("fsd"), m.sem("frs"), m.sem("fok")
        with nc.Block() as block:
            @block.sync
            def _(sp):
                sp.dma_start(fg[:], I["final_g"].partition_broadcast(P)).then_inc(fg_in, 16)
                def one(i):
                    for b in range(NBUF):
                        wait(sp, y_out[b], i * 16)
                        sp.dma_start(yt[:, b], scr["y"][bass.ds((i * NBUF + b) * P, P), :]).then_inc(y_in[b], 16)
                peeled(sp, NT // NBUF, one)

            @block.gpsimd
            def _(pool):
                def one(i):
                    for b in range(NBUF):
                        wait(pool, ok, i * NBUF + b + 1)
                        pool.dma_start(out[0, bass.ds((i * NBUF + b) * P, P), :], yt[:, b]).then_inc(y_out[b], 16)
                peeled(pool, NT // NBUF, one)
                for b in range(NBUF):
                    wait(pool, y_out[b], 16 * NT // NBUF)

            @block.scalar
            def _(act):
                def one(i):
                    for b in range(NBUF):
                        wait(act, y_in[b], i * 16 + 16)
                        nc.scalar.activation(junk[:], yt[:, b], ACT.Square, accum_out=st[:, b, 0:1]).then_inc(ss, 1)
                        wait(act, ss, i * NBUF + b + 1)
                        nc.scalar.activation(st[:, b, 1:2], st[:, b, 0:1], ACT.Sqrt, bias=K["eps"][:, 0:1], scale=1.0 / D)\
                            .then_inc(sd, 1)
                peeled(act, NT // NBUF, one)

            @block.vector
            def _(dve):
                wait(dve, fg_in, 16)
                def one(i):
                    for b in range(NBUF):
                        wait(dve, sd, i * NBUF + b + 1)
                        nc.vector.reciprocal(st[:, b, 2:3], st[:, b, 1:2]).then_inc(rs, 1)
                        wait(dve, rs, i * NBUF + b + 1)
                        nc.vector.scalar_tensor_tensor(yt[:, b], yt[:, b], st[:, b, 2:3], fg[:], ALU.mult, ALU.mult)\
                            .then_inc(ok, 1)
                peeled(dve, NT // NBUF, one)


def build(nc, I, out, debug=False):
    kind = "ExternalOutput" if debug else "Internal"
    scr = {
        "modrows": nc.dram_tensor("s_modrows", [8, SEG], F32, kind=kind).ap(),
        "q": nc.dram_tensor("s_q", [HEADS, P, T], F32, kind=kind).ap(),
        "g": nc.dram_tensor("s_g", [HEADS, P, T], F32, kind=kind).ap(),
        "v": nc.dram_tensor("s_v", [HEADS, P, TC // P + NT, P], F32, kind=kind).ap(),
        "mixed": nc.dram_tensor("s_mixed", [NT, P, 2, KD, P], BF16, kind=kind).ap(),
        "rows": nc.dram_tensor("s_rows", [T, ROWW], I32, kind=kind).ap(),
        "pT": nc.dram_tensor("s_pT", [NE, T], F32, kind=kind).ap(),
        "y": nc.dram_tensor("s_y", [T, D], F32, kind=kind).ap(),
    }
    with ExitStack() as whole:
        m = Mem(nc, whole)
        K = {"ident": m.sb("ident", [P, P]), "identb": m.sb("identb", [P, P], BF16), "ones": m.sb("ones", [P, P]),
             "mean_cw": m.sb("mean_cw", [P, P]), "mean_p": m.sb("mean_p", [P, P]), "eps": m.sb("eps", [P, 1]),
             "const_ok": m.sem("const_ok"), "n_const": 8}
        with nc.Block() as block:
            @block.gpsimd
            def _(pool):
                for t, val in (("ident", 0.0), ("identb", 0.0), ("ones", 1.0), ("mean_cw", 1.0 / CW),
                               ("mean_p", 1.0 / P), ("eps", EPS)):
                    nc.gpsimd.memset(K[t][:], val).then_inc(K["const_ok"], 1)
                wait(pool, K["const_ok"], 6)
                for t in ("ident", "identb"):
                    nc.gpsimd.affine_select(out=K[t][:], in_=K[t][:], compare_op=ALU.not_equal, fill=1.0, base=0,
                                            pattern=[[-1, P]], channel_multiplier=1).then_inc(K["const_ok"], 1)
        with ExitStack() as mixer:
            mm = Mem(nc, mixer)
            K["hhi"] = mm.sb("hhi", [P, KD, TC + T], BF16)
            K["hlo"] = mm.sb("hlo", [P, KD, TC + T], BF16)
            modulate_stage(nc, K, I, scr)
            conv_stage(nc, K, I, scr)
            heads_stage(nc, K, I, scr)
        outproj_stage(nc, K, I, scr)
        K["place"] = m.sb("place", [P, NE, NT])
        K["R"] = m.sb("R", [P, NE, NT, 4], BF16)
        with nc.cleanup_on_exit(), ExitStack() as experts:
            EW = ExpertWeights(Mem(nc, experts), I)
            topk_stage(nc, K, I, scr, EW)
            moe_stage(nc, K, I, scr, EW)
        finish_stage(nc, K, I, scr, out)


_INS = ["x", "c", "ctx", "c_ctx", "ada_w", "ada_b", "norm1_g", "w_in", "conv_taps", "conv_bias", "conv_ln_g",
        "conv_ln_b", "hgrn_lb_logits", "hgrn_norm_g", "w_out", "norm2_g", "router_w", "w_gate", "w_up", "w_down",
        "final_g"]
DEBUG = False


def kernel(**inputs):
    import numpy as np
    import concourse.bacc as bacc
    from concourse.bass_utils import run_bass_kernel_spmd as run

    nc = bacc.Bacc("TRN2", target_bir_lowering=False, num_devices=1)
    arrays, aps = {}, {}
    for name in _INS:
        a = np.ascontiguousarray(inputs[name])
        arrays[f"in_{name}"] = a
        aps[name] = nc.dram_tensor(f"in_{name}", a.shape, mybir.dt.from_np(a.dtype), kind="ExternalInput").ap()
    o = nc.dram_tensor("out_0", (1, T, D), F32, kind="ExternalOutput").ap()
    build(nc, aps, o, debug=DEBUG)
    r = run(nc, [arrays], core_ids=[0])
    return r.results[0]["out_0"]
```
